# Optimizing a Trainium2 kernel written in Bass

```python
import math
import jax, jax.numpy as jnp
from jax import lax
import numpy as np

D_MODEL = 1024
BATCH = 1
SEQ = 1024
DEPTH = 2

GRID_W = 64
ATTN_Q_HEADS = 8
ATTN_KV_HEADS = 2
ATTN_HEAD_DIM = 64
ATTN_WIDTH = ATTN_Q_HEADS * ATTN_HEAD_DIM
ATTN_KV_WIDTH = ATTN_KV_HEADS * ATTN_HEAD_DIM
Q_BLOCK = 128
RET_HEADS = 4
RET_HEAD_DIM = 128
RET_WIDTH = RET_HEADS * RET_HEAD_DIM
RET_CHUNK = 128
N_BRANCHES = 2
ROPE_THETA = 10000.0
EPS = 1e-6
IN_SPLITS = (ATTN_WIDTH, ATTN_KV_WIDTH, ATTN_KV_WIDTH, ATTN_WIDTH,
             RET_WIDTH, RET_WIDTH, RET_WIDTH, RET_WIDTH, N_BRANCHES * D_MODEL)
D_IN = sum(IN_SPLITS)

kernel_name = "hybrid_gqa_retention_gated_encoder"

def rms_norm(x, g):
    xf = x.astype(jnp.float32)
    y = xf * lax.rsqrt(jnp.mean(xf * xf, axis=-1, keepdims=True) + EPS)
    return (y * g.astype(jnp.float32)).astype(x.dtype)

def head_group_norm(o, w):
    mu = jnp.mean(o, axis=-1, keepdims=True)
    var = jnp.mean(jnp.square(o - mu), axis=-1, keepdims=True)
    y = (o - mu) * lax.rsqrt(var + EPS)
    b, s, h, d = o.shape
    return y.reshape(b, s, h * d) * w.astype(jnp.float32)

def axial_rope_tables(seq_len, head_dim):
    n_rows = seq_len // GRID_W
    row = jnp.repeat(jnp.arange(n_rows, dtype=jnp.float32), GRID_W)
    col = jnp.tile(jnp.arange(GRID_W, dtype=jnp.float32), n_rows)
    d_axis = head_dim // 2
    inv_freq = ROPE_THETA ** (-jnp.arange(0, d_axis, 2, dtype=jnp.float32) / d_axis)
    ang = jnp.concatenate([row[:, None] * inv_freq, col[:, None] * inv_freq], axis=-1)
    return jnp.cos(ang), jnp.sin(ang)

def apply_axial_rope(x, cos, sin):
    b, s, h, hd = x.shape
    q = hd // 4
    xf = x.astype(jnp.float32).reshape(b, s, h, 2, 2, q)
    x1 = xf[..., 0, :]
    x2 = xf[..., 1, :]
    c = cos.reshape(s, 1, 2, q)
    sn = sin.reshape(s, 1, 2, q)
    out = jnp.stack([x1 * c - x2 * sn, x1 * sn + x2 * c], axis=-2)
    return out.reshape(b, s, h, hd).astype(x.dtype)

def block_attention(q, k, v):
    b, s, hq, hd = q.shape
    hkv = k.shape[2]
    g = hq // hkv
    nb = s // Q_BLOCK
    qb = q.reshape(b, nb, Q_BLOCK, hkv, g, hd).transpose(1, 0, 2, 3, 4, 5)
    scale = hd ** -0.5

    def one_block(q_blk):
        sc = jnp.einsum('bqkgd,bskd->bkgqs', q_blk, k,
                        preferred_element_type=jnp.float32) * scale
        p = jax.nn.softmax(sc, axis=-1).astype(v.dtype)
        return jnp.einsum('bkgqs,bskd->bqkgd', p, v)

    o = lax.map(one_block, qb)
    return o.transpose(1, 0, 2, 3, 4, 5).reshape(b, s, hq * hd)

def retention_scan(q, k, v, log_gamma, strict):
    b, s, h, dk = q.shape
    dv = v.shape[-1]
    c = RET_CHUNK
    nc = s // c

    def to_chunks(t):
        return t.reshape(b, nc, c, h, t.shape[-1]).transpose(1, 0, 3, 2, 4)

    lg = log_gamma.astype(jnp.float32)[:, None]
    idx = jnp.arange(c, dtype=jnp.float32)
    diff = idx[:, None] - idx[None, :]
    mask = (diff > 0) if strict else (diff >= 0)
    dmat = jnp.where(mask[None], jnp.exp(jnp.maximum(diff, 0.0)[None] * lg[:, :, None]), 0.0)
    q_decay = jnp.exp((idx + 1.0)[None] * lg)
    k_decay = jnp.exp((c - 1.0 - idx)[None] * lg)
    chunk_decay = jnp.exp(c * lg[:, 0])

    def step(state, inp):
        qi, ki, vi = inp
        qf = qi.astype(jnp.float32)
        kf = ki.astype(jnp.float32)
        vf = vi.astype(jnp.float32)
        intra = jnp.einsum('bhij,bhje->bhie', jnp.einsum('bhid,bhjd->bhij', qf, kf) * dmat, vf)
        cross = jnp.einsum('bhid,bhde->bhie', qf, state) * q_decay[..., None]
        state = state * chunk_decay[:, None, None] + jnp.einsum(
            'bhjd,bhje->bhde', kf * k_decay[..., None], vf)
        return state, intra + cross

    state0 = jnp.zeros((b, h, dk, dv), jnp.float32)
    _, o = lax.scan(step, state0, (to_chunks(q), to_chunks(k), to_chunks(v)))
    return o.transpose(1, 0, 3, 2, 4).reshape(b, s, h, dv)

def bidirectional_retention(q, k, v, log_gamma_fwd, log_gamma_bwd):
    fwd = retention_scan(q, k, v, log_gamma_fwd, strict=False)
    flip = lambda t: jnp.flip(t, axis=1)
    bwd = flip(retention_scan(flip(q), flip(k), flip(v), log_gamma_bwd, strict=True))
    return fwd + bwd

def split_columns(z):
    offs = []
    acc = 0
    for w in IN_SPLITS[:-1]:
        acc += w
        offs.append(acc)
    return jnp.split(z, offs, axis=-1)

def setup_inputs(seed: int = 0) -> dict:
    key = jax.random.key(seed)
    ks = jax.random.split(key, 14)
    f32 = jnp.float32
    x = jax.random.normal(ks[0], (BATCH, SEQ, D_MODEL), f32)
    norm_g = 1.0 + 0.02 * jax.random.normal(ks[1], (DEPTH, D_MODEL), f32)
    w_in = jax.random.normal(ks[2], (DEPTH, D_MODEL, D_IN), f32) * D_MODEL ** -0.5
    attn_q_norm = 1.0 + 0.02 * jax.random.normal(ks[3], (DEPTH, ATTN_HEAD_DIM), f32)
    attn_k_norm = 1.0 + 0.02 * jax.random.normal(ks[4], (DEPTH, ATTN_HEAD_DIM), f32)
    base_logit = jnp.log(2.0 ** (5.0 + jnp.arange(RET_HEADS, dtype=f32)) - 1.0)
    ret_decay_fwd = base_logit[None] + 0.1 * jax.random.normal(ks[5], (DEPTH, RET_HEADS), f32)
    ret_decay_bwd = base_logit[None] + 0.1 * jax.random.normal(ks[6], (DEPTH, RET_HEADS), f32)
    ret_gn_w = 1.0 + 0.02 * jax.random.normal(ks[7], (DEPTH, RET_WIDTH), f32)
    w_branch_attn = jax.random.normal(ks[8], (DEPTH, ATTN_WIDTH, D_MODEL), f32) * ATTN_WIDTH ** -0.5
    w_branch_ret = jax.random.normal(ks[9], (DEPTH, RET_WIDTH, D_MODEL), f32) * RET_WIDTH ** -0.5
    w_out = jax.random.normal(ks[10], (DEPTH, D_MODEL, D_MODEL), f32) * D_MODEL ** -0.5
    final_norm_g = 1.0 + 0.02 * jax.random.normal(ks[11], (D_MODEL,), f32)
    return {"x": x, "norm_g": norm_g, "w_in": w_in, "attn_q_norm": attn_q_norm,
            "attn_k_norm": attn_k_norm, "ret_decay_fwd": ret_decay_fwd,
            "ret_decay_bwd": ret_decay_bwd, "ret_gn_w": ret_gn_w,
            "w_branch_attn": w_branch_attn, "w_branch_ret": w_branch_ret,
            "w_out": w_out, "final_norm_g": final_norm_g}

def reference(x, norm_g, w_in, attn_q_norm, attn_k_norm, ret_decay_fwd, ret_decay_bwd,
              ret_gn_w, w_branch_attn, w_branch_ret, w_out, final_norm_g):
    b, s, d = x.shape
    dt = x.dtype
    cos_a, sin_a = axial_rope_tables(s, ATTN_HEAD_DIM)
    cos_r, sin_r = axial_rope_tables(s, RET_HEAD_DIM)

    for layer in range(DEPTH):
        h = rms_norm(x, norm_g[layer])
        z = h @ w_in[layer]
        qa, ka, va, ga, qr, kr, vr, gr, gm = split_columns(z)

        qa = rms_norm(qa.reshape(b, s, ATTN_Q_HEADS, ATTN_HEAD_DIM), attn_q_norm[layer])
        ka = rms_norm(ka.reshape(b, s, ATTN_KV_HEADS, ATTN_HEAD_DIM), attn_k_norm[layer])
        qa = apply_axial_rope(qa, cos_a, sin_a)
        ka = apply_axial_rope(ka, cos_a, sin_a)
        va = va.reshape(b, s, ATTN_KV_HEADS, ATTN_HEAD_DIM)
        oa = block_attention(qa, ka, va)
        ya = (jax.nn.silu(ga) * oa) @ w_branch_attn[layer]

        qr = apply_axial_rope(qr.reshape(b, s, RET_HEADS, RET_HEAD_DIM), cos_r, sin_r)
        kr = apply_axial_rope(kr.reshape(b, s, RET_HEADS, RET_HEAD_DIM), cos_r, sin_r)
        kr = kr * (RET_HEAD_DIM ** -0.5)
        vr = vr.reshape(b, s, RET_HEADS, RET_HEAD_DIM)
        lg_f = jax.nn.log_sigmoid(ret_decay_fwd[layer].astype(jnp.float32))
        lg_b = jax.nn.log_sigmoid(ret_decay_bwd[layer].astype(jnp.float32))
        orr = bidirectional_retention(qr, kr, vr, lg_f, lg_b)
        orr = head_group_norm(orr, ret_gn_w[layer]).astype(dt)
        yb = (jax.nn.silu(gr) * orr) @ w_branch_ret[layer]

        gates = jax.nn.sigmoid(gm.astype(jnp.float32)).astype(dt).reshape(b, s, N_BRANCHES, d)
        merged = gates[:, :, 0] * ya + gates[:, :, 1] * yb
        x = x + merged @ w_out[layer]

    return rms_norm(x, final_norm_g)


_drawn_inputs = setup_inputs


def setup_inputs(seed=0):
    import zlib

    import numpy as np

    out = dict(_drawn_inputs(seed))
    spreads = {}
    factors = {'norm_g': 2.789,
     'attn_q_norm': 8.0,
     'attn_k_norm': 8.0,
     'ret_gn_w': 6.353,
     'final_norm_g': 2.831}
    for name, (base, spread) in spreads.items():
        noise = np.random.default_rng([zlib.crc32(name.encode()), seed]).standard_normal(out[name].shape)
        drawn = base * np.exp(spread * noise) if base else spread * noise
        out[name] = __import__('jax').numpy.asarray(drawn.astype(out[name].dtype))
    for name, factor in factors.items():
        out[name] = (out[name] * factor).astype(out[name].dtype)
    return out
```

```python
from contextlib import ExitStack

import numpy as np

import concourse.bass as bass
from concourse import mybir

F32 = mybir.dt.float32
F32R = mybir.dt.float32r
I32 = mybir.dt.int32
ALU = mybir.AluOpType
ACT = mybir.ActivationFunctionType
AXX = mybir.AxisListType.X

P = 128
DM = 1024
SEQ = 1024
DEPTH = 2
GRID_W = 64
QH, KVH, HD = 8, 2, 64
GRP = QH // KVH
RH, RD = 4, 128
AW, KVW, RW = QH * HD, KVH * HD, RH * RD
EPS = 1e-6
THETA = 10000.0
T = SEQ // P
K = DM // P
KA = AW // P
OFF = np.cumsum([0, AW, KVW, KVW, AW, RW, RW, RW, RW]).tolist()
C_QA, C_KA, C_VA, C_GA, C_QR, C_KR, C_VR, C_GR, C_GM = OFF
D_IN = C_GM + 2 * DM
QK_W = (GRP + 1) * HD
N_B, N_C, N_D1, N_D2 = 5, 4, 3, 2
U_C = KVH * N_B
U_D1 = U_C + RH * N_C
U_D2 = U_D1 + K * N_D1
U_L = U_D2 + 4 * N_D2
PH_L = 3 * (1 + KVH + RH + 2)
MAGIC = 1597463007.0


def build(nc, x, norm_g, w_in, qn, kn, dec_f, dec_b, gn_w, w_a, w_r, w_o, fin_g,
          ident, rope_a, rope_r, dist, idx, xs, out):
    with ExitStack() as ctx:
        def sem(name):
            return ctx.enter_context(nc.semaphore(name))

        def sb(c, name, shape, dt=F32):
            return c.enter_context(nc.sbuf_tensor(name, [P] + shape, dt))

        ps = ctx.enter_context(nc.psum_tensor("ps", [P, 8, 512], F32))
        hT_hi = sb(ctx, "hT_hi", [K, SEQ], F32R)
        hT_lo = sb(ctx, "hT_lo", [K, SEQ], F32R)
        w_hi = sb(ctx, "w_hi", [K, 4 * P], F32R)
        w_lo = sb(ctx, "w_lo", [K, 4 * P], F32R)
        raw = sb(ctx, "raw", [2, K, P])
        idf = sb(ctx, "idf", [P])
        idr = sb(ctx, "idr", [P], F32R)
        dst = sb(ctx, "dst", [2, P])
        dec = sb(ctx, "dec", [DEPTH * RH, 8])
        dcur = sb(ctx, "dcur", [8])
        icol = sb(ctx, "icol", [6])
        lgw = sb(ctx, "lgw", [6, 2 * DEPTH * RH])
        msk = sb(ctx, "msk", [P])
        gwc = sb(ctx, "gwc", [RH])
        ss = sb(ctx, "ss", [T * (GRP + 1)])
        rs = sb(ctx, "rs", [T * (GRP + 1)])
        nt = sb(ctx, "nt", [T * (GRP + 1)])
        st6 = sb(ctx, "st6", [T, 6])
        mv = sb(ctx, "mv", [T, 2])
        nmx = sb(ctx, "nmx", [4])
        rsm = sb(ctx, "rsm", [4])
        rrc = sb(ctx, "rrc", [4])
        ua_hi = sb(ctx, "ua_hi", [KA, SEQ], F32R)
        ua_lo = sb(ctx, "ua_lo", [KA, SEQ], F32R)
        with ExitStack() as pb:
            gT = sb(pb, "gT", [2, SEQ])
            q_st = sb(pb, "q_st", [GRP, SEQ], F32R)
            k_st = sb(pb, "k_st", [2, SEQ], F32R)
            v_st = sb(pb, "v_st", [T, 2 * HD], F32R)
            av = sb(pb, "av", [2, 256])
            with ExitStack() as p1:
                zqk = sb(p1, "zqk", [T, QK_W])
                ctA = sb(p1, "ctA", [2, T, HD])
                gqk = sb(p1, "gqk", [QK_W])
                sq = sb(p1, "sq", [2, QK_W])
                rta = sb(p1, "rta", [2, QK_W])
                rtb = sb(p1, "rtb", [2, QK_W])
                qs = sb(p1, "qs", [2, GRP + 2, P], F32R)
                thA = sb(p1, "thA", [2, 512])
            with ExitStack() as p2:
                pp = sb(p2, "pp", [3, SEQ])
                pT_hi = sb(p2, "pT_hi", [2, T, 256], F32R)
                pT_lo = sb(p2, "pT_lo", [2, T, 256], F32R)
        ur_hi = sb(ctx, "ur_hi", [KA, SEQ], F32R)
        ur_lo = sb(ctx, "ur_lo", [KA, SEQ], F32R)
        with ExitStack() as pc:
            us = sb(pc, "us", [2, T, RD])
            oc = sb(pc, "oc", [T, RD])
            g2 = sb(pc, "g2", [T, RD])
            ctR = sb(pc, "ctR", [2, T, RD])
            ra = sb(pc, "ra", [2, 2 * RD])
            rb = sb(pc, "rb", [2 * RD])
            pm = sb(pc, "pm", [2, P])
            thC = sb(pc, "thC", [RD])
            qT_hi = sb(pc, "qT_hi", [T, P], F32R)
            qT_lo = sb(pc, "qT_lo", [T, P], F32R)
            kT = sb(pc, "kT", [2, 2, P], F32R)
            kn_ = sb(pc, "kn_", [2, 2, RD], F32R)
            vn = sb(pc, "vn", [2, 2, RD], F32R)
            vd = sb(pc, "vd", [2, 2, 2 * RD], F32R)
            pq = sb(pc, "pq", [2, 2, P], F32R)
            sst = sb(pc, "sst", [2, 2 * RD], F32R)
        xm = sb(ctx, "xm", [T, DM])
        with ExitStack() as pa:
            hb = sb(pa, "hb", [2, DM])
            gB = sb(pa, "gB", [DM])
            junk = sb(pa, "junk", [DM])
        with ExitStack() as pd:
            tA = sb(pd, "tA", [2, 512])
            tB = sb(pd, "tB", [2, 512])

        consts_in, x_in, x_saved, x_back = map(sem, ("consts_in", "x_in", "x_saved", "x_back"))
        out_done = [sem("out_done0"), sem("out_done1")]
        raw_in = [sem("raw_in0"), sem("raw_in1")]
        w_rounded, w_ready, phase_end = map(sem, ("w_rounded", "w_ready", "phase_end"))
        pro_dve, pro_act, newton = map(sem, ("pro_dve", "pro_act", "newton"))
        gain_in, a_sq, h_ready, h_tr, h_hi, h_lo = map(sem, ("gain_in", "a_sq", "h_ready", "h_tr", "h_hi", "h_lo"))
        b_tab, b_gain, b_proj, b_z, b_sq, b_vh, b_ssum, b_free = map(sem, (
            "b_tab", "b_gain", "b_proj", "b_z", "b_sq", "b_vh", "b_ssum", "b_free"))
        b_gate, b_tanh, b_gated, b_norm, b_cos, b_sin, b_rot, b_hi, b_lo, b_tr, b_qT, b_kT = map(sem, (
            "b_gate", "b_tanh", "b_gated", "b_norm", "b_cos", "b_sin", "b_rot", "b_hi", "b_lo", "b_tr", "b_qT", "b_kT"))
        s_done, s_max, s_exp, s_rcp, p_norm, p_tr, p_hi, p_lo = map(sem, (
            "s_done", "s_max", "s_exp", "s_rcp", "p_norm", "p_tr", "p_hi", "p_lo"))
        pv_done, av_lo, av_sum, av_gated, ua_h, ua_l = map(sem, ("pv_done", "av_lo", "av_sum", "av_gated", "ua_h", "ua_l"))
        c_tab, c_dec, c_proj, c_rot, c_o, c_vh, c_th, c_kh, c_vl, c_g, c_kl = map(sem, (
            "c_tab", "c_dec", "c_proj", "c_rot", "c_o", "c_vh", "c_th", "c_kh", "c_vl", "c_g", "c_kl"))
        c_arg, c_mexp, c_mask = map(sem, ("c_arg", "c_mexp", "c_mask"))
        c_tr, c_Th, c_Tl, c_u, c_uf, c_ub, c_qk, c_pm, c_ph, c_pl, c_pv, c_oc = map(sem, (
            "c_tr", "c_Th", "c_Tl", "c_u", "c_uf", "c_ub", "c_qk", "c_pm", "c_ph", "c_pl", "c_pv", "c_oc"))
        c_back, c_sh, c_sl, c_x, c_xa, c_xb, c_bn, c_mv, c_y, c_yg, c_ytr, c_uh, c_ul = map(sem, (
            "c_back", "c_sh", "c_sl", "c_x", "c_xa", "c_xb", "c_bn", "c_mv", "c_y", "c_yg", "c_ytr", "c_uh", "c_ul"))
        d_gA, d_gB, d_ya, d_yb, d_tA, d_tB, d_mA, d_mB, d_mg = map(sem, (
            "d_gA", "d_gB", "d_ya", "d_yb", "d_tA", "d_tB", "d_mA", "d_mB", "d_mg"))
        d_hi, d_lo, d_out, d_res = map(sem, ("d_hi", "d_lo", "d_out", "d_res"))
        f_sq, f_y = map(sem, ("f_sq", "f_y"))
        NCONST = 16 * 9

        held = {}

        def wait_apart(eng, sem_, value):
            eng.reg_add(held[eng], value, 0)
            eng.wait_ge(consts_in, NCONST)
            eng.wait_ge(sem_, held[eng])

        block = ctx.enter_context(nc.Block())

        def xtile(t):
            return xm[:, t, :]

        @block.sync
        def _(sp):
            def unit(slot, wait_for, parts):
                sp.wait_ge(w_ready, 1 + wait_for)
                for dst_ap, src in parts:
                    sp.dma_start(dst_ap, src).then_inc(raw_in[slot], 16)

            def cols(slot, L, c0, half_rows=K // 2):
                src = w_in[bass.ds(L * DM, DM), bass.ds(c0, P)].rearrange("(k p) c -> p k c", p=P)
                return [(raw[:, slot, a:a + half_rows], src[:, a:a + half_rows]) for a in (0, half_rows)]

            with sp.Fori(0, DEPTH) as L:
                u0 = L * U_L
                with sp.Fori(0, KVH) as j:
                    n0 = u0 + j * N_B
                    for i in range(N_B):
                        before = n0 + (i - 1 if i > 1 else 0)
                        if i in (0, 1):
                            parts = cols(i % 2, L, C_QA + j * (GRP * HD) + i * P)
                        elif i == 2:
                            parts = [(raw[:, 0, :, s * HD:(s + 1) * HD],
                                      w_in[bass.ds(L * DM, DM), bass.ds(c0 + j * HD, HD)].rearrange("(k p) c -> p k c", p=P))
                                     for s, c0 in ((0, C_KA), (1, C_VA))]
                        else:
                            parts = cols(i % 2, L, C_GA + j * (GRP * HD) + (i - 3) * P)
                        unit(i % 2, before, parts)
                with sp.Fori(0, RH) as h:
                    n0 = u0 + U_C + h * N_C
                    for i, c0 in enumerate((C_QR, C_KR, C_VR, C_GR)):
                        unit(i % 2, n0 + (i - 1 if i else 0), cols(i % 2, L, c0 + h * RD))
                with sp.Fori(0, K // 2) as mm:
                    n0 = u0 + U_D1 + mm * (2 * N_D1)
                    for i in range(2 * N_D1):
                        m = mm * 2 + i // N_D1
                        slot = i % 2
                        if i % N_D1 < 2:
                            parts = cols(slot, L, C_GM + (i % N_D1) * DM + m * P)
                        else:
                            parts = [(raw[:, slot, a:a + KA], w[bass.ds(L * AW, AW), bass.ds(m * P, P)].rearrange("(k p) c -> p k c", p=P))
                                     for a, w in ((0, w_a), (KA, w_r))]
                        unit(slot, n0 + i - 1, parts)
                with sp.Fori(0, 4) as nn:
                    n0 = u0 + U_D2 + nn * N_D2
                    for i in range(N_D2):
                        src = w_o[bass.ds(L * DM, DM), bass.ds(nn * (2 * P) + i * P, P)].rearrange("(k p) c -> p k c", p=P)
                        unit(i, n0 + i - 1, [(raw[:, i, a:a + K // 2], src[:, a:a + K // 2]) for a in (0, K // 2)])

        @block.gpsimd
        def _(pool):
            held[pool] = pool.alloc_register("held_pool")
            def fill(slot, pos, n_slot, n):
                wait_apart(pool, raw_in[slot], n_slot * 32 + 32)
                hi, lo = w_hi[:, :, pos * P:(pos + 1) * P], w_lo[:, :, pos * P:(pos + 1) * P]
                nc.gpsimd.tensor_scalar(hi, raw[:, slot], 1.0, 1.0, ALU.mult, ALU.mult).then_inc(w_rounded, 1)
                pool.wait_ge(w_rounded, n + 1)
                nc.gpsimd.tensor_tensor(lo, raw[:, slot], hi.bitcast(F32), ALU.subtract).then_inc(w_ready, 1)

            pool.sem_inc(w_ready, 1)
            PER = (3 * KVH + (U_L - U_C) // 2, 2 * KVH + (U_L - U_C) // 2)
            with pool.Fori(0, DEPTH) as L:
                n0 = L * U_L
                pool.wait_ge(phase_end, 3 + L * PH_L)
                for i in range(4):
                    fill(i % 2, i, L * PER[i % 2] + i // 2, n0 + i)
                with pool.Fori(0, KVH) as j:
                    pool.wait_ge(b_proj, L * (KVH * T) + j * T + T)
                    fill(0, 0, L * PER[0] + j * 3 + 2, n0 + j * N_B + 4)
                    for t in range(T):
                        bt = L * (KVH * T) + j * T + t
                        pool.wait_ge(b_norm, bt * 2 + 2)
                        if t >= 2:
                            pool.wait_ge(b_lo, bt * 2 - 2)
                        nc.gpsimd.tensor_tensor(rta[:, t % 2].rearrange("p (h d) -> p h d", d=HD),
                                                zqk[:, t].rearrange("p (h d) -> p h d", d=HD),
                                                ctA[:, 0, t:t + 1].to_broadcast([P, GRP + 1, HD]), ALU.mult).then_inc(b_cos, 1)
                        pool.wait_ge(b_cos, bt + 1)
                        pool.wait_ge(b_sin, bt * 2 + 2)
                        nc.gpsimd.tensor_tensor(rta[:, t % 2], rta[:, t % 2], rtb[:, t % 2], ALU.add).then_inc(b_rot, 1)
                    for it in range(2 * T):
                        for s in range(2):
                            tile = L * (KVH * 4 * T) + j * (4 * T) + it * 2 + s
                            slot = (2 * it + s) % 4
                            wait_apart(pool, s_rcp, tile + 1)
                            nc.gpsimd.tensor_scalar(pp[:, (2 * it + s) % 3], pp[:, (2 * it + s) % 3], rrc[:, slot:slot + 1], 1.0,
                                                    ALU.mult, ALU.mult).then_inc(p_norm, 1)
                        if it in (2, 5, 8, 11):
                            i = (2, 5, 8, 11).index(it)
                            pool.wait_ge(b_gate, L * (KVH * 4) + j * 4 + 4)
                            fill(i % 2, i, L * PER[i % 2] + j * (3 if i % 2 == 0 else 2) + (3 if i % 2 == 0 else 2) + i // 2,
                                 n0 + j * N_B + N_B + i)
                with pool.Fori(0, RH) as h:
                    for t in range(T):
                        ct = L * (RH * T) + h * T + t
                        pool.wait_ge(c_rot, ct * 3 + 3)
                        nc.gpsimd.tensor_tensor(ra[:, t % 2], ra[:, t % 2], rb[:], ALU.add).then_inc(c_o, 1)
                    pool.wait_ge(c_proj, L * (RH * T) + h * T + T)
                    for i in range(4):
                        fill(i % 2, i, L * PER[i % 2] + (3, 2)[i % 2] * KVH + h * 2 + 2 + i // 2,
                             n0 + U_C + h * N_C + N_C + i)
                with pool.Fori(0, 2) as b:
                    for i in range(12):
                        m = L * K + b * 4 + i // 3
                        pool.wait_ge((d_gA, d_gB, d_yb)[i % 3], m * 2 + 2)
                        fill(i % 2, i % 4, L * PER[i % 2] + (3, 2)[i % 2] * KVH + 2 * RH + 2 + b * 6 + i // 2,
                             n0 + U_D1 + 4 + b * 12 + i)
                for i in range(4):
                    pool.wait_ge(d_out, L * (4 * T) + (i // 2 + 1) * T)
                    fill(i % 2, i, L * PER[i % 2] + (3, 2)[i % 2] * KVH + 2 * RH + K * N_D1 // 2 + 2 + i // 2,
                         n0 + U_D2 + 4 + i)

        @block.tensor
        def _(pe):
            held[pe] = pe.alloc_register("held_pe")
            def prod3(outp, pairs, n):
                for i, ((ah, al), (bh, bl)) in enumerate(pairs):
                    nc.tensor.matmul(outp, ah, bh, start=(i == 0), stop=False)
                    nc.tensor.matmul(outp, ah, bl, start=False, stop=False)
                    last = nc.tensor.matmul(outp, al, bh, start=False, stop=(i == len(pairs) - 1))
                return last

            def h_l(k, t):
                return hT_hi[:, k, t * P:(t + 1) * P], hT_lo[:, k, t * P:(t + 1) * P]

            def h_r(k, n):
                return hT_hi[:, k, n * 512:(n + 1) * 512], hT_lo[:, k, n * 512:(n + 1) * 512]

            def w_u(k, a, b):
                return w_hi[:, k, a:b], w_lo[:, k, a:b]

            pe.wait_ge(consts_in, NCONST)
            pe.wait_ge(pro_act, 1)
            pe.drain().then_inc(phase_end, 1)
            with pe.Fori(0, DEPTH) as L:
                pe.wait_ge(phase_end, 3 + L * PH_L)
                for t in range(T):
                    pe.wait_ge(h_ready, L * T + t + 1)
                    if t >= 2:
                        pe.wait_ge(h_lo, L * (2 * T) + 2 * t - 2)
                    for k in range(K):
                        last = nc.tensor.transpose(ps[:, 2 * (t % 2) + k // 4, (k % 4) * P:(k % 4 + 1) * P],
                                                   hb[:, t % 2, k * P:(k + 1) * P], idf[:])
                    last.then_inc(h_tr, 1)
                pe.drain().then_inc(phase_end, 1)

                with pe.Fori(0, KVH) as j:
                    pe.wait_ge(phase_end, 3 + L * PH_L + j * 3 + 3)
                    pe.wait_ge(w_ready, 1 + L * U_L + j * N_B + 3)
                    for t in range(T):
                        bt = L * (KVH * T) + j * T + t
                        if t >= 2:
                            pe.wait_ge(b_free, bt - 1)
                        prod3(ps[:, t % 2, 0:3 * P], [(h_l(k, t), w_u(k, 0, 3 * P)) for k in range(K)], 3 * P).then_inc(b_proj, 1)
                    for g in range(4):
                        mt, n = g // 2, g % 2
                        pos = (3, 0)[mt]
                        if n == 0:
                            pe.wait_ge(w_ready, 1 + L * U_L + j * N_B + 4 + mt)
                        if g >= 2:
                            pe.wait_ge(b_gated, L * (KVH * 4) + j * 4 + g - 1)
                        prod3(ps[:, 2 + n, :], [(w_u(k, pos * P, (pos + 1) * P), h_r(k, n)) for k in range(K)], 512).then_inc(b_gate, 1)
                    for t in range(T):
                        bt = L * (KVH * T) + j * T + t
                        pe.wait_ge(b_lo, bt * 2 + 2)
                        pe.wait_ge(b_hi, bt * 2 + 2)
                        if t >= 2:
                            pe.wait_ge(b_kT, bt - 1)
                            pe.wait_ge(b_qT, bt - 1)
                        for c in range(GRP + 2):
                            bank = 4 + 2 * (t % 2) + c // GRP
                            last = nc.tensor.transpose(ps[:, bank, (c % GRP) * P:(c % GRP + 1) * P].bitcast(F32R),
                                                       qs[:, t % 2, c], idr[:])
                        last.then_inc(b_tr, 1)
                    b2 = L * (KVH * T) + j * T
                    a0 = L * (KVH * 4 * T) + j * (4 * T)
                    pe.wait_ge(b_qT, b2 + T)
                    pe.wait_ge(b_kT, b2 + T)
                    pe.wait_ge(b_free, b2 + T)
                    pe.wait_ge(b_gated, L * (KVH * 4) + j * 4 + 4)
                    for i in range(2 * T + 2):
                        if i < 2 * T:
                            for s in range(2):
                                tile = 2 * i + s
                                hh, t = tile // T, tile % T
                                if i >= 1:
                                    pe.wait_ge(s_exp, a0 + tile - 1)
                                for c in range(2):
                                    for n in range(2):
                                        last = nc.tensor.matmul(ps[:, 2 * s + n, :], q_st[:, hh, t * P:(t + 1) * P],
                                                                k_st[:, c, n * 512:(n + 1) * 512], start=(c == 0), stop=(c == 1))
                                last.then_inc(s_done, 1)
                        if 1 <= i <= 2 * T:
                            for s in range(2):
                                tile = 2 * (i - 1) + s
                                pe.wait_ge(p_norm, a0 + tile + 1)
                                for half in range(2):
                                    g = 2 * tile + half
                                    if g >= 2:
                                        pe.wait_ge(p_lo, a0 * 2 + g - 1)
                                    for kb in range(4):
                                        last = nc.tensor.transpose(ps[:, 4 + g % 2, kb * P:(kb + 1) * P],
                                                                   pp[:, tile % 3, (4 * half + kb) * P:(4 * half + kb + 1) * P], idf[:])
                                    last.then_inc(p_tr, 1)
                        if i >= 2:
                            e = i - 2
                            it = L * (KVH * 2 * T) + j * (2 * T) + e
                            pe.wait_ge(p_lo, a0 * 2 + 4 * e + 4)
                            if e >= 2:
                                pe.wait_ge(av_sum, it - 1)
                            for kb in range(T):
                                nc.tensor.matmul(ps[:, 6 + e % 2, 0:256], v_st[:, kb], pT_hi[:, e % 2, kb],
                                                 start=(kb == 0), stop=False)
                                last = nc.tensor.matmul(ps[:, 6 + e % 2, 0:256], v_st[:, kb], pT_lo[:, e % 2, kb],
                                                        start=False, stop=(kb == T - 1))
                            last.then_inc(pv_done, 1)
                    pe.drain().then_inc(phase_end, 1)

                with pe.Fori(0, RH) as h:
                    pe.wait_ge(phase_end, 3 + L * PH_L + h * 3 + 3 * (1 + KVH))
                    pe.wait_ge(w_ready, 1 + L * U_L + h * N_C + U_C + N_C)
                    c0 = L * (RH * T) + h * T
                    f0 = L * (RH * (T - 1)) + h * (T - 1)

                    def project(t):
                        if t >= 2:
                            pe.wait_ge(c_g, c0 + t - 1)
                            pe.wait_ge(c_rot, c0 * 3 + 3 * t - 3)
                        prod3(ps[:, t % 2, :], [(h_l(k, t), w_u(k, 0, 512)) for k in range(K)], 512).then_inc(c_proj, 1)

                    def chunk(t):
                        pe.wait_ge(c_o, c0 + t + 1)
                        if t >= 1:
                            pe.wait_ge(c_Tl, c0 * 2 + 2 * t)
                        nc.tensor.transpose(ps[:, 2, 0:P], ra[:, t % 2, 0:RD], idf[:])
                        nc.tensor.transpose(ps[:, 2, P:2 * P], ra[:, t % 2, RD:2 * RD], idf[:]).then_inc(c_tr, 1)
                        pe.wait_ge(c_vl, c0 * 3 + 3 * t + 3)
                        pe.wait_ge(c_kl, c0 + t + 1)
                        if t >= 1:
                            pe.wait_ge(c_uf, f0 + t)
                            if t >= 2:
                                pe.wait_ge(c_ub, f0 + t - 1)
                        prod3(ps[:, 3, 0:2 * RD], [((kn_[:, t % 2, 0], kn_[:, t % 2, 1]), (vd[:, t % 2, 0], vd[:, t % 2, 1]))], 256).then_inc(c_u, 1)
                        pe.wait_ge(c_Tl, c0 * 2 + 2 * t + 2)
                        if t >= 1:
                            pe.wait_ge(c_pm, c0 + t)
                        prod3(ps[:, 4, 0:P], [((kT[:, t % 2, 0], kT[:, t % 2, 1]), (qT_hi[:, t], qT_lo[:, t]))], P).then_inc(c_qk, 1)

                    def within(t):
                        pe.wait_ge(c_pl, c0 + t + 1)
                        if t >= 1:
                            pe.wait_ge(c_oc, c0 + t)
                        prod3(ps[:, 5, 0:RD], [((pq[:, t % 2, 0], pq[:, t % 2, 1]), (vn[:, t % 2, 0], vn[:, t % 2, 1]))], RD).then_inc(c_pv, 1)

                    for t in range(T + 2):
                        if t < T:
                            project(t)
                        if t >= 2:
                            within(t - 2)
                        if 1 <= t <= T:
                            chunk(t - 1)
                    for t in range(T):
                        pe.wait_ge(c_sl, c0 + t + 1)
                        if t >= 2:
                            pe.wait_ge(c_xb, c0 + t - 1)
                        prod3(ps[:, 6 + t % 2, 0:2 * RD], [((qT_hi[:, t], qT_lo[:, t]), (sst[:, 0], sst[:, 1]))], 256).then_inc(c_x, 1)
                    for t in range(T):
                        pe.wait_ge(c_yg, c0 + t + 1)
                        nc.tensor.transpose(ps[:, 2 + t // 4, (t % 4) * P:(t % 4 + 1) * P], pm[:, t % 2], idf[:]).then_inc(c_ytr, 1)
                    pe.drain().then_inc(phase_end, 1)

                wait_apart(pe, phase_end, 3 + L * PH_L + 3 * (1 + KVH + RH))
                with pe.Fori(0, 2) as b:
                    for i in range(4):
                        m = L * K + b * 4 + i
                        for kind in range(3):
                            pos = (3 * i + kind) % 4
                            pe.wait_ge(w_ready, 1 + L * U_L + b * 12 + U_D1 + 3 * i + kind + 1)
                            if kind < 2:
                                for n in range(2):
                                    pe.wait_ge((d_tA, d_tB)[kind], m * 2 + n if i else m * 2 + 1)
                                    prod3(ps[:, 4 * n + kind, :], [(w_u(k, pos * P, (pos + 1) * P), h_r(k, n)) for k in range(K)],
                                          512).then_inc((d_gA, d_gB)[kind], 1)
                            else:
                                for br, (uh, ul) in enumerate(((ua_hi, ua_lo), (ur_hi, ur_lo))):
                                    for n in range(2):
                                        pe.wait_ge((d_mA, d_mB)[br], m * 2 + n if i else m * 2 + 1)
                                        prod3(ps[:, 4 * n + 2 + br, :],
                                              [(w_u(br * KA + k, pos * P, (pos + 1) * P),
                                                (uh[:, k, n * 512:(n + 1) * 512], ul[:, k, n * 512:(n + 1) * 512])) for k in range(KA)],
                                              512).then_inc((d_ya, d_yb)[br], 1)
                pe.drain().then_inc(phase_end, 1)

                wait_apart(pe, phase_end, 3 + L * PH_L + 3 * (2 + KVH + RH))
                with pe.Fori(0, 2) as b:
                    pe.wait_ge(d_lo, L * K + K)
                    for i in range(2):
                        pe.wait_ge(w_ready, 1 + L * U_L + b * 4 + U_D2 + 2 * i + 2)
                        for t in range(T):
                            o = L * (4 * T) + b * (2 * T) + i * T + t
                            pe.wait_ge(d_res, o - T + 2 if i else L * (4 * T) + b * (2 * T) + 1)
                            prod3(ps[:, t, 0:256], [(h_l(k, t), w_u(k, 256 * i, 256 * (i + 1))) for k in range(K)], 256).then_inc(d_out, 1)
                pe.drain().then_inc(phase_end, 1)

        @block.scalar
        def _(act):
            for d, s in ((idf[:], ident), (dst[:], dist), (icol[:], idx)):
                act.dma_start(d, s).then_inc(consts_in, 16)
            for i, src in enumerate((dec_f, dec_b)):
                for L in range(DEPTH):
                    act.dma_start(lgw[:, 0, (i * DEPTH + L) * RH:(i * DEPTH + L + 1) * RH],
                                  src[L:L + 1, :].to_broadcast([P, RH])).then_inc(consts_in, 16)
            for a in (0, 1):
                act.dma_start(xm[:, a * 4:a * 4 + 4], x.rearrange("(t p) d -> p t d", p=P)[:, a * 4:a * 4 + 4]).then_inc(consts_in, 16)
            act.wait_ge(consts_in, NCONST)
            nc.scalar.copy(idr[:], idf[:]).then_inc(pro_act, 1)
            act.wait_ge(pro_dve, 2)
            nc.scalar.activation(lgw[:, 2], lgw[:, 1], ACT.Exp).then_inc(pro_act, 1)
            act.wait_ge(pro_dve, 22)
            nc.scalar.activation(dec[:, :, 0:6], dec[:, :, 0:6], ACT.Exp).then_inc(pro_act, 1)
            for s in (d_tA, d_tB):
                act.sem_inc(s, 1)
            act.drain().then_inc(phase_end, 1)

            with act.Fori(0, DEPTH) as L:
                act.wait_ge(phase_end, 3 + L * PH_L)
                act.dma_start(gB[:], norm_g[bass.ds(L, 1), :].to_broadcast([P, DM])).then_inc(gain_in, 16)
                act.dma_start(xs.rearrange("(t p) d -> p t d", p=P), xm[:]).then_inc(x_saved, 16)
                for t in range(T):
                    if t:
                        act.wait_ge(a_sq, L * T + t)
                    nc.scalar.activation(junk[:], xtile(t), ACT.Square, accum_out=ss[:, t:t + 1]).then_inc(a_sq, 1)
                for t in range(T):
                    if t == T - 1:
                        act.wait_ge(x_saved, L * 16 + 16)
                    act.wait_ge(h_tr, L * T + t + 1)
                    for half in range(2):
                        nc.scalar.copy(hT_hi[:, 4 * half:4 * half + 4, t * P:(t + 1) * P],
                                       ps[:, 2 * (t % 2) + half].rearrange("p (k c) -> p k c", c=P)).then_inc(h_hi, 1)
                act.drain().then_inc(phase_end, 1)

                with act.Fori(0, KVH) as j:
                    act.wait_ge(phase_end, 3 + L * PH_L + j * 3 + 3)
                    for c in range(2):
                        act.dma_start(ctA[:, c], rope_a[:, c]).then_inc(b_tab, 16)
                    for hh in range(GRP):
                        act.dma_start(gqk[:, hh * HD:(hh + 1) * HD], qn[bass.ds(L, 1), :].to_broadcast([P, HD])).then_inc(b_tab, 16)
                    act.dma_start(gqk[:, GRP * HD:], kn[bass.ds(L, 1), :].to_broadcast([P, HD])).then_inc(b_tab, 16)
                    for t in range(T):
                        bt = L * (KVH * T) + j * T + t
                        act.wait_ge(b_proj, bt + 1)
                        if t >= 2:
                            act.wait_ge(b_ssum, bt - 1)
                        nc.scalar.activation(sq[:, t % 2], ps[:, t % 2, 0:QK_W], ACT.Square).then_inc(b_sq, 1)
                        nc.scalar.copy(v_st[:, t, 0:HD], ps[:, t % 2, QK_W:QK_W + HD]).then_inc(b_vh, 1)
                    for g in range(4):
                        act.wait_ge(b_gate, L * (KVH * 4) + j * 4 + g + 1)
                        if g >= 2:
                            act.wait_ge(b_gated, L * (KVH * 4) + j * 4 + g - 1)
                        nc.scalar.activation(thA[:, g % 2], ps[:, 2 + g % 2], ACT.Tanh, scale=0.5).then_inc(b_tanh, 1)
                    for t in range(T + 1):
                        if t < T:
                            bt = L * (KVH * T) + j * T + t
                            act.wait_ge(b_rot, bt + 1)
                            if t >= 2:
                                act.wait_ge(b_tr, bt - 1)
                            nc.scalar.copy(qs[:, t % 2, 0:GRP, 0:HD],
                                           rta[:, t % 2, 0:GRP * HD].rearrange("p (h d) -> p h d", d=HD)).then_inc(b_hi, 1)
                            nc.scalar.copy(qs[:, t % 2, GRP].rearrange("p (r d) -> p r d", d=HD),
                                           rta[:, t % 2:t % 2 + 1, GRP * HD:].to_broadcast([P, 2, HD])).then_inc(b_hi, 1)
                        if t >= 1:
                            act.wait_ge(b_tr, L * (KVH * T) + j * T + t)
                            nc.scalar.copy(q_st[:, :, (t - 1) * P:t * P],
                                           ps[:, 4 + 2 * ((t - 1) % 2)].rearrange("p (h c) -> p h c", c=P)).then_inc(b_qT, 1)
                    a0 = L * (KVH * 4 * T) + j * (4 * T)
                    for i in range(2 * T + 2):
                        if i < 2 * T:
                            for s in range(2):
                                tile = 2 * i + s
                                act.wait_ge(s_max, a0 + tile + 1)
                                if tile >= 3:
                                    act.wait_ge(p_tr, a0 * 2 + 2 * tile - 4)
                                nc.scalar.activation(pp[:, tile % 3], ps[:, 2 * s:2 * s + 2].rearrange("p a b -> p (a b)"), ACT.Exp,
                                                     bias=nmx[:, tile % 4:tile % 4 + 1],
                                                     accum_out=rsm[:, tile % 4:tile % 4 + 1]).then_inc(s_exp, 1)
                        if 1 <= i <= 2 * T:
                            e = i - 1
                            for gg in range(4):
                                g = 4 * e + gg
                                act.wait_ge(p_tr, a0 * 2 + g + 1)
                                if e >= 2:
                                    act.wait_ge(pv_done, L * (KVH * 2 * T) + j * (2 * T) + e - 1)
                                nc.scalar.copy(pT_hi[:, e % 2, 4 * (gg % 2):4 * (gg % 2) + 4, (gg // 2) * P:(gg // 2 + 1) * P],
                                               ps[:, 4 + g % 2].rearrange("p (k c) -> p k c", c=P)).then_inc(p_hi, 1)
                        if i >= 2:
                            e = i - 2
                            it = L * (KVH * 2 * T) + j * (2 * T) + e
                            hh, qp = e // 4, e % 4
                            pr = HD * (hh % 2)
                            act.wait_ge(pv_done, it + 1)
                            if e >= 2:
                                act.wait_ge(ua_l, it - 1)
                            nc.scalar.copy(av[pr:pr + HD, e % 2], ps[HD:2 * HD, 6 + e % 2, 0:256]).then_inc(av_lo, 1)
                            act.wait_ge(consts_in, NCONST)
                            act.wait_ge(av_gated, it + 1)
                            nc.scalar.copy(ua_hi[pr:pr + HD, bass.ds(j * 2 + hh // 2, 1), qp * 256:(qp + 1) * 256],
                                           av[pr:pr + HD, e % 2:e % 2 + 1]).then_inc(ua_h, 1)
                    act.drain().then_inc(phase_end, 1)

                act.wait_ge(phase_end, 3 + L * PH_L + 3 * (1 + KVH))
                for c in range(2):
                    act.dma_start(ctR[:, c], rope_r[:, c]).then_inc(c_tab, 16)
                act.dma_start(gwc[:], gn_w[:, bass.ds(L, 1), :].rearrange("p a h -> p (a h)")).then_inc(c_tab, 16)
                with act.Fori(0, RH) as h:
                    act.wait_ge(phase_end, 3 + L * PH_L + h * 3 + 3 * (1 + KVH))
                    c0 = L * (RH * T) + h * T
                    f0 = L * (RH * (T - 1)) + h * (T - 1)
                    act.wait_ge(c_arg, (L * RH + h) * 2 + 2)
                    nc.scalar.activation(thC[:], msk[:], ACT.Exp).then_inc(c_mexp, 1)

                    def outputs(t):
                        act.wait_ge(c_proj, c0 + t + 1)
                        if t >= 2:
                            act.wait_ge(c_pv, c0 + t - 1)
                        v = ps[:, t % 2, 2 * RD:3 * RD]
                        nc.scalar.copy(vn[:, t % 2, 0], v).then_inc(c_vh, 1)
                        nc.scalar.activation(vd[:, t % 2, 0, 0:RD], v, ACT.Copy, scale=dcur[:, 2:3]).then_inc(c_vh, 1)
                        nc.scalar.activation(vd[:, t % 2, 0, RD:], v, ACT.Copy, scale=dcur[:, 3:4]).then_inc(c_vh, 1)
                        if t == 0:
                            act.wait_ge(c_mask, L * RH + h + 1)
                        else:
                            act.wait_ge(c_g, c0 + t)
                        nc.scalar.activation(thC[:], ps[:, t % 2, 3 * RD:], ACT.Tanh, scale=0.5).then_inc(c_th, 1)

                    def chunk(t):
                        act.wait_ge(c_o, c0 + t + 1)
                        nc.scalar.copy(kn_[:, t % 2, 0], ra[:, t % 2, RD:]).then_inc(c_kh, 1)
                        act.wait_ge(c_tr, c0 + t + 1)
                        nc.scalar.copy(qT_hi[:, t], ps[:, 2, 0:P]).then_inc(c_Th, 1)
                        nc.scalar.copy(kT[:, t % 2, 0], ps[:, 2, P:2 * P]).then_inc(c_Th, 1)
                        act.wait_ge(c_u, c0 + t + 1)
                        if t >= 1:
                            nc.scalar.copy(us[:, 1, t - 1], ps[:, 3, RD:2 * RD]).then_inc(c_ub, 1)
                        act.wait_ge(c_pm, c0 + t + 1)
                        if t >= 2:
                            act.wait_ge(c_pv, c0 + t - 1)
                        nc.scalar.copy(pq[:, t % 2, 0], pm[:, t % 2]).then_inc(c_ph, 1)

                    for t in range(T + 2):
                        if t < T:
                            outputs(t)
                        if 1 <= t <= T:
                            chunk(t - 1)
                        if t >= 2:
                            act.wait_ge(c_pv, c0 + t - 1)
                            nc.scalar.copy(oc[:, t - 2], ps[:, 5, 0:RD]).then_inc(c_oc, 1)
                    for t in range(T):
                        act.wait_ge(c_back, (L * RH + h) * 8 + 8)
                        if t >= 1:
                            act.wait_ge(c_x, c0 + t)
                        nc.scalar.copy(sst[:, 0].rearrange("p (s d) -> p s d", d=RD), us[:, :, t]).then_inc(c_sh, 1)
                    for half in range(2):
                        act.wait_ge(consts_in, NCONST)
                        act.wait_ge(c_ytr, c0 + 4 * half + 4)
                        nc.scalar.activation(ur_hi[:, bass.ds(h, 1), half * 512:(half + 1) * 512], ps[:, 2 + half:3 + half], ACT.Copy,
                                             scale=dcur[:, 6:7]).then_inc(c_uh, 1)
                    act.drain().then_inc(phase_end, 1)

                act.wait_ge(consts_in, NCONST)
                act.wait_ge(phase_end, 3 + L * PH_L + 3 * (1 + KVH + RH))
                with act.Fori(0, 2) as b:
                    for i in range(4):
                        m = L * K + b * 4 + i
                        for kind in range(2):
                            for n in range(2):
                                act.wait_ge((d_gA, d_gB)[kind], m * 2 + n + 1)
                                act.wait_ge(d_mg, m * 2 + n if i else m * 2 + 1)
                                nc.scalar.activation((tA, tB)[kind][:, n], ps[:, 4 * n + kind], ACT.Tanh, scale=0.5).then_inc((d_tA, d_tB)[kind], 1)
                act.drain().then_inc(phase_end, 1)

                act.wait_ge(phase_end, 3 + L * PH_L + 3 * (2 + KVH + RH))
                for k in range(K):
                    nc.scalar.copy(hT_hi[:, k], xm[:, k]).then_inc(d_hi, 1)
                act.wait_ge(d_lo, L * K + K)
                act.wait_ge(x_saved, L * 16 + 16)
                act.dma_start(xm[:], xs.rearrange("(t p) d -> p t d", p=P)).then_inc(x_back, 16)
                act.drain().then_inc(phase_end, 1)

            act.wait_ge(phase_end, 3 + DEPTH * PH_L)
            act.dma_start(gB[:], fin_g.to_broadcast([P, DM])).then_inc(gain_in, 16)
            for t in range(T):
                if t:
                    act.wait_ge(f_sq, t)
                nc.scalar.activation(junk[:], xtile(t), ACT.Square, accum_out=ss[:, t:t + 1]).then_inc(f_sq, 1)
            for t in range(T):
                act.wait_ge(f_y, t + 1)
                act.dma_start(out.rearrange("(t p) d -> p t d", p=P)[:, t], hb[:, t % 2]).then_inc(out_done[t % 2], 16)
            for s in range(2):
                act.wait_ge(out_done[s], 16 * (T // 2))

        @block.vector
        def _(dve):
            held[dve] = dve.alloc_register("held_dve")
            V = nc.vector

            def rsqrt(v, n, base):
                y, t_ = rs[:, 0:n], nt[:, 0:n]
                V.tensor_scalar(y.bitcast(I32), v.bitcast(I32), -0.5, MAGIC, ALU.mult, ALU.add).then_inc(newton, 1)
                for r in range(3):
                    dve.wait_ge(newton, base + 3 * r + 1)
                    V.scalar_tensor_tensor(t_, y, -0.5, y, ALU.mult, ALU.mult).then_inc(newton, 1)
                    dve.wait_ge(newton, base + 3 * r + 2)
                    V.tensor_tensor(t_, t_, v, ALU.mult).then_inc(newton, 1)
                    dve.wait_ge(newton, base + 3 * r + 3)
                    V.scalar_tensor_tensor(y, t_, 1.5, y, ALU.add, ALU.mult).then_inc(newton, 1)
                dve.wait_ge(newton, base + 10)

            NW_L = 11 * (1 + KVH + RH)

            done = [0]

            def step(ins):
                done[0] += 1
                ins.then_inc(pro_dve, 1)
                dve.wait_ge(pro_dve, done[0])

            dve.wait_ge(consts_in, NCONST)
            step(V.tensor_scalar(lgw[:, 1], lgw[:, 0], -1.0, None, ALU.mult))
            step(V.tensor_tensor(lgw[:, 1], lgw[:, 1], lgw[:, 0], ALU.min))
            dve.wait_ge(pro_act, 2)
            step(V.tensor_scalar(lgw[:, 3], lgw[:, 2], 2.0, None, ALU.add))
            step(V.reciprocal(lgw[:, 3], lgw[:, 3]))
            step(V.tensor_tensor(lgw[:, 3], lgw[:, 3], lgw[:, 2], ALU.mult))
            step(V.tensor_tensor(lgw[:, 4], lgw[:, 3], lgw[:, 3], ALU.mult))
            step(V.tensor_scalar(lgw[:, 5], lgw[:, 4], 1.0 / 15, None, ALU.mult))
            for c in (13, 11, 9, 7, 5, 3):
                step(V.scalar_tensor_tensor(lgw[:, 5], lgw[:, 5], 1.0 / c, lgw[:, 4], ALU.add, ALU.mult))
            step(V.scalar_tensor_tensor(lgw[:, 5], lgw[:, 5], 1.0, lgw[:, 3], ALU.add, ALU.mult))
            step(V.tensor_scalar(lgw[:, 2], lgw[:, 0], 0.0, None, ALU.min))
            step(V.scalar_tensor_tensor(lgw[:, 2], lgw[:, 5], -2.0, lgw[:, 2], ALU.mult, ALU.add))
            half = DEPTH * RH
            for c in range(6):
                a = (c % 2) * half
                ins = V.tensor_scalar(dec[:, :, c], lgw[:, 2, a:a + half], icol[:, c:c + 1], None, ALU.mult)
                if c == 5:
                    step(ins)
                else:
                    ins.then_inc(pro_dve, 1)
                    done[0] += 1
            assert done[0] == 22, done
            dve.wait_ge(pro_act, 3)
            for c in (2, 3):
                step(V.tensor_scalar(dec[:, :, c], dec[:, :, c], RD ** -0.5, None, ALU.mult))
            for c in (6, 7):
                step(V.tensor_copy(dec[:, :, c], lgw[:, 2, (c - 6) * half:(c - 5) * half]))
            for s in (d_mA, d_mB, d_mg, d_res):
                dve.sem_inc(s, 1)
            dve.drain().then_inc(phase_end, 1)

            with dve.Fori(0, DEPTH) as L:
                dve.wait_ge(phase_end, 3 + L * PH_L)
                dve.wait_ge(a_sq, L * T + T)
                nw = L * NW_L
                V.tensor_scalar(ss[:, 0:T], ss[:, 0:T], 1.0 / DM, EPS, ALU.mult, ALU.add).then_inc(newton, 1)
                dve.wait_ge(newton, nw + 1)
                rsqrt(ss[:, 0:T], T, nw + 1)
                dve.wait_ge(gain_in, L * 16 + 16)
                for t in range(T + 1):
                    if t < T:
                        if t >= 2:
                            dve.wait_ge(h_tr, L * T + t - 1)
                        V.scalar_tensor_tensor(hb[:, t % 2], xtile(t), rs[:, t:t + 1], gB[:], ALU.mult, ALU.mult).then_inc(h_ready, 1)
                    if t >= 1:
                        for hf in range(2):
                            dve.wait_ge(h_hi, L * (2 * T) + 2 * (t - 1) + hf + 1)
                            o = (slice(None), slice(4 * hf, 4 * hf + 4), slice((t - 1) * P, t * P))
                            V.tensor_tensor(hT_lo[o], ps[:, 2 * ((t - 1) % 2) + hf].rearrange("p (k c) -> p k c", c=P),
                                            hT_hi[o].bitcast(F32), ALU.subtract).then_inc(h_lo, 1)
                dve.drain().then_inc(phase_end, 1)

                with dve.Fori(0, KVH) as j:
                    dve.wait_ge(phase_end, 3 + L * PH_L + j * 3 + 3)
                    lj = L * KVH + j
                    dve.wait_ge(b_tab, lj * (16 * (3 + GRP)) + 16 * (3 + GRP))
                    V.tensor_scalar(gqk[:, 0:GRP * HD], gqk[:, 0:GRP * HD], HD ** -0.5, None, ALU.mult).then_inc(b_gain, 1)
                    for t in range(T):
                        bt = lj * T + t
                        dve.wait_ge(b_vh, bt + 1)
                        V.tensor_copy(zqk[:, t], ps[:, t % 2, 0:QK_W]).then_inc(b_z, 1)
                        dve.wait_ge(b_sq, bt + 1)
                        V.tensor_reduce(ss[:, t * (GRP + 1):(t + 1) * (GRP + 1)],
                                        sq[:, t % 2].rearrange("p (h d) -> p h d", d=HD), AXX, ALU.add).then_inc(b_ssum, 1)
                        V.tensor_tensor(v_st[:, t, HD:], ps[:, t % 2, QK_W:QK_W + HD], v_st[:, t, 0:HD].bitcast(F32),
                                        ALU.subtract).then_inc(b_free, 1)
                    n5 = T * (GRP + 1)
                    nw = L * NW_L + j * 11 + 11
                    dve.wait_ge(b_ssum, lj * T + T)
                    V.tensor_scalar(ss[:, 0:n5], ss[:, 0:n5], 1.0 / HD, EPS, ALU.mult, ALU.add).then_inc(newton, 1)
                    dve.wait_ge(newton, nw + 1)
                    rsqrt(ss[:, 0:n5], n5, nw + 1)
                    dve.wait_ge(b_gain, lj + 1)

                    def gate(g):
                        dve.wait_ge(b_tanh, lj * 4 + g + 1)
                        V.scalar_tensor_tensor(gT[:, g // 2, (g % 2) * 512:(g % 2 + 1) * 512], thA[:, g % 2], 1.0, ps[:, 2 + g % 2],
                                               ALU.add, ALU.mult).then_inc(b_gated, 1)

                    def rotate(t):
                        bt = lj * T + t
                        z = zqk[:, t].rearrange("p (h d) -> p h d", d=HD)
                        if t == 0:
                            dve.wait_ge(b_z, lj * T + T)
                        V.tensor_tensor(z, z, rs[:, t * (GRP + 1):(t + 1) * (GRP + 1)].rearrange("p (h o) -> p h o", o=1)
                                        .to_broadcast([P, GRP + 1, HD]), ALU.mult).then_inc(b_norm, 1)
                        dve.wait_ge(b_norm, bt * 2 + 1)
                        V.tensor_tensor(zqk[:, t], zqk[:, t], gqk[:], ALU.mult).then_inc(b_norm, 1)
                        dve.wait_ge(b_norm, bt * 2 + 2)
                        if t >= 2:
                            dve.wait_ge(b_rot, bt - 1)
                        z5 = zqk[:, t].rearrange("p (h a s d) -> p h a s d", a=2, s=2, d=HD // 4)
                        r5 = rtb[:, t % 2].rearrange("p (h a s d) -> p h a s d", a=2, s=2, d=HD // 4)
                        s5 = ctA[:, 1, t:t + 1].rearrange("p o (a s d) -> p o a s d", a=2, s=2, d=HD // 4)
                        for s in range(2):
                            V.tensor_tensor(r5[:, :, :, s], z5[:, :, :, 1 - s],
                                            s5[:, :, :, s].to_broadcast([P, GRP + 1, 2, HD // 4]), ALU.mult).then_inc(b_sin, 1)

                    def split(t):
                        bt = lj * T + t
                        dve.wait_ge(b_hi, bt * 2 + 2)
                        if t >= 2:
                            dve.wait_ge(b_tr, bt - 1)
                        V.tensor_tensor(qs[:, t % 2, 0:GRP, HD:], rta[:, t % 2, 0:GRP * HD].rearrange("p (h d) -> p h d", d=HD),
                                        qs[:, t % 2, 0:GRP, 0:HD].bitcast(F32), ALU.subtract).then_inc(b_lo, 1)
                        V.tensor_tensor(qs[:, t % 2, GRP + 1].rearrange("p (r d) -> p r d", d=HD),
                                        rta[:, t % 2:t % 2 + 1, GRP * HD:].to_broadcast([P, 2, HD]),
                                        qs[:, t % 2, GRP].rearrange("p (r d) -> p r d", d=HD).bitcast(F32), ALU.subtract).then_inc(b_lo, 1)

                    for t in range(T + 2):
                        if t < T:
                            rotate(t)
                            if t < 4:
                                gate(t)
                        if 1 <= t <= T:
                            split(t - 1)
                        if t >= 2:
                            dve.wait_ge(b_tr, lj * T + t - 1)
                            V.tensor_copy(k_st[:, :, (t - 2) * P:(t - 1) * P],
                                          ps[:, 5 + 2 * (t % 2), 0:2 * P].rearrange("p (h c) -> p h c", c=P)).then_inc(b_kT, 1)
                    a0 = lj * (4 * T)
                    for i in range(2 * T + 2):
                        if i < 2 * T:
                            for s in range(2):
                                tile = 2 * i + s
                                dve.wait_ge(s_done, a0 + tile + 1)
                                V.tensor_reduce(nmx[:, tile % 4:tile % 4 + 1], ps[:, 2 * s:2 * s + 2].rearrange("p a b -> p (a b)"),
                                                AXX, ALU.max, negate=True).then_inc(s_max, 1)
                        if 1 <= i <= 2 * T:
                            e = i - 1
                            for gg in range(4):
                                g = 4 * e + gg
                                dve.wait_ge(p_hi, a0 * 2 + g + 1)
                                o = (slice(None), e % 2, slice(4 * (gg % 2), 4 * (gg % 2) + 4), slice((gg // 2) * P, (gg // 2 + 1) * P))
                                V.tensor_tensor(pT_lo[o], ps[:, 4 + g % 2].rearrange("p (k c) -> p k c", c=P),
                                                pT_hi[o].bitcast(F32), ALU.subtract).then_inc(p_lo, 1)
                        if i < 2 * T:
                            for s in range(2):
                                tile = 2 * i + s
                                dve.wait_ge(s_exp, a0 + tile + 1)
                                V.reciprocal(rrc[:, tile % 4:tile % 4 + 1], rsm[:, tile % 4:tile % 4 + 1]).then_inc(s_rcp, 1)
                        if i >= 2:
                            e = i - 2
                            it = lj * (2 * T) + e
                            hh, qp = e // 4, e % 4
                            pr = HD * (hh % 2)
                            dve.wait_ge(av_lo, it + 1)
                            V.tensor_tensor(av[pr:pr + HD, e % 2], ps[0:HD, 6 + e % 2, 0:256], av[pr:pr + HD, e % 2],
                                            ALU.add).then_inc(av_sum, 1)
                            dve.wait_ge(av_sum, it + 1)
                            V.scalar_tensor_tensor(av[pr:pr + HD, e % 2], av[pr:pr + HD, e % 2], 0.5,
                                                   gT[pr:pr + HD, hh // 2, qp * 256:(qp + 1) * 256], ALU.mult, ALU.mult).then_inc(av_gated, 1)
                            dve.wait_ge(consts_in, NCONST)
                            dve.wait_ge(ua_h, it + 1)
                            o = (slice(pr, pr + HD), bass.ds(j * 2 + hh // 2, 1), slice(qp * 256, (qp + 1) * 256))
                            V.tensor_tensor(ua_lo[o], av[pr:pr + HD, e % 2:e % 2 + 1], ua_hi[o].bitcast(F32), ALU.subtract).then_inc(ua_l, 1)
                    dve.drain().then_inc(phase_end, 1)

                with dve.Fori(0, RH) as h:
                    dve.wait_ge(consts_in, NCONST)
                    dve.wait_ge(phase_end, 3 + L * PH_L + h * 3 + 3 * (1 + KVH))
                    dve.wait_ge(c_tab, L * 48 + 48)
                    lh = L * RH + h
                    c0, f0 = lh * T, lh * (T - 1)
                    V.tensor_copy(dcur[:], dec[:, bass.ds(lh, 1)].rearrange("p o c -> p (o c)")).then_inc(c_dec, 1)
                    dve.wait_ge(c_dec, lh * 2 + 1)
                    V.tensor_scalar(msk[:], dst[:, 0], dcur[:, 6:7], None, ALU.mult).then_inc(c_arg, 1)
                    dve.wait_ge(c_arg, lh * 2 + 1)
                    V.scalar_tensor_tensor(msk[:], dst[:, 1], dcur[:, 7:8], msk[:], ALU.mult, ALU.add).then_inc(c_arg, 1)
                    dve.wait_ge(consts_in, NCONST)
                    dve.wait_ge(c_arg, lh * 2 + 2)
                    V.tensor_scalar(dcur[:, 6:7], gwc[:, bass.ds(h, 1)], 0.5, None, ALU.mult).then_inc(c_dec, 1)
                    dve.wait_ge(c_mexp, lh + 1)
                    V.tensor_scalar(msk[:], thC[:], RD ** -0.5, None, ALU.mult).then_inc(c_mask, 1)
                    V.memset(us[:, 0, 0], 0.0).then_inc(c_back, 1)
                    V.memset(us[:, 1, T - 1], 0.0).then_inc(c_back, 1)
                    dve.wait_ge(c_mask, lh + 1)

                    def outputs(t):
                        dve.wait_ge(c_th, c0 + t + 1)
                        b = t % 2
                        if t >= 2:
                            dve.wait_ge(c_tr, c0 + t - 1)
                            dve.wait_ge(c_kl, c0 + t - 1)
                        if t >= 1:
                            dve.wait_ge(c_o, c0 + t)
                        z = ps[:, b, 0:2 * RD]
                        V.tensor_tensor(ra[:, b].rearrange("p (h d) -> p h d", d=RD), z.rearrange("p (h d) -> p h d", d=RD),
                                        ctR[:, 0, t:t + 1].to_broadcast([P, 2, RD]), ALU.mult).then_inc(c_rot, 1)
                        z5 = z.rearrange("p (h a s d) -> p h a s d", a=2, s=2, d=RD // 4)
                        r5 = rb[:].rearrange("p (h a s d) -> p h a s d", a=2, s=2, d=RD // 4)
                        s5 = ctR[:, 1, t:t + 1].rearrange("p o (a s d) -> p o a s d", a=2, s=2, d=RD // 4)
                        for s in range(2):
                            V.tensor_tensor(r5[:, :, :, s], z5[:, :, :, 1 - s],
                                            s5[:, :, :, s].to_broadcast([P, 2, 2, RD // 4]), ALU.mult).then_inc(c_rot, 1)
                        v = ps[:, b, 2 * RD:3 * RD]
                        V.tensor_tensor(vn[:, b, 1], v, vn[:, b, 0].bitcast(F32), ALU.subtract).then_inc(c_vl, 1)
                        for s in range(2):
                            o = slice(s * RD, (s + 1) * RD)
                            V.scalar_tensor_tensor(vd[:, b, 1, o], v, dcur[:, 2 + s:3 + s], vd[:, b, 0, o].bitcast(F32),
                                                   ALU.mult, ALU.subtract).then_inc(c_vl, 1)
                        V.scalar_tensor_tensor(g2[:, t], thC[:], 1.0, ps[:, b, 3 * RD:], ALU.add, ALU.mult).then_inc(c_g, 1)

                    def chunk(t):
                        b = t % 2
                        dve.wait_ge(c_kh, c0 + t + 1)
                        V.tensor_tensor(kn_[:, b, 1], ra[:, b, RD:], kn_[:, b, 0].bitcast(F32), ALU.subtract).then_inc(c_kl, 1)
                        dve.wait_ge(c_Th, c0 * 2 + 2 * t + 2)
                        V.tensor_tensor(qT_lo[:, t], ps[:, 2, 0:P], qT_hi[:, t].bitcast(F32), ALU.subtract).then_inc(c_Tl, 1)
                        V.tensor_tensor(kT[:, b, 1], ps[:, 2, P:2 * P], kT[:, b, 0].bitcast(F32), ALU.subtract).then_inc(c_Tl, 1)
                        dve.wait_ge(c_u, c0 + t + 1)
                        if t < T - 1:
                            if t >= 1:
                                dve.wait_ge(c_ub, f0 + t)
                                dve.wait_ge(c_uf, f0 + t)
                            else:
                                dve.wait_ge(c_back, lh * 8 + 2)
                            V.scalar_tensor_tensor(us[:, 0, t + 1], us[:, 0, t], dcur[:, 4:5], ps[:, 3, 0:RD],
                                                   ALU.mult, ALU.add).then_inc(c_uf, 1)
                        dve.wait_ge(c_qk, c0 + t + 1)
                        if t >= 2:
                            dve.wait_ge(c_pl, c0 + t - 1)
                        V.tensor_tensor(pm[:, b], ps[:, 4, 0:P], msk[:], ALU.mult).then_inc(c_pm, 1)
                        dve.wait_ge(c_ph, c0 + t + 1)
                        V.tensor_tensor(pq[:, b, 1], pm[:, b], pq[:, b, 0].bitcast(F32), ALU.subtract).then_inc(c_pl, 1)

                    for t in range(T + 1):
                        if t < T:
                            outputs(t)
                        if t >= 1:
                            chunk(t - 1)
                    dve.wait_ge(c_ub, f0 + T - 1)
                    for n, c in enumerate(range(T - 3, -1, -1)):
                        if n:
                            dve.wait_ge(c_back, lh * 8 + 2 + n)
                        V.scalar_tensor_tensor(us[:, 1, c], us[:, 1, c + 1], dcur[:, 5:6], us[:, 1, c], ALU.mult, ALU.add).then_inc(c_back, 1)
                    dve.wait_ge(c_oc, c0 + T)
                    for t in range(T + 1):
                        if t < T:
                            dve.wait_ge(c_sh, c0 + t + 1)
                            V.tensor_tensor(sst[:, 1].rearrange("p (s d) -> p s d", d=RD), us[:, :, t],
                                            sst[:, 0].rearrange("p (s d) -> p s d", d=RD).bitcast(F32), ALU.subtract).then_inc(c_sl, 1)
                        if t >= 1:
                            u = t - 1
                            dve.wait_ge(c_x, c0 + u + 1)
                            bank = ps[:, 6 + u % 2]
                            V.scalar_tensor_tensor(oc[:, u], bank[:, 0:RD], dcur[:, 0:1], oc[:, u], ALU.mult, ALU.add).then_inc(c_xa, 1)
                            dve.wait_ge(c_xa, c0 + u + 1)
                            V.scalar_tensor_tensor(oc[:, u], bank[:, RD:2 * RD], dcur[:, 1:2], oc[:, u], ALU.mult, ALU.add).then_inc(c_xb, 1)
                            dve.wait_ge(c_xb, c0 + u + 1)
                            V.bn_stats(st6[:, u], oc[:, u]).then_inc(c_bn, 1)
                    dve.wait_ge(consts_in, NCONST)
                    dve.wait_ge(c_bn, c0 + T)
                    for u in range(T):
                        V.bn_aggr(mv[:, u], st6[:, u]).then_inc(c_mv, 1)
                    dve.wait_ge(c_mv, c0 + T)
                    nw = L * NW_L + h * 11 + 11 * (1 + KVH)
                    V.tensor_scalar(ss[:, 0:T], mv[:, :, 1], EPS, None, ALU.add).then_inc(newton, 1)
                    dve.wait_ge(newton, nw + 1)
                    rsqrt(ss[:, 0:T], T, nw + 1)
                    for t in range(T):
                        V.tensor_scalar(oc[:, t], oc[:, t], mv[:, t, 0:1], rs[:, t:t + 1], ALU.subtract, ALU.mult).then_inc(c_y, 1)
                    for t in range(T):
                        dve.wait_ge(c_y, c0 + t + 1)
                        if t >= 2:
                            dve.wait_ge(c_ytr, c0 + t - 1)
                        V.tensor_tensor(pm[:, t % 2], oc[:, t], g2[:, t], ALU.mult).then_inc(c_yg, 1)
                    for hf in range(2):
                        dve.wait_ge(consts_in, NCONST)
                        dve.wait_ge(c_uh, lh * 2 + hf + 1)
                        o = (slice(None), bass.ds(h, 1), slice(hf * 512, (hf + 1) * 512))
                        V.scalar_tensor_tensor(ur_lo[o], ps[:, 2 + hf:3 + hf], dcur[:, 6:7], ur_hi[o].bitcast(F32),
                                               ALU.mult, ALU.subtract).then_inc(c_ul, 1)
                    dve.drain().then_inc(phase_end, 1)

                wait_apart(dve, phase_end, 3 + L * PH_L + 3 * (1 + KVH + RH))
                with dve.Fori(0, 2) as b:
                    for i in range(4):
                        m = L * K + b * 4 + i
                        for n in range(2):
                            dve.wait_ge(d_tA, m * 2 + n + 2)
                            dve.wait_ge(d_ya, m * 2 + n + 1)
                            V.scalar_tensor_tensor(tA[:, n], tA[:, n], 1.0, ps[:, 4 * n + 2], ALU.add, ALU.mult).then_inc(d_mA, 1)
                        for n in range(2):
                            dve.wait_ge(d_tB, m * 2 + n + 2)
                            dve.wait_ge(d_yb, m * 2 + n + 1)
                            V.scalar_tensor_tensor(tB[:, n], tB[:, n], 1.0, ps[:, 4 * n + 3], ALU.add, ALU.mult).then_inc(d_mB, 1)
                            dve.wait_ge(consts_in, NCONST)
                            dve.wait_ge(d_mB, m * 2 + n + 2)
                            dve.wait_ge(d_mA, m * 2 + n + 2)
                            V.tensor_tensor(xm[:, bass.ds(b * 4 + i, 1), n * 512:(n + 1) * 512], tA[:, n:n + 1], tB[:, n:n + 1],
                                            ALU.add).then_inc(d_mg, 1)
                dve.drain().then_inc(phase_end, 1)

                dve.wait_ge(phase_end, 3 + L * PH_L + 3 * (2 + KVH + RH))
                for k in range(K):
                    dve.wait_ge(d_hi, L * K + k + 1)
                    V.tensor_tensor(hT_lo[:, k], xm[:, k], hT_hi[:, k].bitcast(F32), ALU.subtract).then_inc(d_lo, 1)
                dve.wait_ge(consts_in, NCONST)
                dve.wait_ge(x_back, L * 16 + 16)
                with dve.Fori(0, 2) as b:
                    for i in range(2):
                        for t in range(T):
                            dve.wait_ge(consts_in, NCONST)
                            dve.wait_ge(d_out, L * (4 * T) + b * (2 * T) + i * T + t + 1)
                            o = (slice(None), slice(t, t + 1), bass.ds(b * 512 + i * 256, 256))
                            V.scalar_tensor_tensor(xm[o], ps[:, t:t + 1, 0:256], 0.5, xm[o], ALU.mult, ALU.add).then_inc(d_res, 1)
                dve.drain().then_inc(phase_end, 1)

            dve.wait_ge(f_sq, T)
            dve.wait_ge(gain_in, DEPTH * 16 + 16)
            nw = DEPTH * NW_L
            V.tensor_scalar(ss[:, 0:T], ss[:, 0:T], 1.0 / DM, EPS, ALU.mult, ALU.add).then_inc(newton, 1)
            dve.wait_ge(newton, nw + 1)
            rsqrt(ss[:, 0:T], T, nw + 1)
            for t in range(T):
                if t >= 2:
                    dve.wait_ge(out_done[t % 2], 16 * (t // 2))
                V.scalar_tensor_tensor(hb[:, t % 2], xtile(t), rs[:, t:t + 1], gB[:], ALU.mult, ALU.mult).then_inc(f_y, 1)


def _rope(width):
    d_axis = width // 2
    q = width // 4
    inv = (THETA ** (-np.arange(0, d_axis, 2, dtype=np.float32) / np.float32(d_axis))).astype(np.float32)
    t = np.arange(SEQ)
    ang = np.stack([(t // GRID_W)[:, None].astype(np.float32) * inv, (t % GRID_W)[:, None].astype(np.float32) * inv], 1)
    c, s = np.cos(ang), np.sin(ang)
    full = np.stack([np.stack([c, c], 2), np.stack([-s, s], 2)], 0).reshape(2, T, P, 4 * q)
    return np.ascontiguousarray(full.transpose(2, 0, 1, 3)).astype(np.float32)


def _constants():
    i = np.arange(P, dtype=np.float32)
    diff = i[None, :] - i[:, None]
    dist = np.stack([np.maximum(diff, 0), np.maximum(-diff, 0)], 1)
    full = np.full(P, P, np.float32)
    idx = np.stack([i + 1, P - i, P - 1 - i, i, full, full], 1)
    return {"ident": np.eye(P, dtype=np.float32), "rope_a": _rope(HD), "rope_r": _rope(RD),
            "dist": np.ascontiguousarray(dist), "idx": np.ascontiguousarray(idx)}


def kernel(x, norm_g, w_in, attn_q_norm, attn_k_norm, ret_decay_fwd, ret_decay_bwd, ret_gn_w,
           w_branch_attn, w_branch_ret, w_out, final_norm_g):
    import concourse.bacc as bacc
    from concourse.bass_utils import run_bass_kernel_spmd

    a = lambda v, *s: np.ascontiguousarray(np.asarray(v).reshape(*s))
    arrays = {
        "x": a(x, SEQ, DM), "norm_g": a(norm_g, DEPTH, DM), "w_in": a(w_in, DEPTH * DM, D_IN),
        "qn": a(attn_q_norm, DEPTH, HD), "kn": a(attn_k_norm, DEPTH, HD),
        "dec_f": a(ret_decay_fwd, DEPTH, RH), "dec_b": a(ret_decay_bwd, DEPTH, RH),
        "gn_w": np.ascontiguousarray(np.asarray(ret_gn_w).reshape(DEPTH, RH, RD).transpose(2, 0, 1)),
        "w_a": a(w_branch_attn, DEPTH * AW, DM), "w_r": a(w_branch_ret, DEPTH * RW, DM),
        "w_o": a(w_out, DEPTH * DM, DM), "fin_g": a(final_norm_g, 1, DM), **_constants(),
    }
    nc = bacc.Bacc("TRN2", target_bir_lowering=False, num_devices=1, dynamic_dma_scratch_size=1024)
    aps = {n: nc.dram_tensor(n, v.shape, mybir.dt.from_np(v.dtype), kind="ExternalInput").ap() for n, v in arrays.items()}
    xs = nc.dram_tensor("xs", (SEQ, DM), F32, kind="Internal").ap()
    out = nc.dram_tensor("out", (SEQ, DM), F32, kind="ExternalOutput").ap()
    build(nc, xs=xs, out=out, **aps)
    r = run_bass_kernel_spmd(nc, [arrays], core_ids=[0])
    return r.results[0]["out"].reshape(np.asarray(x).shape)
```

```python
from contextlib import ExitStack

import numpy as np

import concourse.bass as bass
from concourse import mybir

F32 = mybir.dt.float32
F32R = mybir.dt.float32r
I32 = mybir.dt.int32
ALU = mybir.AluOpType
ACT = mybir.ActivationFunctionType
AXX = mybir.AxisListType.X

P = 128
DM = 1024
SEQ = 1024
DEPTH = 2
GRID_W = 64
QH, KVH, HD = 8, 2, 64
GRP = QH // KVH
RH, RD = 4, 128
AW, KVW, RW = QH * HD, KVH * HD, RH * RD
EPS = 1e-6
THETA = 10000.0
T = SEQ // P
K = DM // P
KA = AW // P
OFF = np.cumsum([0, AW, KVW, KVW, AW, RW, RW, RW, RW]).tolist()
C_QA, C_KA, C_VA, C_GA, C_QR, C_KR, C_VR, C_GR, C_GM = OFF
D_IN = C_GM + 2 * DM
QK_W = (GRP + 1) * HD
N_B, N_C, N_D1, N_D2 = 5, 4, 3, 2
U_C = KVH * N_B
U_D1 = U_C + RH * N_C
U_D2 = U_D1 + K * N_D1
U_L = U_D2 + 4 * N_D2
PH_L = 3 * (1 + KVH + 3)
G_BANK = (2, 3, 2, 6)
GATE_BANK = ((0, 1), (2, 5))
BRANCH_BANK = ((3, 4), (6, 7))
MAGIC = 1597463007.0


def build(nc, x, norm_g, w_in, qn, kn, dec_f, dec_b, gn_w, w_a, w_r, w_o, fin_g,
          ident, rope_a, rope_r, dist, idx, xs, out):
    with ExitStack() as ctx:
        def sem(name):
            return ctx.enter_context(nc.semaphore(name))

        def sb(c, name, shape, dt=F32):
            return c.enter_context(nc.sbuf_tensor(name, [P] + shape, dt))

        ps = ctx.enter_context(nc.psum_tensor("ps", [P, 8, 512], F32))
        hT_hi = sb(ctx, "hT_hi", [K, SEQ], F32R)
        hT_lo = sb(ctx, "hT_lo", [K, SEQ], F32R)
        w_hi = sb(ctx, "w_hi", [K, 4 * P], F32R)
        w_lo = sb(ctx, "w_lo", [K, 4 * P], F32R)
        raw = sb(ctx, "raw", [2, K, P])
        idf = sb(ctx, "idf", [P])
        idr = sb(ctx, "idr", [P], F32R)
        dst = sb(ctx, "dst", [2, P])
        dec = sb(ctx, "dec", [DEPTH * RH, 8])
        dcur = sb(ctx, "dcur", [8])
        icol = sb(ctx, "icol", [6])
        lgw = sb(ctx, "lgw", [6, 2 * DEPTH * RH])
        msk = sb(ctx, "msk", [P])
        gwh = sb(ctx, "gwh", [1])
        gwc = sb(ctx, "gwc", [RH])
        ss = sb(ctx, "ss", [T * (GRP + 1)])
        rs = sb(ctx, "rs", [T * (GRP + 1)])
        nt = sb(ctx, "nt", [T * (GRP + 1)])
        st6 = sb(ctx, "st6", [T, 6])
        mv = sb(ctx, "mv", [T, 2])
        nmx = sb(ctx, "nmx", [4])
        rsm = sb(ctx, "rsm", [4])
        rrc = sb(ctx, "rrc", [4])
        ua_hi = sb(ctx, "ua_hi", [KA, SEQ], F32R)
        ua_lo = sb(ctx, "ua_lo", [KA, SEQ], F32R)
        with ExitStack() as pb:
            gT = sb(pb, "gT", [2, SEQ])
            q_st = sb(pb, "q_st", [GRP, SEQ], F32R)
            k_st = sb(pb, "k_st", [2, SEQ], F32R)
            v_st = sb(pb, "v_st", [T, 2 * HD], F32R)
            av = sb(pb, "av", [2, 256])
            with ExitStack() as p1:
                zqk = sb(p1, "zqk", [T, QK_W])
                ctA = sb(p1, "ctA", [2, T, HD])
                gqk = sb(p1, "gqk", [QK_W])
                sq = sb(p1, "sq", [2, QK_W])
                rta = sb(p1, "rta", [2, QK_W])
                rtb = sb(p1, "rtb", [2, QK_W])
                qs = sb(p1, "qs", [2, GRP + 2, P], F32R)
                thA = sb(p1, "thA", [2, 512])
            with ExitStack() as p2:
                pp = sb(p2, "pp", [3, SEQ])
                pT_hi = sb(p2, "pT_hi", [2, T, 256], F32R)
                pT_lo = sb(p2, "pT_lo", [2, T, 256], F32R)
        ur_hi = sb(ctx, "ur_hi", [KA, SEQ], F32R)
        ur_lo = sb(ctx, "ur_lo", [KA, SEQ], F32R)
        with ExitStack() as pc:
            us = sb(pc, "us", [T, 2, RD])
            oc = sb(pc, "oc", [T, RD])
            g2 = sb(pc, "g2", [T, RD])
            ctR = sb(pc, "ctR", [2, T, RD])
            ra = sb(pc, "ra", [T, 2 * RD])
            rb = sb(pc, "rb", [2, 2 * RD])
            qkT = sb(pc, "qkT", [T, 2 * P])
            pm = sb(pc, "pm", [2, P])
            vv = sb(pc, "vv", [2, RD])
            vd = sb(pc, "vd", [2, 2 * RD])
        xm = sb(ctx, "xm", [T, DM])
        with ExitStack() as pa:
            hb = sb(pa, "hb", [2, DM])
            gB = sb(pa, "gB", [DM])
            junk = sb(pa, "junk", [DM])
        with ExitStack() as pd:
            tA = sb(pd, "tA", [2, 512])
            tB = sb(pd, "tB", [2, 512])

        consts_in, x_saved = map(sem, ("consts_in", "x_saved"))
        x_back = [sem("x_back0"), sem("x_back1")]
        out_done = [sem("out_done0"), sem("out_done1")]
        raw_in = [sem("raw_in0"), sem("raw_in1")]
        w_rounded, w_ready, phase_end = map(sem, ("w_rounded", "w_ready", "phase_end"))
        pro_dve, pro_act, newton = map(sem, ("pro_dve", "pro_act", "newton"))
        gain_in, a_sq, h_ready, h_tr, h_hi, h_lo = map(sem, ("gain_in", "a_sq", "h_ready", "h_tr", "h_hi", "h_lo"))
        b_tab, b_gain, b_proj, b_z, b_sq, b_vh, b_ssum, b_free = map(sem, (
            "b_tab", "b_gain", "b_proj", "b_z", "b_sq", "b_vh", "b_ssum", "b_free"))
        b_gate, b_tanh, b_gated, b_norm, b_cos, b_sin, b_rot, b_hi, b_lo, b_tr, b_qT, b_kT = map(sem, (
            "b_gate", "b_tanh", "b_gated", "b_norm", "b_cos", "b_sin", "b_rot", "b_hi", "b_lo", "b_tr", "b_qT", "b_kT"))
        s_done, s_max, s_exp, s_rcp, p_norm, p_tr, p_hi, p_lo = map(sem, (
            "s_done", "s_max", "s_exp", "s_rcp", "p_norm", "p_tr", "p_hi", "p_lo"))
        pv_done, av_lo, av_sum, av_gated, ua_h, ua_l = map(sem, ("pv_done", "av_lo", "av_sum", "av_gated", "ua_h", "ua_l"))
        c_tab, c_dec, c_arg, c_mexp, c_gw, c_zero = map(sem, ("c_tab", "c_dec", "c_arg", "c_mexp", "c_gw", "c_zero"))
        c_qkp, c_rot, c_o, c_tr, c_T = map(sem, ("c_qkp", "c_rot", "c_o", "c_tr", "c_T"))
        c_vgp, c_v, c_th, c_g, c_qk, c_pm, c_u, c_uf, c_ub, c_pv, c_oc = map(sem, (
            "c_vgp", "c_v", "c_th", "c_g", "c_qk", "c_pm", "c_u", "c_uf", "c_ub", "c_pv", "c_oc"))
        c_back, c_x, c_xa, c_xb, c_bn, c_mv, c_y, c_yg, c_ytr, c_uh, c_ul = map(sem, (
            "c_back", "c_x", "c_xa", "c_xb", "c_bn", "c_mv", "c_y", "c_yg", "c_ytr", "c_uh", "c_ul"))
        d_gA, d_gB, d_ya, d_yb, d_tA, d_tB, d_mA, d_mB, d_mg = map(sem, (
            "d_gA", "d_gB", "d_ya", "d_yb", "d_tA", "d_tB", "d_mA", "d_mB", "d_mg"))
        d_hi, d_lo, d_out, d_res = map(sem, ("d_hi", "d_lo", "d_out", "d_res"))
        f_sq, f_y = map(sem, ("f_sq", "f_y"))
        NCONST = 16 * 9

        held = {}

        def wait_apart(eng, sem_, value):
            eng.reg_add(held[eng], value, 0)
            eng.wait_ge(consts_in, NCONST)
            eng.wait_ge(sem_, held[eng])

        block = ctx.enter_context(nc.Block())

        def tanh_gate(g):
            return pp[:, 2, 0:512] if g == 3 else thA[:, g % 2]

        def xtile(t):
            return xm[:, t, :]

        @block.sync
        def _(sp):
            def unit(slot, wait_for, parts):
                sp.wait_ge(w_ready, 1 + wait_for)
                for dst_ap, src in parts:
                    sp.dma_start(dst_ap, src).then_inc(raw_in[slot], 16)

            def cols(slot, L, c0, half_rows=K // 2):
                src = w_in[bass.ds(L * DM, DM), bass.ds(c0, P)].rearrange("(k p) c -> p k c", p=P)
                return [(raw[:, slot, a:a + half_rows], src[:, a:a + half_rows]) for a in (0, half_rows)]

            with sp.Fori(0, DEPTH) as L:
                u0 = L * U_L
                with sp.Fori(0, KVH) as j:
                    n0 = u0 + j * N_B
                    for i in range(N_B):
                        before = n0 + (i - 1 if i > 1 else 0)
                        if i in (0, 1):
                            parts = cols(i % 2, L, C_QA + j * (GRP * HD) + i * P)
                        elif i == 2:
                            parts = [(raw[:, 0, :, s * HD:(s + 1) * HD],
                                      w_in[bass.ds(L * DM, DM), bass.ds(c0 + j * HD, HD)].rearrange("(k p) c -> p k c", p=P))
                                     for s, c0 in ((0, C_KA), (1, C_VA))]
                        else:
                            parts = cols(i % 2, L, C_GA + j * (GRP * HD) + (i - 3) * P)
                        unit(i % 2, before, parts)
                with sp.Fori(0, RH) as h:
                    n0 = u0 + U_C + h * N_C
                    for i, c0 in enumerate((C_QR, C_KR, C_VR, C_GR)):
                        unit(i % 2, n0 + (i - 1 if i else 0), cols(i % 2, L, c0 + h * RD))
                with sp.Fori(0, K // 2) as mm:
                    n0 = u0 + U_D1 + mm * (2 * N_D1)
                    for i in range(2 * N_D1):
                        m = mm * 2 + i // N_D1
                        slot = i % 2
                        if i % N_D1 < 2:
                            parts = cols(slot, L, C_GM + (i % N_D1) * DM + m * P)
                        else:
                            parts = [(raw[:, slot, a:a + KA], w[bass.ds(L * AW, AW), bass.ds(m * P, P)].rearrange("(k p) c -> p k c", p=P))
                                     for a, w in ((0, w_a), (KA, w_r))]
                        unit(slot, n0 + i - 1, parts)
                with sp.Fori(0, 4) as nn:
                    n0 = u0 + U_D2 + nn * N_D2
                    for i in range(N_D2):
                        src = w_o[bass.ds(L * DM, DM), bass.ds(nn * (2 * P) + i * P, P)].rearrange("(k p) c -> p k c", p=P)
                        unit(i, n0 + i - 1, [(raw[:, i, a:a + K // 2], src[:, a:a + K // 2]) for a in (0, K // 2)])

        @block.gpsimd
        def _(pool):
            held[pool] = pool.alloc_register("held_pool")
            def place(pos):
                return w_hi[:, :, pos * P:(pos + 1) * P], w_lo[:, :, pos * P:(pos + 1) * P]

            def fill_hi(slot, pos, n_slot):
                wait_apart(pool, raw_in[slot], n_slot * 32 + 32)
                nc.gpsimd.tensor_scalar(place(pos)[0], raw[:, slot], 1.0, 1.0, ALU.mult, ALU.mult).then_inc(w_rounded, 1)

            def fill_lo(slot, pos, n):
                hi, lo = place(pos)
                pool.wait_ge(w_rounded, n + 1)
                nc.gpsimd.tensor_tensor(lo, raw[:, slot], hi.bitcast(F32), ALU.subtract).then_inc(w_ready, 1)

            def fill(slot, pos, n_slot, n):
                fill_hi(slot, pos, n_slot)
                fill_lo(slot, pos, n)

            pool.sem_inc(w_ready, 1)
            PER = (3 * KVH + (U_L - U_C) // 2, 2 * KVH + (U_L - U_C) // 2)
            with pool.Fori(0, DEPTH) as L:
                n0 = L * U_L
                pool.wait_ge(phase_end, 3 + L * PH_L)
                for i in range(4):
                    fill(i % 2, i, L * PER[i % 2] + i // 2, n0 + i)
                with pool.Fori(0, KVH) as j:
                    for t in range(T):
                        bt = L * (KVH * T) + j * T + t
                        pool.wait_ge(b_norm, bt * 2 + 2)
                        if t >= 2:
                            pool.wait_ge(b_lo, bt * 2 - 2)
                        nc.gpsimd.tensor_tensor(rta[:, t % 2].rearrange("p (h d) -> p h d", d=HD),
                                                zqk[:, t].rearrange("p (h d) -> p h d", d=HD),
                                                ctA[:, 0, t:t + 1].to_broadcast([P, GRP + 1, HD]), ALU.mult).then_inc(b_cos, 1)
                        pool.wait_ge(b_cos, bt + 1)
                        pool.wait_ge(b_sin, bt * 2 + 2)
                        nc.gpsimd.tensor_tensor(rta[:, t % 2], rta[:, t % 2], rtb[:, t % 2], ALU.add).then_inc(b_rot, 1)
                        if t == 3:
                            pool.wait_ge(b_proj, L * (KVH * T) + j * T + T)
                            fill(0, 0, L * PER[0] + j * 3 + 2, n0 + j * N_B + 4)
                    a0 = L * (KVH * 4 * T) + j * (4 * T)
                    i0 = L * (KVH * 2 * T) + j * (2 * T)

                    def divide(tile):
                        wait_apart(pool, s_rcp, a0 + tile + 1)
                        nc.gpsimd.tensor_scalar(pp[:, tile % 3], pp[:, tile % 3], rrc[:, tile % 4:tile % 4 + 1], 1.0,
                                                ALU.mult, ALU.mult).then_inc(p_norm, 1)

                    for i in range(2 * T + 3):
                        if i >= 3:
                            pool.wait_ge(consts_in, NCONST)
                            pool.wait_ge(av_gated, i0 + min(i - 2, 2 * T))
                        if 2 <= i < 10:
                            u = i // 2 - 1
                            if i == 2:
                                pool.wait_ge(b_gate, L * (KVH * 4) + j * 4 + 4)
                            if i % 2 == 0:
                                fill_hi(u % 2, u, L * PER[u % 2] + j * (3, 2)[u % 2] + (3, 2)[u % 2] + u // 2)
                            else:
                                fill_lo(u % 2, u, n0 + j * N_B + N_B + u)
                        if i < 2 * T:
                            divide(2 * i)
                        if i >= 3:
                            e = i - 3
                            hh, qp = e // 4, e % 4
                            pr = HD * (hh % 2)
                            pool.wait_ge(consts_in, NCONST)
                            pool.wait_ge(ua_h, i0 + e + 1)
                            if i < 2 * T:
                                pool.wait_ge(p_norm, a0 + 2 * i + 1)
                            else:
                                pool.wait_ge(av_gated, i0 + min(i - 2, 2 * T))
                            o = (slice(pr, pr + HD), bass.ds(j * 2 + hh // 2, 1), slice(qp * 256, (qp + 1) * 256))
                            nc.gpsimd.tensor_tensor(ua_lo[o], av[pr:pr + HD, e % 2:e % 2 + 1], ua_hi[o].bitcast(F32),
                                                    ALU.subtract).then_inc(ua_l, 1)
                            pool.wait_ge(consts_in, NCONST)
                            pool.wait_ge(ua_l, i0 + e + 1)
                        if i < 2 * T:
                            divide(2 * i + 1)
                        if 2 <= i < 2 * T + 2:
                            e = i - 2
                            hh, qp = e // 4, e % 4
                            pr = HD * (hh % 2)
                            pool.wait_ge(av_sum, i0 + e + 1)
                            if i < 2 * T:
                                pool.wait_ge(p_norm, a0 + 2 * i + 2)
                            nc.gpsimd.tensor_tensor(av[pr:pr + HD, e % 2], av[pr:pr + HD, e % 2],
                                                    gT[pr:pr + HD, hh // 2, qp * 256:(qp + 1) * 256], ALU.mult).then_inc(av_gated, 1)
                def rotate(h, fills):
                    c0 = L * (RH * T) + h * T
                    for t in range(T):
                        pool.wait_ge(c_rot, c0 * 3 + 3 * t + 3)
                        nc.gpsimd.tensor_tensor(ra[:, t], ra[:, t], rb[:, t % 2], ALU.add).then_inc(c_o, 1)
                        if fills is not None and t < 4:
                            if t == 0:
                                pool.wait_ge(c_vgp, c0)
                            i = 2 + t // 2
                            if t % 2 == 0:
                                fill_hi(i % 2, i, L * PER[i % 2] + (3, 2)[i % 2] * KVH + fills * 2 + 2 + i // 2)
                            else:
                                fill_lo(i % 2, i, n0 + U_C + fills * N_C + N_C + i)

                def fill_qk(h):
                    pool.wait_ge(c_qkp, L * (RH * T) + h * T + T)
                    for i in range(2):
                        fill(i, i, L * PER[i] + (3, 2)[i] * KVH + h * 2 + 2, n0 + U_C + h * N_C + N_C + i)

                rotate(0, None)
                with pool.Fori(0, RH - 1) as h:
                    fill_qk(h)
                    rotate(h + 1, h)
                fill_qk(RH - 1)
                pool.wait_ge(c_vgp, L * (RH * T) + RH * T)

                def fill_d1(m, kind, pos, u, b):
                    if u > 2:
                        pool.wait_ge((d_gA, d_gB, d_yb)[kind], L * (2 * K) + m * 2)
                    fill(u % 2, pos, L * PER[u % 2] + (3, 2)[u % 2] * KVH + 2 * RH + b * 3 + u // 2, n0 + U_D1 + b * 6 + u)

                fill_d1(0, 2, 2, 2, 0)
                with pool.Fori(0, K // 2 - 1) as b:
                    for i in (1, 2):
                        for kind in range(3):
                            fill_d1(2 * b + i, kind, (0, 1, 2 + i % 2)[kind], 3 * i + kind, b)
                for kind in range(3):
                    fill_d1(K - 1, kind, (0, 1, 3)[kind], 3 + kind, K // 2 - 1)
                for i in range(4):
                    pool.wait_ge((d_gA, d_gB, d_yb, d_yb)[i], L * (2 * K) + 2 * K - (2 if i == 2 else 0))
                    fill(i % 2, i, L * PER[i % 2] + (3, 2)[i % 2] * KVH + 2 * RH + K * N_D1 // 2 + i // 2, n0 + U_D2 + i)
                for i in range(4):
                    pool.wait_ge(d_out, L * (4 * T) + (i // 2 + 1) * T)
                    fill(i % 2, i, L * PER[i % 2] + (3, 2)[i % 2] * KVH + 2 * RH + K * N_D1 // 2 + 2 + i // 2,
                         n0 + U_D2 + 4 + i)

        @block.tensor
        def _(pe):
            held[pe] = pe.alloc_register("held_pe")
            def prod3(outp, pairs, start=True, stop=True):
                for i, ((ah, al), (bh, bl)) in enumerate(pairs):
                    nc.tensor.matmul(outp, ah, bh, start=(start and i == 0), stop=False)
                    nc.tensor.matmul(outp, ah, bl, start=False, stop=False)
                    last = nc.tensor.matmul(outp, al, bh, start=False, stop=(stop and i == len(pairs) - 1))
                return last

            def h_l(k, t):
                return hT_hi[:, k, t * P:(t + 1) * P], hT_lo[:, k, t * P:(t + 1) * P]

            def h_r(k, n):
                return hT_hi[:, k, n * 512:(n + 1) * 512], hT_lo[:, k, n * 512:(n + 1) * 512]

            def w_u(k, a, b):
                return w_hi[:, k, a:b], w_lo[:, k, a:b]

            pe.wait_ge(consts_in, NCONST)
            pe.wait_ge(pro_act, 1)
            pe.drain().then_inc(phase_end, 1)
            with pe.Fori(0, DEPTH) as L:
                for t in range(T):
                    pe.wait_ge(h_ready, L * T + t + 1)
                    if t >= 2:
                        pe.wait_ge(h_lo, L * (2 * T) + 2 * t - 2)
                    for k in range(K):
                        last = nc.tensor.transpose(ps[:, 2 * (t % 2) + k // 4, (k % 4) * P:(k % 4 + 1) * P],
                                                   hb[:, t % 2, k * P:(k + 1) * P], idf[:])
                    last.then_inc(h_tr, 1)
                pe.drain().then_inc(phase_end, 1)

                with pe.Fori(0, KVH) as j:
                    pe.wait_ge(h_lo, L * (2 * T) + 2 * T)
                    pe.wait_ge(w_ready, 1 + L * U_L + j * N_B + 3)

                    def project(t):
                        if t >= 2:
                            pe.wait_ge(b_free, L * (KVH * T) + j * T + t - 1)
                        prod3(ps[:, t % 2, 0:3 * P], [(h_l(k, t), w_u(k, 0, 3 * P)) for k in range(K)]).then_inc(b_proj, 1)

                    def gate(g, part):
                        mt, n = g // 2, g % 2
                        pos = (3, 0)[mt]
                        if part == 0:
                            if n == 0:
                                pe.wait_ge(w_ready, 1 + L * U_L + j * N_B + 4 + mt)
                            if g == 2:
                                pe.wait_ge(b_gated, L * (KVH * 4) + j * 4 + 1)
                            elif g == 3:
                                pe.wait_ge(b_qT, L * (KVH * T) + j * T + T)
                        last = prod3(ps[:, G_BANK[g], :],
                                     [(w_u(k, pos * P, (pos + 1) * P), h_r(k, n)) for k in range(4 * part, 4 * part + 4)],
                                     start=(part == 0), stop=(part == 1))
                        if part == 1:
                            last.then_inc(b_gate, 1)

                    def turn(t):
                        bt = L * (KVH * T) + j * T + t
                        pe.wait_ge(b_lo, bt * 2 + 2)
                        pe.wait_ge(b_hi, bt * 2 + 2)
                        if t >= 2:
                            pe.wait_ge(b_kT, bt - 1)
                            pe.wait_ge(b_qT, bt - 1)
                        for c in range(GRP + 2):
                            bank = 4 + 2 * (t % 2) + c // GRP
                            last = nc.tensor.transpose(ps[:, bank, (c % GRP) * P:(c % GRP + 1) * P].bitcast(F32R),
                                                       qs[:, t % 2, c], idr[:])
                        last.then_inc(b_tr, 1)

                    for t in range(T):
                        project(t)
                        if t >= 5:
                            turn(t - 5)
                    for i in range(5):
                        gate(i // 2, i % 2)
                        turn(i + 3)
                    gate(2, 1)
                    b2 = L * (KVH * T) + j * T
                    a0 = L * (KVH * 4 * T) + j * (4 * T)

                    def scores(tile):
                        hh, t = tile // T, tile % T
                        if tile >= 2:
                            pe.wait_ge(s_exp, a0 + tile - 1)
                        for c in range(2):
                            for n in range(2):
                                last = nc.tensor.matmul(ps[:, 2 * (tile % 2) + n, :], q_st[:, hh, t * P:(t + 1) * P],
                                                        k_st[:, c, n * 512:(n + 1) * 512], start=(c == 0), stop=(c == 1))
                        last.then_inc(s_done, 1)

                    def turn_probs(tile):
                        pe.wait_ge(p_norm, a0 + tile + 1)
                        for half in range(2):
                            g = 2 * tile + half
                            if g >= 2:
                                pe.wait_ge(p_lo, a0 * 2 + g - 1)
                            for kb in range(4):
                                last = nc.tensor.transpose(ps[:, 4 + g % 2, kb * P:(kb + 1) * P],
                                                           pp[:, tile % 3, (4 * half + kb) * P:(4 * half + kb + 1) * P], idf[:])
                            last.then_inc(p_tr, 1)

                    def values(e):
                        it = L * (KVH * 2 * T) + j * (2 * T) + e
                        pe.wait_ge(p_lo, a0 * 2 + 4 * e + 4)
                        if e >= 2:
                            pe.wait_ge(av_sum, it - 1)
                        elif e == 0:
                            pe.wait_ge(b_gated, L * (KVH * 4) + j * 4 + 4)
                        for kb in range(T):
                            nc.tensor.matmul(ps[:, 6 + e % 2, 0:256], v_st[:, kb], pT_hi[:, e % 2, kb],
                                             start=(kb == 0), stop=False)
                            last = nc.tensor.matmul(ps[:, 6 + e % 2, 0:256], v_st[:, kb], pT_lo[:, e % 2, kb],
                                                    start=False, stop=(kb == T - 1))
                        last.then_inc(pv_done, 1)

                    pe.wait_ge(b_qT, b2 + T)
                    pe.wait_ge(b_kT, b2 + T)
                    pe.wait_ge(b_free, b2 + T)
                    scores(0)
                    gate(3, 0)
                    pe.wait_ge(b_gated, L * (KVH * 4) + j * 4 + 3)
                    scores(1)
                    gate(3, 1)
                    for i in range(2 * T + 1):
                        if i >= 1:
                            turn_probs(2 * i - 1)
                        if i + 1 < 2 * T:
                            scores(2 * i + 2)
                        if i < 2 * T:
                            turn_probs(2 * i)
                        if i + 1 < 2 * T:
                            scores(2 * i + 3)
                        if i >= 1:
                            values(i - 1)
                    pe.drain().then_inc(phase_end, 1)

                def project_qk(h, t, done):
                    c0 = L * (RH * T) + h * T
                    if t == 0:
                        pe.wait_ge(w_ready, 1 + L * U_L + h * N_C + U_C + 2)
                    if t >= 2:
                        pe.wait_ge(c_rot, c0 * 3 + 3 * t - 3)
                    elif done is not None:
                        pe.wait_ge(c_g, c0 + t - 1)
                    prod3(ps[:, t % 2, 0:256], [(h_l(k, t), w_u(k, 0, 256)) for k in range(K)]).then_inc(c_qkp, 1)

                def project_vg(h, t):
                    c0 = L * (RH * T) + h * T
                    if t == 0:
                        pe.wait_ge(w_ready, 1 + L * U_L + h * N_C + U_C + N_C)
                    if t >= 2:
                        pe.wait_ge(c_g, c0 + t - 1)
                    else:
                        pe.wait_ge(c_rot, c0 * 3 + 3 * (T - 1 + t))
                    prod3(ps[:, t % 2, 0:256], [(h_l(k, t), w_u(k, 256, 512)) for k in range(K)]).then_inc(c_vgp, 1)

                def turn(h, t):
                    c0 = L * (RH * T) + h * T
                    pe.wait_ge(c_o, c0 + t + 1)
                    if t >= 1:
                        pe.wait_ge(c_T, c0 + t)
                    nc.tensor.transpose(ps[:, 5, 0:P], ra[:, t, 0:RD], idf[:])
                    nc.tensor.transpose(ps[:, 5, P:2 * P], ra[:, t, RD:2 * RD], idf[:]).then_inc(c_tr, 1)

                def chunk_scores(h, t):
                    c0 = L * (RH * T) + h * T
                    pe.wait_ge(c_T, c0 + t + 1)
                    if t >= 1:
                        pe.wait_ge(c_pm, c0 + t)
                    nc.tensor.matmul(ps[:, 2, 0:P], qkT[:, t, P:2 * P], qkT[:, t, 0:P], start=True, stop=True).then_inc(c_qk, 1)

                def update(h, t):
                    c0 = L * (RH * T) + h * T
                    f0 = L * (RH * (T - 1)) + h * (T - 1)
                    pe.wait_ge(c_v, c0 * 3 + 3 * t + 3)
                    if t >= 1:
                        pe.wait_ge(c_uf, f0 + t)
                    if t >= 2:
                        pe.wait_ge(c_ub, f0 + t - 1)
                    nc.tensor.matmul(ps[:, 3, 0:2 * RD], ra[:, t, RD:2 * RD], vd[:, t % 2], start=True, stop=True).then_inc(c_u, 1)
                    pe.wait_ge(c_pm, c0 + t + 1)
                    if t >= 1:
                        pe.wait_ge(c_oc, c0 + t)
                    nc.tensor.matmul(ps[:, 4, 0:RD], pm[:, t % 2], vv[:, t % 2], start=True, stop=True).then_inc(c_pv, 1)

                def cross(h, e):
                    x0 = L * (RH * 4) + h * 4
                    if e == 0:
                        pe.wait_ge(c_back, L * (RH * 6) + h * 6 + 6)
                        pe.wait_ge(c_zero, L * 2 + 2)
                    else:
                        pe.wait_ge(c_xb, x0 + e)
                    for i in range(2):
                        t = 2 * e + i
                        last = nc.tensor.matmul(ps[:, 6, i * 256:(i + 1) * 256], qkT[:, t, 0:P], us[:, t].rearrange("p s d -> p (s d)"),
                                                start=True, stop=True)
                    last.then_inc(c_x, 1)

                def turn_out(h, half):
                    pe.wait_ge(c_yg, L * (RH * 2) + h * 2 + half + 1)
                    for i in range(4):
                        last = nc.tensor.transpose(ps[:, 7 - half, i * P:(i + 1) * P], oc[:, 4 * half + i], idf[:])
                    last.then_inc(c_ytr, 1)

                def first_pass(h, done):
                    for t in range(T):
                        project_qk(h, t, done)
                        if done is not None and t == 0:
                            update(done, T - 1)
                        if t >= 2:
                            turn(h, t - 2)
                        if done is not None and 1 <= t <= 4:
                            cross(done, t - 1)
                    chunk_scores(h, 0)
                    project_vg(h, 0)
                    if done is not None:
                        turn_out(done, 0)
                        turn_out(done, 1)

                def second_pass(h):
                    for t in range(T):
                        if t >= 1:
                            chunk_scores(h, t)
                            project_vg(h, t)
                        if t < 2:
                            turn(h, T - 2 + t)
                        if t >= 1:
                            update(h, t - 1)

                first_pass(0, None)
                with pe.Fori(0, RH - 1) as h:
                    second_pass(h)
                    first_pass(h + 1, h)
                second_pass(RH - 1)

                def gate_part(m, kind, n, part):
                    if part == 0:
                        if n == 0:
                            pe.wait_ge(w_ready, 1 + L * U_L + m * N_D1 + U_D1 + kind + 1)
                        if type(m) is not int or m > 0:
                            pe.wait_ge((d_tA, d_tB)[kind], L * (2 * K) + m * 2 + n)
                    last = prod3(ps[:, GATE_BANK[kind][n], :],
                                 [(w_u(k, kind * P, (kind + 1) * P), h_r(k, n)) for k in range(4 * part, 4 * part + 4)],
                                 start=(part == 0), stop=(part == 1))
                    if part == 1:
                        last.then_inc((d_gA, d_gB)[kind], 1)

                update(RH - 1, T - 1)
                pe.wait_ge(c_g, L * (RH * T) + RH * T)
                parts = [(kind, n, part) for kind in range(2) for n in range(2) for part in range(2)]
                for i, (kind, n, part) in enumerate(parts):
                    gate_part(0, kind, n, part)
                    if 1 <= i <= 4:
                        cross(RH - 1, i - 1)
                turn_out(RH - 1, 0)
                turn_out(RH - 1, 1)
                pe.drain().then_inc(phase_end, 1)

                def gates(m):
                    for kind in range(2):
                        for n in range(2):
                            for part in range(2):
                                gate_part(m, kind, n, part)

                def branches(m, pos):
                    pe.wait_ge(w_ready, 1 + L * U_L + m * N_D1 + U_D1 + 3)
                    for br, (uh, ul) in enumerate(((ua_hi, ua_lo), (ur_hi, ur_lo))):
                        for n in range(2):
                            pe.wait_ge((d_mA, d_mB)[br], L * (2 * K) + m * 2 + 1)
                            prod3(ps[:, BRANCH_BANK[br][n], :],
                                  [(w_u(br * KA + k, pos * P, (pos + 1) * P),
                                    (uh[:, k, n * 512:(n + 1) * 512], ul[:, k, n * 512:(n + 1) * 512])) for k in range(KA)]
                                  ).then_inc((d_ya, d_yb)[br], 1)

                wait_apart(pe, c_ul, L * (RH * 2) + RH * 2)
                with pe.Fori(0, K // 2 - 1) as b:
                    branches(2 * b, 2)
                    gates(2 * b + 1)
                    branches(2 * b + 1, 3)
                    gates(2 * b + 2)
                branches(K - 2, 2)
                gates(K - 1)
                branches(K - 1, 3)
                pe.drain().then_inc(phase_end, 1)

                with pe.Fori(0, 2) as b:
                    for i in range(2):
                        pe.wait_ge(w_ready, 1 + L * U_L + b * 4 + U_D2 + 2 * i + 2)
                        for t in range(T):
                            o = L * (4 * T) + b * (2 * T) + i * T + t
                            pe.wait_ge(d_res, o + 1)
                            if i == 0:
                                pe.wait_ge(d_lo, L * T + t + 1)
                            prod3(ps[:, t, 0:256], [(h_l(k, t), w_u(k, 256 * i, 256 * (i + 1))) for k in range(K)]).then_inc(d_out, 1)
                pe.drain().then_inc(phase_end, 1)

        @block.scalar
        def _(act):
            for d, s in ((idf[:], ident), (dst[:], dist), (icol[:], idx)):
                act.dma_start(d, s).then_inc(consts_in, 16)
            for i, src in enumerate((dec_f, dec_b)):
                for L in range(DEPTH):
                    act.dma_start(lgw[:, 0, (i * DEPTH + L) * RH:(i * DEPTH + L + 1) * RH],
                                  src[L:L + 1, :].to_broadcast([P, RH])).then_inc(consts_in, 16)
            for a in (0, 1):
                act.dma_start(xm[:, a * 4:a * 4 + 4], x.rearrange("(t p) d -> p t d", p=P)[:, a * 4:a * 4 + 4]).then_inc(consts_in, 16)
            act.wait_ge(consts_in, NCONST)
            nc.scalar.copy(idr[:], idf[:]).then_inc(pro_act, 1)
            act.wait_ge(pro_dve, 2)
            nc.scalar.activation(lgw[:, 2], lgw[:, 1], ACT.Exp).then_inc(pro_act, 1)
            act.wait_ge(pro_dve, 22)
            nc.scalar.activation(dec[:, :, 0:6], dec[:, :, 0:6], ACT.Exp).then_inc(pro_act, 1)
            for s in (d_tA, d_tB):
                act.sem_inc(s, 1)
            act.drain().then_inc(phase_end, 1)

            with act.Fori(0, DEPTH) as L:
                act.wait_ge(phase_end, 3 + L * PH_L)
                act.dma_start(gB[:], norm_g[bass.ds(L, 1), :].to_broadcast([P, DM])).then_inc(gain_in, 16)
                act.dma_start(xs.rearrange("(t p) d -> p t d", p=P), xm[:]).then_inc(x_saved, 16)
                for t in range(T):
                    if t:
                        act.wait_ge(a_sq, L * T + t)
                    nc.scalar.activation(junk[:], xtile(t), ACT.Square, accum_out=ss[:, t:t + 1]).then_inc(a_sq, 1)
                for t in range(T):
                    if t == T - 1:
                        act.wait_ge(x_saved, L * 16 + 16)
                    act.wait_ge(h_tr, L * T + t + 1)
                    for half in range(2):
                        nc.scalar.copy(hT_hi[:, 4 * half:4 * half + 4, t * P:(t + 1) * P],
                                       ps[:, 2 * (t % 2) + half].rearrange("p (k c) -> p k c", c=P)).then_inc(h_hi, 1)
                act.drain().then_inc(phase_end, 1)

                with act.Fori(0, KVH) as j:
                    act.wait_ge(phase_end, 3 + L * PH_L + j * 3 + 3)
                    for c in range(2):
                        act.dma_start(ctA[:, c], rope_a[:, c]).then_inc(b_tab, 16)
                    for hh in range(GRP):
                        act.dma_start(gqk[:, hh * HD:(hh + 1) * HD], qn[bass.ds(L, 1), :].to_broadcast([P, HD])).then_inc(b_tab, 16)
                    act.dma_start(gqk[:, GRP * HD:], kn[bass.ds(L, 1), :].to_broadcast([P, HD])).then_inc(b_tab, 16)
                    b0 = L * (KVH * T) + j * T

                    def outputs(t):
                        act.wait_ge(b_proj, b0 + t + 1)
                        if t >= 2:
                            act.wait_ge(b_ssum, b0 + t - 1)
                        nc.scalar.activation(sq[:, t % 2], ps[:, t % 2, 0:QK_W], ACT.Square).then_inc(b_sq, 1)
                        nc.scalar.copy(v_st[:, t, 0:HD], ps[:, t % 2, QK_W:QK_W + HD]).then_inc(b_vh, 1)

                    def gate(g):
                        act.wait_ge(b_gate, L * (KVH * 4) + j * 4 + g + 1)
                        if g >= 2:
                            act.wait_ge(b_gated, L * (KVH * 4) + j * 4 + g - 1)
                        nc.scalar.activation(tanh_gate(g), ps[:, G_BANK[g]], ACT.Tanh, scale=0.5).then_inc(b_tanh, 1)

                    def hi_parts(t):
                        act.wait_ge(b_rot, b0 + t + 1)
                        if t >= 2:
                            act.wait_ge(b_tr, b0 + t - 1)
                        nc.scalar.copy(qs[:, t % 2, 0:GRP, 0:HD],
                                       rta[:, t % 2, 0:GRP * HD].rearrange("p (h d) -> p h d", d=HD)).then_inc(b_hi, 1)
                        nc.scalar.copy(qs[:, t % 2, GRP].rearrange("p (r d) -> p r d", d=HD),
                                       rta[:, t % 2:t % 2 + 1, GRP * HD:].to_broadcast([P, 2, HD])).then_inc(b_hi, 1)

                    def keep_q(t):
                        act.wait_ge(b_tr, b0 + t + 1)
                        nc.scalar.copy(q_st[:, :, t * P:(t + 1) * P],
                                       ps[:, 4 + 2 * (t % 2)].rearrange("p (h c) -> p h c", c=P)).then_inc(b_qT, 1)

                    for t in range(T):
                        outputs(t)
                        if t >= 4:
                            hi_parts(t - 4)
                        if t >= 5:
                            keep_q(t - 5)
                    hi_parts(4)
                    keep_q(3)
                    gate(0)
                    hi_parts(5)
                    keep_q(4)
                    hi_parts(6)
                    keep_q(5)
                    gate(1)
                    hi_parts(7)
                    keep_q(6)
                    keep_q(7)
                    gate(2)

                    a0 = L * (KVH * 4 * T) + j * (4 * T)
                    i0 = L * (KVH * 2 * T) + j * (2 * T)

                    def exponent(tile):
                        act.wait_ge(s_max, a0 + tile + 1)
                        if tile >= 3:
                            act.wait_ge(p_tr, a0 * 2 + 2 * tile - 4)
                        s = tile % 2
                        nc.scalar.activation(pp[:, tile % 3], ps[:, 2 * s:2 * s + 2].rearrange("p a b -> p (a b)"), ACT.Exp,
                                             bias=nmx[:, tile % 4:tile % 4 + 1],
                                             accum_out=rsm[:, tile % 4:tile % 4 + 1]).then_inc(s_exp, 1)

                    def hi_probs(tile):
                        e = tile // 2
                        for half in range(2):
                            g = 2 * tile + half
                            act.wait_ge(p_tr, a0 * 2 + g + 1)
                            if e >= 2:
                                act.wait_ge(pv_done, i0 + e - 1)
                            nc.scalar.copy(pT_hi[:, e % 2, 4 * half:4 * half + 4, (tile % 2) * P:(tile % 2 + 1) * P],
                                           ps[:, 4 + half].rearrange("p (k c) -> p k c", c=P)).then_inc(p_hi, 1)

                    for i in range(2 * T + 3):
                        for s in range(2):
                            if 1 <= i <= 2 * T:
                                hi_probs(2 * (i - 1) + s)
                            if s == 1 and 2 <= i < 2 * T + 2:
                                e = i - 2
                                pr = HD * (e // 4 % 2)
                                act.wait_ge(pv_done, i0 + e + 1)
                                if e >= 2:
                                    act.wait_ge(ua_l, i0 + e - 1)
                                nc.scalar.activation(av[pr:pr + HD, e % 2], ps[HD:2 * HD, 6 + e % 2, 0:256], ACT.Copy,
                                                     scale=0.5).then_inc(av_lo, 1)
                            if i < 2 * T:
                                exponent(2 * i + s)
                            if s == 0 and i >= 3:
                                e = i - 3
                                hh, qp = e // 4, e % 4
                                pr = HD * (hh % 2)
                                act.wait_ge(consts_in, NCONST)
                                act.wait_ge(av_gated, i0 + e + 1)
                                nc.scalar.copy(ua_hi[pr:pr + HD, bass.ds(j * 2 + hh // 2, 1), qp * 256:(qp + 1) * 256],
                                               av[pr:pr + HD, e % 2:e % 2 + 1]).then_inc(ua_h, 1)
                        if i == 0:
                            gate(3)
                    act.wait_ge(consts_in, NCONST)
                    act.wait_ge(ua_l, i0 + 2 * T)
                    act.drain().then_inc(phase_end, 1)

                act.wait_ge(phase_end, 3 + L * PH_L + 3 * (1 + KVH))
                for c in range(2):
                    act.dma_start(ctR[:, c], rope_r[:, c]).then_inc(c_tab, 16)
                act.dma_start(gwc[:], gn_w[:, bass.ds(L, 1), :].rearrange("p a h -> p (a h)")).then_inc(c_tab, 16)
                act.wait_ge(c_arg, L * (RH * 2) + 2)
                nc.scalar.activation(msk[:], msk[:], ACT.Exp).then_inc(c_mexp, 1)

                def keep_qk(h, t):
                    act.wait_ge(c_tr, L * (RH * T) + h * T + t + 1)
                    nc.scalar.copy(qkT[:, t], ps[:, 5, 0:2 * P]).then_inc(c_T, 1)

                def outputs(h, t):
                    c0 = L * (RH * T) + h * T
                    act.wait_ge(c_vgp, c0 + t + 1)
                    if t >= 2:
                        act.wait_ge(c_pv, c0 + t - 1)
                    v = ps[:, t % 2, 0:RD]
                    nc.scalar.copy(vv[:, t % 2], v).then_inc(c_v, 1)
                    for d in range(2):
                        nc.scalar.activation(vd[:, t % 2, d * RD:(d + 1) * RD], v, ACT.Copy, scale=dcur[:, 2 + d:3 + d]).then_inc(c_v, 1)
                    nc.scalar.activation(g2[:, t], ps[:, t % 2, RD:2 * RD], ACT.Tanh, scale=0.5).then_inc(c_th, 1)

                def update(h, t):
                    c0 = L * (RH * T) + h * T
                    if t >= 1:
                        act.wait_ge(c_u, c0 + t + 1)
                        nc.scalar.copy(us[:, t - 1, 1], ps[:, 3, RD:2 * RD]).then_inc(c_ub, 1)
                    act.wait_ge(c_pv, c0 + t + 1)
                    nc.scalar.copy(oc[:, t], ps[:, 4, 0:RD]).then_inc(c_oc, 1)

                def keep_out(h, half):
                    act.wait_ge(consts_in, NCONST)
                    act.wait_ge(c_ytr, L * (RH * 2) + h * 2 + half + 1)
                    nc.scalar.activation(ur_hi[:, bass.ds(h, 1), half * 512:(half + 1) * 512], ps[:, 7 - half:8 - half], ACT.Copy,
                                         scale=gwh[:]).then_inc(c_uh, 1)

                def first_pass(h, done):
                    for t in range(T):
                        if done is not None and t == 0:
                            update(done, T - 1)
                        if t >= 2:
                            keep_qk(h, t - 2)
                        if done is not None and t == 6:
                            act.wait_ge(c_arg, L * (RH * 2) + h * 2 + 2)
                            nc.scalar.activation(msk[:], msk[:], ACT.Exp).then_inc(c_mexp, 1)
                    if done is not None:
                        keep_out(done, 0)
                        keep_out(done, 1)

                def second_pass(h):
                    for t in range(T):
                        if t < 2:
                            keep_qk(h, T - 2 + t)
                        outputs(h, t)
                        if t >= 1:
                            update(h, t - 1)

                first_pass(0, None)
                with act.Fori(0, RH - 1) as h:
                    second_pass(h)
                    first_pass(h + 1, h)
                second_pass(RH - 1)
                update(RH - 1, T - 1)
                keep_out(RH - 1, 0)
                keep_out(RH - 1, 1)
                act.drain().then_inc(phase_end, 1)

                act.wait_ge(consts_in, NCONST)
                act.wait_ge(phase_end, 3 + L * PH_L + 3 * (2 + KVH))
                with act.Fori(0, 2) as b:
                    for i in range(4):
                        m = L * K + b * 4 + i
                        for kind in range(2):
                            for n in range(2):
                                act.wait_ge((d_gA, d_gB)[kind], m * 2 + n + 1)
                                act.wait_ge(d_mg, m * 2 + n if i else m * 2 + 1)
                                nc.scalar.activation((tA, tB)[kind][:, n], ps[:, GATE_BANK[kind][n]], ACT.Tanh, scale=0.5).then_inc((d_tA, d_tB)[kind], 1)
                act.drain().then_inc(phase_end, 1)

                act.wait_ge(phase_end, 3 + L * PH_L + 3 * (3 + KVH))
                for t in range(T):
                    nc.scalar.copy(hT_hi[:, :, t * P:(t + 1) * P], xm[:, :, t * P:(t + 1) * P]).then_inc(d_hi, 1)
                act.wait_ge(d_lo, L * T + T)
                act.wait_ge(x_saved, L * 16 + 16)
                for a in (0, 1):
                    act.dma_start(xm[:, 4 * a:4 * a + 4], xs.rearrange("(t p) d -> p t d", p=P)[:, 4 * a:4 * a + 4]).then_inc(x_back[a], 16)
                act.drain().then_inc(phase_end, 1)

            act.wait_ge(phase_end, 3 + DEPTH * PH_L)
            act.dma_start(gB[:], fin_g.to_broadcast([P, DM])).then_inc(gain_in, 16)
            for t in range(T):
                if t:
                    act.wait_ge(f_sq, t)
                nc.scalar.activation(junk[:], xtile(t), ACT.Square, accum_out=ss[:, t:t + 1]).then_inc(f_sq, 1)
            for t in range(T):
                act.wait_ge(f_y, t + 1)
                act.dma_start(out.rearrange("(t p) d -> p t d", p=P)[:, t], hb[:, t % 2]).then_inc(out_done[t % 2], 16)
            for s in range(2):
                act.wait_ge(out_done[s], 16 * (T // 2))

        @block.vector
        def _(dve):
            held[dve] = dve.alloc_register("held_dve")
            V = nc.vector

            def rsqrt(a, b, base):
                v, y, t_ = ss[:, a:b], rs[:, a:b], nt[:, a:b]
                V.tensor_scalar(y.bitcast(I32), v.bitcast(I32), -0.5, MAGIC, ALU.mult, ALU.add).then_inc(newton, 1)
                for r in range(3):
                    dve.wait_ge(newton, base + 3 * r + 1)
                    V.scalar_tensor_tensor(t_, y, -0.5, y, ALU.mult, ALU.mult).then_inc(newton, 1)
                    dve.wait_ge(newton, base + 3 * r + 2)
                    V.tensor_tensor(t_, t_, v, ALU.mult).then_inc(newton, 1)
                    dve.wait_ge(newton, base + 3 * r + 3)
                    V.scalar_tensor_tensor(y, t_, 1.5, y, ALU.add, ALU.mult).then_inc(newton, 1)
                dve.wait_ge(newton, base + 10)

            NW_L = 11 * (1 + 2 * KVH + RH)

            done = [0]

            def step(ins):
                done[0] += 1
                ins.then_inc(pro_dve, 1)
                dve.wait_ge(pro_dve, done[0])

            dve.wait_ge(consts_in, NCONST)
            step(V.tensor_scalar(lgw[:, 1], lgw[:, 0], -1.0, None, ALU.mult))
            step(V.tensor_tensor(lgw[:, 1], lgw[:, 1], lgw[:, 0], ALU.min))
            dve.wait_ge(pro_act, 2)
            step(V.tensor_scalar(lgw[:, 3], lgw[:, 2], 2.0, None, ALU.add))
            step(V.reciprocal(lgw[:, 3], lgw[:, 3]))
            step(V.tensor_tensor(lgw[:, 3], lgw[:, 3], lgw[:, 2], ALU.mult))
            step(V.tensor_tensor(lgw[:, 4], lgw[:, 3], lgw[:, 3], ALU.mult))
            step(V.tensor_scalar(lgw[:, 5], lgw[:, 4], 1.0 / 15, None, ALU.mult))
            for c in (13, 11, 9, 7, 5, 3):
                step(V.scalar_tensor_tensor(lgw[:, 5], lgw[:, 5], 1.0 / c, lgw[:, 4], ALU.add, ALU.mult))
            step(V.scalar_tensor_tensor(lgw[:, 5], lgw[:, 5], 1.0, lgw[:, 3], ALU.add, ALU.mult))
            step(V.tensor_scalar(lgw[:, 2], lgw[:, 0], 0.0, None, ALU.min))
            step(V.scalar_tensor_tensor(lgw[:, 2], lgw[:, 5], -2.0, lgw[:, 2], ALU.mult, ALU.add))
            half = DEPTH * RH
            for c in range(6):
                a = (c % 2) * half
                ins = V.tensor_scalar(dec[:, :, c], lgw[:, 2, a:a + half], icol[:, c:c + 1], None, ALU.mult)
                if c == 5:
                    step(ins)
                else:
                    ins.then_inc(pro_dve, 1)
                    done[0] += 1
            assert done[0] == 22, done
            dve.wait_ge(pro_act, 3)
            for c in (2, 3):
                step(V.tensor_scalar(dec[:, :, c], dec[:, :, c], RD ** -0.5, None, ALU.mult))
            for c in (6, 7):
                step(V.tensor_copy(dec[:, :, c], lgw[:, 2, (c - 6) * half:(c - 5) * half]))
            dve.sem_inc(d_res, T)
            for s in (d_mA, d_mB, d_mg):
                dve.sem_inc(s, 1)
            dve.drain().then_inc(phase_end, 1)

            with dve.Fori(0, DEPTH) as L:
                dve.wait_ge(phase_end, 3 + L * PH_L)
                dve.wait_ge(a_sq, L * T + T)
                nw = L * NW_L
                V.tensor_scalar(ss[:, 0:T], ss[:, 0:T], 1.0 / DM, EPS, ALU.mult, ALU.add).then_inc(newton, 1)
                dve.wait_ge(newton, nw + 1)
                rsqrt(0, T, nw + 1)
                dve.wait_ge(gain_in, L * 16 + 16)
                for t in range(T + 1):
                    if t < T:
                        if t >= 2:
                            dve.wait_ge(h_tr, L * T + t - 1)
                        V.scalar_tensor_tensor(hb[:, t % 2], xtile(t), rs[:, t:t + 1], gB[:], ALU.mult, ALU.mult).then_inc(h_ready, 1)
                    if t >= 1:
                        for hf in range(2):
                            dve.wait_ge(h_hi, L * (2 * T) + 2 * (t - 1) + hf + 1)
                            o = (slice(None), slice(4 * hf, 4 * hf + 4), slice((t - 1) * P, t * P))
                            V.tensor_tensor(hT_lo[o], ps[:, 2 * ((t - 1) % 2) + hf].rearrange("p (k c) -> p k c", c=P),
                                            hT_hi[o].bitcast(F32), ALU.subtract).then_inc(h_lo, 1)
                dve.drain().then_inc(phase_end, 1)

                with dve.Fori(0, KVH) as j:
                    dve.wait_ge(phase_end, 3 + L * PH_L + j * 3 + 3)
                    lj = L * KVH + j
                    dve.wait_ge(b_tab, lj * (16 * (3 + GRP)) + 16 * (3 + GRP))
                    V.tensor_scalar(gqk[:, 0:GRP * HD], gqk[:, 0:GRP * HD], HD ** -0.5, None, ALU.mult).then_inc(b_gain, 1)

                    def outputs(t):
                        bt = lj * T + t
                        dve.wait_ge(b_vh, bt + 1)
                        V.tensor_copy(zqk[:, t], ps[:, t % 2, 0:QK_W]).then_inc(b_z, 1)
                        dve.wait_ge(b_sq, bt + 1)
                        V.tensor_reduce(ss[:, t * (GRP + 1):(t + 1) * (GRP + 1)],
                                        sq[:, t % 2].rearrange("p (h d) -> p h d", d=HD), AXX, ALU.add).then_inc(b_ssum, 1)
                        V.tensor_tensor(v_st[:, t, HD:], ps[:, t % 2, QK_W:QK_W + HD], v_st[:, t, 0:HD].bitcast(F32),
                                        ALU.subtract).then_inc(b_free, 1)

                    def norms(half):
                        n = T // 2 * (GRP + 1)
                        nw = L * NW_L + j * 22 + 11 * half + 11
                        dve.wait_ge(b_ssum, lj * T + T // 2 * (half + 1))
                        V.tensor_scalar(ss[:, half * n:(half + 1) * n], ss[:, half * n:(half + 1) * n], 1.0 / HD, EPS,
                                        ALU.mult, ALU.add).then_inc(newton, 1)
                        dve.wait_ge(newton, nw + 1)
                        rsqrt(half * n, (half + 1) * n, nw + 1)
                        dve.wait_ge(b_z, lj * T + T // 2 * (half + 1))
                        dve.wait_ge(b_gain, lj + 1)

                    def gate(g):
                        dve.wait_ge(b_tanh, lj * 4 + g + 1)
                        V.scalar_tensor_tensor(gT[:, g // 2, (g % 2) * 512:(g % 2 + 1) * 512], tanh_gate(g), 1.0, ps[:, G_BANK[g]],
                                               ALU.add, ALU.mult).then_inc(b_gated, 1)

                    def rotate(t):
                        bt = lj * T + t
                        z = zqk[:, t].rearrange("p (h d) -> p h d", d=HD)
                        V.tensor_tensor(z, z, rs[:, t * (GRP + 1):(t + 1) * (GRP + 1)].rearrange("p (h o) -> p h o", o=1)
                                        .to_broadcast([P, GRP + 1, HD]), ALU.mult).then_inc(b_norm, 1)
                        dve.wait_ge(b_norm, bt * 2 + 1)
                        V.tensor_tensor(zqk[:, t], zqk[:, t], gqk[:], ALU.mult).then_inc(b_norm, 1)
                        dve.wait_ge(b_norm, bt * 2 + 2)
                        if t >= 2:
                            dve.wait_ge(b_rot, bt - 1)
                        z5 = zqk[:, t].rearrange("p (h a s d) -> p h a s d", a=2, s=2, d=HD // 4)
                        r5 = rtb[:, t % 2].rearrange("p (h a s d) -> p h a s d", a=2, s=2, d=HD // 4)
                        s5 = ctA[:, 1, t:t + 1].rearrange("p o (a s d) -> p o a s d", a=2, s=2, d=HD // 4)
                        for s in range(2):
                            V.tensor_tensor(r5[:, :, :, s], z5[:, :, :, 1 - s],
                                            s5[:, :, :, s].to_broadcast([P, GRP + 1, 2, HD // 4]), ALU.mult).then_inc(b_sin, 1)

                    def split(t):
                        bt = lj * T + t
                        dve.wait_ge(b_hi, bt * 2 + 2)
                        if t >= 2:
                            dve.wait_ge(b_tr, bt - 1)
                        V.tensor_tensor(qs[:, t % 2, 0:GRP, HD:], rta[:, t % 2, 0:GRP * HD].rearrange("p (h d) -> p h d", d=HD),
                                        qs[:, t % 2, 0:GRP, 0:HD].bitcast(F32), ALU.subtract).then_inc(b_lo, 1)
                        V.tensor_tensor(qs[:, t % 2, GRP + 1].rearrange("p (r d) -> p r d", d=HD),
                                        rta[:, t % 2:t % 2 + 1, GRP * HD:].to_broadcast([P, 2, HD]),
                                        qs[:, t % 2, GRP].rearrange("p (r d) -> p r d", d=HD).bitcast(F32), ALU.subtract).then_inc(b_lo, 1)

                    def keep_k(t):
                        dve.wait_ge(b_tr, lj * T + t + 1)
                        V.tensor_copy(k_st[:, :, t * P:(t + 1) * P],
                                      ps[:, 5 + 2 * (t % 2), 0:2 * P].rearrange("p (h c) -> p h c", c=P)).then_inc(b_kT, 1)

                    for t in range(4):
                        outputs(t)
                    norms(0)
                    rotate(0)
                    for t in range(4, T):
                        outputs(t)
                        if t < 7:
                            rotate(t - 3)
                        if t >= 5:
                            keep_k(t - 5)
                        if t < 7:
                            split(t - 4)
                    norms(1)
                    split(3)
                    rotate(4)
                    split(4)
                    keep_k(3)
                    rotate(5)
                    gate(0)
                    split(5)
                    keep_k(4)
                    rotate(6)
                    split(6)
                    keep_k(5)
                    gate(1)
                    rotate(7)
                    split(7)
                    keep_k(6)
                    keep_k(7)
                    gate(2)

                    a0 = lj * (4 * T)
                    i0 = lj * (2 * T)

                    def row_max(tile):
                        s = tile % 2
                        dve.wait_ge(s_done, a0 + tile + 1)
                        V.tensor_reduce(nmx[:, tile % 4:tile % 4 + 1], ps[:, 2 * s:2 * s + 2].rearrange("p a b -> p (a b)"),
                                        AXX, ALU.max, negate=True).then_inc(s_max, 1)

                    def lo_probs(tile):
                        e = tile // 2
                        for half in range(2):
                            dve.wait_ge(p_hi, a0 * 2 + 2 * tile + half + 1)
                            o = (slice(None), e % 2, slice(4 * half, 4 * half + 4), slice((tile % 2) * P, (tile % 2 + 1) * P))
                            V.tensor_tensor(pT_lo[o], ps[:, 4 + half].rearrange("p (k c) -> p k c", c=P),
                                            pT_hi[o].bitcast(F32), ALU.subtract).then_inc(p_lo, 1)

                    for i in range(2 * T + 2):
                        for s in range(2):
                            if i < 2 * T:
                                row_max(2 * i + s)
                            if 1 <= i <= 2 * T:
                                lo_probs(2 * (i - 1) + s)
                            if i < 2 * T:
                                tile = 2 * i + s
                                dve.wait_ge(s_exp, a0 + tile + 1)
                                V.reciprocal(rrc[:, tile % 4:tile % 4 + 1], rsm[:, tile % 4:tile % 4 + 1]).then_inc(s_rcp, 1)
                        if i == 0:
                            gate(3)
                        if i >= 2:
                            e = i - 2
                            pr = HD * (e // 4 % 2)
                            dve.wait_ge(av_lo, i0 + e + 1)
                            V.scalar_tensor_tensor(av[pr:pr + HD, e % 2], ps[0:HD, 6 + e % 2, 0:256], 0.5, av[pr:pr + HD, e % 2],
                                                   ALU.mult, ALU.add).then_inc(av_sum, 1)
                    dve.drain().then_inc(phase_end, 1)

                dve.wait_ge(phase_end, 3 + L * PH_L + 3 * (1 + KVH))
                dve.wait_ge(c_tab, L * 48 + 48)

                def factors(h):
                    lh = L * RH + h
                    V.tensor_copy(dcur[:], dec[:, bass.ds(lh, 1)].rearrange("p o c -> p (o c)")).then_inc(c_dec, 1)
                    dve.wait_ge(c_dec, lh + 1)
                    V.tensor_scalar(msk[:], dst[:, 0], dcur[:, 6:7], None, ALU.mult).then_inc(c_arg, 1)
                    dve.wait_ge(c_arg, lh * 2 + 1)
                    V.scalar_tensor_tensor(msk[:], dst[:, 1], dcur[:, 7:8], msk[:], ALU.mult, ALU.add).then_inc(c_arg, 1)

                def rotate(h, t):
                    c0 = L * (RH * T) + h * T
                    dve.wait_ge(c_qkp, c0 + t + 1)
                    if t >= 2:
                        dve.wait_ge(c_o, c0 + t - 1)
                    z = ps[:, t % 2, 0:2 * RD]
                    V.tensor_tensor(ra[:, t].rearrange("p (h d) -> p h d", d=RD), z.rearrange("p (h d) -> p h d", d=RD),
                                    ctR[:, 0, t:t + 1].to_broadcast([P, 2, RD]), ALU.mult).then_inc(c_rot, 1)
                    z5 = z.rearrange("p (h a s d) -> p h a s d", a=2, s=2, d=RD // 4)
                    r5 = rb[:, t % 2].rearrange("p (h a s d) -> p h a s d", a=2, s=2, d=RD // 4)
                    s5 = ctR[:, 1, t:t + 1].rearrange("p o (a s d) -> p o a s d", a=2, s=2, d=RD // 4)
                    for s in range(2):
                        V.tensor_tensor(r5[:, :, :, s], z5[:, :, :, 1 - s],
                                        s5[:, :, :, s].to_broadcast([P, 2, 2, RD // 4]), ALU.mult).then_inc(c_rot, 1)

                def decay_scores(h, t):
                    c0 = L * (RH * T) + h * T
                    dve.wait_ge(c_qk, c0 + t + 1)
                    if t == 0:
                        dve.wait_ge(c_mexp, L * RH + h + 1)
                    if t >= 2:
                        dve.wait_ge(c_pv, c0 + t - 1)
                    V.scalar_tensor_tensor(pm[:, t % 2], ps[:, 2, 0:P], RD ** -0.5, msk[:], ALU.mult, ALU.mult).then_inc(c_pm, 1)

                def gate(h, t):
                    dve.wait_ge(c_th, L * (RH * T) + h * T + t + 1)
                    V.scalar_tensor_tensor(g2[:, t], g2[:, t], 1.0, ps[:, t % 2, RD:2 * RD], ALU.add, ALU.mult).then_inc(c_g, 1)

                def update(h, t):
                    f0 = L * (RH * (T - 1)) + h * (T - 1)
                    dve.wait_ge(c_u, L * (RH * T) + h * T + t + 1)
                    if t >= 1:
                        dve.wait_ge(c_ub, f0 + t)
                        dve.wait_ge(c_uf, f0 + t)
                    else:
                        dve.wait_ge(c_zero, L * 2 + 2)
                    V.scalar_tensor_tensor(us[:, t + 1, 0], us[:, t, 0], dcur[:, 4:5], ps[:, 3, 0:RD], ALU.mult, ALU.add).then_inc(c_uf, 1)

                def backward(h):
                    dve.wait_ge(c_ub, L * (RH * (T - 1)) + h * (T - 1) + T - 1)
                    for n, c in enumerate(range(T - 3, -1, -1)):
                        if n:
                            dve.wait_ge(c_back, L * (RH * 6) + h * 6 + n)
                        V.scalar_tensor_tensor(us[:, c, 1], us[:, c + 1, 1], dcur[:, 5:6], us[:, c, 1], ALU.mult, ALU.add).then_inc(c_back, 1)
                    dve.wait_ge(consts_in, NCONST)
                    dve.wait_ge(c_oc, L * (RH * T) + h * T + T)

                def cross(h, e):
                    x0 = L * (RH * 4) + h * 4 + e + 1
                    dve.wait_ge(c_x, x0)
                    bank = ps[:, 6].rearrange("p (t s d) -> p t s d", t=2, s=2)
                    o = oc[:, 2 * e:2 * e + 2]
                    V.scalar_tensor_tensor(o, bank[:, :, 0], dcur[:, 0:1], o, ALU.mult, ALU.add).then_inc(c_xa, 1)
                    dve.wait_ge(c_xa, x0)
                    V.scalar_tensor_tensor(o, bank[:, :, 1], dcur[:, 1:2], o, ALU.mult, ALU.add).then_inc(c_xb, 1)
                    dve.wait_ge(c_xb, x0)
                    for t in (2 * e, 2 * e + 1):
                        V.bn_stats(st6[:, t], oc[:, t]).then_inc(c_bn, 1)

                def norms(h):
                    c0 = L * (RH * T) + h * T
                    V.tensor_scalar(gwh[:], gwc[:, bass.ds(h, 1)], 0.5, None, ALU.mult).then_inc(c_gw, 1)
                    dve.wait_ge(consts_in, NCONST)
                    dve.wait_ge(c_bn, c0 + T)
                    for t in range(T):
                        V.bn_aggr(mv[:, t], st6[:, t]).then_inc(c_mv, 1)
                    dve.wait_ge(c_mv, c0 + T)
                    nw = L * NW_L + h * 11 + 11 * (1 + 2 * KVH)
                    V.tensor_scalar(ss[:, 0:T], mv[:, :, 1], EPS, None, ALU.add).then_inc(newton, 1)
                    dve.wait_ge(newton, nw + 1)
                    rsqrt(0, T, nw + 1)

                def normed(h, half):
                    for t in range(4 * half, 4 * half + 4):
                        V.tensor_scalar(oc[:, t], oc[:, t], mv[:, t, 0:1], rs[:, t:t + 1], ALU.subtract, ALU.mult).then_inc(c_y, 1)
                    dve.wait_ge(c_y, L * (RH * T) + h * T + 4 * half + 4)
                    o = slice(4 * half, 4 * half + 4)
                    V.tensor_tensor(oc[:, o], oc[:, o], g2[:, o], ALU.mult).then_inc(c_yg, 1)

                def keep_out(h, half):
                    dve.wait_ge(consts_in, NCONST)
                    dve.wait_ge(c_uh, L * (RH * 2) + h * 2 + half + 1)
                    dve.wait_ge(c_gw, L * RH + h + 1)
                    o = (slice(None), bass.ds(h, 1), slice(half * 512, (half + 1) * 512))
                    V.scalar_tensor_tensor(ur_lo[o], ps[:, 7 - half:8 - half], gwh[:], ur_hi[o].bitcast(F32),
                                           ALU.mult, ALU.subtract).then_inc(c_ul, 1)

                def first_pass(h, done):
                    for t in range(T):
                        if done is not None and 2 <= t <= 5:
                            cross(done, t - 2)
                        rotate(h, t)
                        if done is not None:
                            if t == 0:
                                backward(done)
                            if t == 5:
                                norms(done)
                            if t >= 6:
                                normed(done, t - 6)
                            if t == 6:
                                factors(h)
                    if done is not None:
                        keep_out(done, 0)
                        keep_out(done, 1)

                def second_pass(h):
                    decay_scores(h, 0)
                    for t in range(T):
                        if t >= 1:
                            update(h, t - 1)
                        if t + 1 < T:
                            decay_scores(h, t + 1)
                        gate(h, t)

                factors(0)
                V.memset(us[:, 0, 0], 0.0).then_inc(c_zero, 1)
                V.memset(us[:, T - 1, 1], 0.0).then_inc(c_zero, 1)
                first_pass(0, None)
                with dve.Fori(0, RH - 1) as h:
                    second_pass(h)
                    first_pass(h + 1, h)
                second_pass(RH - 1)
                backward(RH - 1)
                for e in range(4):
                    cross(RH - 1, e)
                norms(RH - 1)
                for half in range(2):
                    normed(RH - 1, half)
                for half in range(2):
                    keep_out(RH - 1, half)
                dve.drain().then_inc(phase_end, 1)

                wait_apart(dve, phase_end, 3 + L * PH_L + 3 * (2 + KVH))
                with dve.Fori(0, 2) as b:
                    for i in range(4):
                        m = L * K + b * 4 + i
                        for n in range(2):
                            dve.wait_ge(d_tA, m * 2 + n + 2)
                            dve.wait_ge(d_ya, m * 2 + n + 1)
                            V.scalar_tensor_tensor(tA[:, n], tA[:, n], 1.0, ps[:, BRANCH_BANK[0][n]], ALU.add, ALU.mult).then_inc(d_mA, 1)
                        for n in range(2):
                            dve.wait_ge(d_tB, m * 2 + n + 2)
                            dve.wait_ge(d_yb, m * 2 + n + 1)
                            V.scalar_tensor_tensor(tB[:, n], tB[:, n], 1.0, ps[:, BRANCH_BANK[1][n]], ALU.add, ALU.mult).then_inc(d_mB, 1)
                            dve.wait_ge(consts_in, NCONST)
                            dve.wait_ge(d_mB, m * 2 + n + 2)
                            dve.wait_ge(d_mA, m * 2 + n + 2)
                            V.tensor_tensor(xm[:, bass.ds(b * 4 + i, 1), n * 512:(n + 1) * 512], tA[:, n:n + 1], tB[:, n:n + 1],
                                            ALU.add).then_inc(d_mg, 1)
                dve.drain().then_inc(phase_end, 1)

                dve.wait_ge(phase_end, 3 + L * PH_L + 3 * (3 + KVH))
                for t in range(T):
                    dve.wait_ge(d_hi, L * T + t + 1)
                    o = (slice(None), slice(None), slice(t * P, (t + 1) * P))
                    V.tensor_tensor(hT_lo[o], xm[o], hT_hi[o].bitcast(F32), ALU.subtract).then_inc(d_lo, 1)
                with dve.Fori(0, 2) as b:
                    for i in range(2):
                        for t in range(T):
                            dve.wait_ge(consts_in, NCONST)
                            dve.wait_ge(d_out, L * (4 * T) + b * (2 * T) + i * T + t + 1)
                            if i == 0 and t % 4 == 0:
                                dve.wait_ge(x_back[t // 4], L * 16 + 16)
                            o = (slice(None), slice(t, t + 1), bass.ds(b * 512 + i * 256, 256))
                            V.scalar_tensor_tensor(xm[o], ps[:, t:t + 1, 0:256], 0.5, xm[o], ALU.mult, ALU.add).then_inc(d_res, 1)
                dve.drain().then_inc(phase_end, 1)

            dve.wait_ge(f_sq, T)
            dve.wait_ge(gain_in, DEPTH * 16 + 16)
            nw = DEPTH * NW_L
            V.tensor_scalar(ss[:, 0:T], ss[:, 0:T], 1.0 / DM, EPS, ALU.mult, ALU.add).then_inc(newton, 1)
            dve.wait_ge(newton, nw + 1)
            rsqrt(0, T, nw + 1)
            for t in range(T):
                if t >= 2:
                    dve.wait_ge(out_done[t % 2], 16 * (t // 2))
                V.scalar_tensor_tensor(hb[:, t % 2], xtile(t), rs[:, t:t + 1], gB[:], ALU.mult, ALU.mult).then_inc(f_y, 1)


def _rope(width):
    d_axis = width // 2
    q = width // 4
    inv = (THETA ** (-np.arange(0, d_axis, 2, dtype=np.float32) / np.float32(d_axis))).astype(np.float32)
    t = np.arange(SEQ)
    ang = np.stack([(t // GRID_W)[:, None].astype(np.float32) * inv, (t % GRID_W)[:, None].astype(np.float32) * inv], 1)
    c, s = np.cos(ang), np.sin(ang)
    full = np.stack([np.stack([c, c], 2), np.stack([-s, s], 2)], 0).reshape(2, T, P, 4 * q)
    return np.ascontiguousarray(full.transpose(2, 0, 1, 3)).astype(np.float32)


def _constants():
    i = np.arange(P, dtype=np.float32)
    diff = i[None, :] - i[:, None]
    dist = np.stack([np.maximum(diff, 0), np.maximum(-diff, 0)], 1)
    full = np.full(P, P, np.float32)
    idx = np.stack([i + 1, P - i, P - 1 - i, i, full, full], 1)
    return {"ident": np.eye(P, dtype=np.float32), "rope_a": _rope(HD), "rope_r": _rope(RD),
            "dist": np.ascontiguousarray(dist), "idx": np.ascontiguousarray(idx)}


def kernel(x, norm_g, w_in, attn_q_norm, attn_k_norm, ret_decay_fwd, ret_decay_bwd, ret_gn_w,
           w_branch_attn, w_branch_ret, w_out, final_norm_g):
    import concourse.bacc as bacc
    from concourse.bass_utils import run_bass_kernel_spmd

    a = lambda v, *s: np.ascontiguousarray(np.asarray(v).reshape(*s))
    arrays = {
        "x": a(x, SEQ, DM), "norm_g": a(norm_g, DEPTH, DM), "w_in": a(w_in, DEPTH * DM, D_IN),
        "qn": a(attn_q_norm, DEPTH, HD), "kn": a(attn_k_norm, DEPTH, HD),
        "dec_f": a(ret_decay_fwd, DEPTH, RH), "dec_b": a(ret_decay_bwd, DEPTH, RH),
        "gn_w": np.ascontiguousarray(np.asarray(ret_gn_w).reshape(DEPTH, RH, RD).transpose(2, 0, 1)),
        "w_a": a(w_branch_attn, DEPTH * AW, DM), "w_r": a(w_branch_ret, DEPTH * RW, DM),
        "w_o": a(w_out, DEPTH * DM, DM), "fin_g": a(final_norm_g, 1, DM), **_constants(),
    }
    nc = bacc.Bacc("TRN2", target_bir_lowering=False, num_devices=1, dynamic_dma_scratch_size=1024)
    aps = {n: nc.dram_tensor(n, v.shape, mybir.dt.from_np(v.dtype), kind="ExternalInput").ap() for n, v in arrays.items()}
    xs = nc.dram_tensor("xs", (SEQ, DM), F32, kind="Internal").ap()
    out = nc.dram_tensor("out", (SEQ, DM), F32, kind="ExternalOutput").ap()
    build(nc, xs=xs, out=out, **aps)
    r = run_bass_kernel_spmd(nc, [arrays], core_ids=[0])
    return r.results[0]["out"].reshape(np.asarray(x).shape)
```

```python
from contextlib import ExitStack

import numpy as np

import concourse.bass as bass
from concourse import mybir

F32 = mybir.dt.float32
F32R = mybir.dt.float32r
I32 = mybir.dt.int32
ALU = mybir.AluOpType
ACT = mybir.ActivationFunctionType
AXX = mybir.AxisListType.X

P = 128
DM = 1024
SEQ = 1024
DEPTH = 2
GRID_W = 64
QH, KVH, HD = 8, 2, 64
GRP = QH // KVH
RH, RD = 4, 128
AW, KVW, RW = QH * HD, KVH * HD, RH * RD
EPS = 1e-6
THETA = 10000.0
T = SEQ // P
K = DM // P
KA = AW // P
OFF = np.cumsum([0, AW, KVW, KVW, AW, RW, RW, RW, RW]).tolist()
C_QA, C_KA, C_VA, C_GA, C_QR, C_KR, C_VR, C_GR, C_GM = OFF
D_IN = C_GM + 2 * DM
QK_W = (GRP + 1) * HD
N_B, N_C, N_D1, N_D2 = 5, 4, 3, 2
U_C = KVH * N_B
U_D1 = U_C + RH * N_C
U_D2 = U_D1 + K * N_D1
U_L = U_D2 + 4 * N_D2
PH_L = 3 * (KVH + 2)
G_BANK = (2, 3, 2, 6)
QK_BANKS = lambda done: 4 if done is None else 2
GATE_BANK = ((0, 1), (2, 5))
BRANCH_BANK = ((3, 4), (6, 7))
X0 = T * (GRP + 1)
MAGIC = 1597463007.0


def build(nc, x, gains, w_in, qn, kn, dec_f, dec_b, gn_w, w_a, w_r, w_o,
          ident, rope_a, rope_r, dist, idx, xs, out):
    with ExitStack() as ctx:
        def sem(name):
            return ctx.enter_context(nc.semaphore(name))

        def sb(c, name, shape, dt=F32):
            return c.enter_context(nc.sbuf_tensor(name, [P] + shape, dt))

        ps = ctx.enter_context(nc.psum_tensor("ps", [P, 8, 512], F32))
        hT_hi = sb(ctx, "hT_hi", [K, SEQ], F32R)
        hT_lo = sb(ctx, "hT_lo", [K, SEQ], F32R)
        w_hi = sb(ctx, "w_hi", [K, 4 * P], F32R)
        w_lo = sb(ctx, "w_lo", [K, 4 * P], F32R)
        raw = sb(ctx, "raw", [2, K, P])
        idf = sb(ctx, "idf", [P])
        idr = sb(ctx, "idr", [P], F32R)
        dst = sb(ctx, "dst", [2, P])
        dec = sb(ctx, "dec", [DEPTH * RH, 8])
        dcur = sb(ctx, "dcur", [8])
        icol = sb(ctx, "icol", [6])
        lgw = sb(ctx, "lgw", [6, 2 * DEPTH * RH])
        msk = sb(ctx, "msk", [P])
        gwh = sb(ctx, "gwh", [1])
        gwc = sb(ctx, "gwc", [RH])
        ss = sb(ctx, "ss", [T * (GRP + 1) + T])
        rs = sb(ctx, "rs", [T * (GRP + 1) + T])
        nt = sb(ctx, "nt", [T * (GRP + 1) + T])
        st6 = sb(ctx, "st6", [T, 6])
        mv = sb(ctx, "mv", [T, 2])
        nmx = sb(ctx, "nmx", [4])
        rsm = sb(ctx, "rsm", [4])
        rrc = sb(ctx, "rrc", [4])
        ua_hi = sb(ctx, "ua_hi", [KA, SEQ], F32R)
        ua_lo = sb(ctx, "ua_lo", [KA, SEQ], F32R)
        ss4 = sb(ctx, "ss4", [4 * T])
        with ExitStack() as p1:
            zqk = sb(p1, "zqk", [T, QK_W])
            ctA = sb(p1, "ctA", [2, T, HD])
            gqk = sb(p1, "gqk", [QK_W])
            sq = sb(p1, "sq", [2, QK_W])
            rta = sb(p1, "rta", [2, QK_W])
            rtb = sb(p1, "rtb", [2, QK_W])
            qs = sb(p1, "qs", [2, GRP + 2, P], F32R)
        with ExitStack() as p2:
            pT_hi = sb(p2, "pT_hi", [2, T, 256], F32R)
            pT_lo = sb(p2, "pT_lo", [2, T, 256], F32R)
        ur_hi = sb(ctx, "ur_hi", [KA, SEQ], F32R)
        ur_lo = sb(ctx, "ur_lo", [KA, SEQ], F32R)
        with ExitStack() as pc:
            us = sb(pc, "us", [T, 2, RD])
            oc = sb(pc, "oc", [T, RD])
            g2 = sb(pc, "g2", [T, RD])
            ctR = sb(pc, "ctR", [2, T, RD])
            ra = sb(pc, "ra", [T, 2 * RD])
            rb = sb(pc, "rb", [2, 2 * RD])
            qkT = sb(pc, "qkT", [T, 2 * P])
            pm = sb(pc, "pm", [2, P])
            vv = sb(pc, "vv", [2, RD])
            vd = sb(pc, "vd", [2, 2 * RD])
        with ExitStack() as pb:
            gT = sb(pb, "gT", [2, SEQ])
            q_st = sb(pb, "q_st", [GRP, SEQ], F32R)
            k_st = sb(pb, "k_st", [2, SEQ], F32R)
        xm = sb(ctx, "xm", [T, DM])
        with ExitStack() as p3:
            thA = sb(p3, "thA", [2, 512])
        with ExitStack() as pp_:
            pp = sb(pp_, "pp", [3, SEQ])
        with ExitStack() as pd:
            tA = sb(pd, "tA", [2, 512])
            tB = sb(pd, "tB", [2, 512])
        hb = sb(ctx, "hb", [2, DM])
        gB = sb(ctx, "gB", [DM])
        with ExitStack() as pv:
            v_st = sb(pv, "v_st", [T, 2 * HD], F32R)
            av = sb(pv, "av", [2, 256])
        with ExitStack() as pj:
            junk = sb(pj, "junk", [DM])

        consts_in, x_saved = map(sem, ("consts_in", "x_saved"))
        x_in = [sem("x_in%d" % i) for i in range(4)]
        x_back = [sem("x_back0"), sem("x_back1")]
        out_done = [sem("out_done0"), sem("out_done1")]
        raw_in = [sem("raw_in0"), sem("raw_in1")]
        w_rounded, w_half, w_ready, phase_end = map(sem, ("w_rounded", "w_half", "w_ready", "phase_end"))
        pro_dve, pro_act, newton = map(sem, ("pro_dve", "pro_act", "newton"))
        gain_in, a_sq, h_ready, h_tr, h_hi, h_lo = map(sem, ("gain_in", "a_sq", "h_ready", "h_tr", "h_hi", "h_lo"))
        b_tab, b_gain, b_proj, b_z, b_sq, b_vh, b_ssum, b_free = map(sem, (
            "b_tab", "b_gain", "b_proj", "b_z", "b_sq", "b_vh", "b_ssum", "b_free"))
        b_gate, b_tanh, b_gated, b_norm, b_cos, b_sin, b_rot, b_hi, b_lo, b_tr, b_qT, b_kT = map(sem, (
            "b_gate", "b_tanh", "b_gated", "b_norm", "b_cos", "b_sin", "b_rot", "b_hi", "b_lo", "b_tr", "b_qT", "b_kT"))
        s_done, s_max, s_exp, s_rcp, p_norm, p_tr, p_hi, p_lo = map(sem, (
            "s_done", "s_max", "s_exp", "s_rcp", "p_norm", "p_tr", "p_hi", "p_lo"))
        pv_done, av_lo, av_sum, av_gated, ua_h, ua_l = map(sem, ("pv_done", "av_lo", "av_sum", "av_gated", "ua_h", "ua_l"))
        c_tab, c_dec, c_arg, c_mexp, c_gw, c_zero = map(sem, ("c_tab", "c_dec", "c_arg", "c_mexp", "c_gw", "c_zero"))
        c_qkp, c_rot, c_o, c_tr, c_T = map(sem, ("c_qkp", "c_rot", "c_o", "c_tr", "c_T"))
        c_vgp, c_v, c_th, c_g, c_qk, c_pm, c_u, c_uf, c_ub, c_pv, c_oc = map(sem, (
            "c_vgp", "c_v", "c_th", "c_g", "c_qk", "c_pm", "c_u", "c_uf", "c_ub", "c_pv", "c_oc"))
        c_back, c_x, c_xa, c_xb, c_bn, c_mv, c_y, c_yg, c_ytr, c_uh, c_ul = map(sem, (
            "c_back", "c_x", "c_xa", "c_xb", "c_bn", "c_mv", "c_y", "c_yg", "c_ytr", "c_uh", "c_ul"))
        d_gA, d_gB, d_ya, d_yb, d_tA, d_tB, d_mA, d_mB, d_mg = map(sem, (
            "d_gA", "d_gB", "d_ya", "d_yb", "d_tA", "d_tB", "d_mA", "d_mB", "d_mg"))
        d_hi, d_lo, d_out, d_res = map(sem, ("d_hi", "d_lo", "d_out", "d_res"))
        f_y, a_zero = sem("f_y"), sem("a_zero")
        NCONST = 16 * 7

        held = {}

        def wait_apart(eng, sem_, value):
            eng.reg_add(held[eng], value, 0)
            eng.wait_ge(consts_in, NCONST)
            eng.wait_ge(sem_, held[eng])

        block = ctx.enter_context(nc.Block())

        def tanh_gate(g):
            return pp[:, 2, 0:512] if g == 3 else thA[:, g % 2]

        def xtile(t):
            return xm[:, t, :]

        def put_out(eng, t):
            if t < 2:
                eng.wait_ge(h_ready, DEPTH * T + t + 1)
            else:
                eng.wait_ge(f_y, t - 1)
            eng.dma_start(out.rearrange("(t p) d -> p t d", p=P)[:, t], hb[:, t] if t < 2 else xtile(t)).then_inc(out_done[t % 2], 16)

        @block.sync
        def _(sp):
            def unit(slot, wait_for, parts):
                sp.wait_ge(w_ready, 1 + wait_for)
                for dst_ap, src in parts:
                    sp.dma_start(dst_ap, src).then_inc(raw_in[slot], 16)

            def cols(slot, L, c0, half_rows=K // 2):
                src = w_in[bass.ds(L * DM, DM), bass.ds(c0, P)].rearrange("(k p) c -> p k c", p=P)
                return [(raw[:, slot, a:a + half_rows], src[:, a:a + half_rows]) for a in (0, half_rows)]

            with sp.Fori(0, DEPTH) as L:
                u0 = L * U_L
                with sp.Fori(0, KVH) as j:
                    n0 = u0 + j * N_B
                    for i in range(N_B):
                        before = n0 + (i - 1 if i > 1 else 0)
                        if i in (0, 1):
                            parts = cols(i % 2, L, C_QA + j * (GRP * HD) + i * P)
                        elif i == 2:
                            parts = [(raw[:, 0, :, s * HD:(s + 1) * HD],
                                      w_in[bass.ds(L * DM, DM), bass.ds(c0 + j * HD, HD)].rearrange("(k p) c -> p k c", p=P))
                                     for s, c0 in ((0, C_KA), (1, C_VA))]
                        else:
                            parts = cols(i % 2, L, C_GA + j * (GRP * HD) + (i - 3) * P)
                        unit(i % 2, before, parts)
                with sp.Fori(0, RH) as h:
                    n0 = u0 + U_C + h * N_C
                    for i, c0 in enumerate((C_QR, C_KR, C_VR, C_GR)):
                        unit(i % 2, n0 + (i - 1 if i else 0), cols(i % 2, L, c0 + h * RD))
                with sp.Fori(0, K // 2) as mm:
                    n0 = u0 + U_D1 + mm * (2 * N_D1)
                    for i in range(2 * N_D1):
                        m = mm * 2 + i // N_D1
                        slot = i % 2
                        if i % N_D1 < 2:
                            parts = cols(slot, L, C_GM + (i % N_D1) * DM + m * P)
                        else:
                            parts = [(raw[:, slot, a:a + KA], w[bass.ds(L * AW, AW), bass.ds(m * P, P)].rearrange("(k p) c -> p k c", p=P))
                                     for a, w in ((0, w_a), (KA, w_r))]
                        unit(slot, n0 + i - 1, parts)
                with sp.Fori(0, 4) as nn:
                    n0 = u0 + U_D2 + nn * N_D2
                    for i in range(N_D2):
                        src = w_o[bass.ds(L * DM, DM), bass.ds(nn * (2 * P) + i * P, P)].rearrange("(k p) c -> p k c", p=P)
                        unit(i, n0 + i - 1, [(raw[:, i, a:a + K // 2], src[:, a:a + K // 2]) for a in (0, K // 2)])
            for t in range(1, T, 2):
                put_out(sp, t)
            sp.wait_ge(out_done[1], 16 * (T // 2))

        @block.gpsimd
        def _(pool):
            held[pool] = pool.alloc_register("held_pool")
            def place(pos):
                return w_hi[:, :, pos * P:(pos + 1) * P], w_lo[:, :, pos * P:(pos + 1) * P]

            def fill_hi(slot, pos, n_slot):
                wait_apart(pool, raw_in[slot], n_slot * 32 + 32)
                nc.gpsimd.tensor_scalar(place(pos)[0], raw[:, slot], 1.0, 1.0, ALU.mult, ALU.mult).then_inc(w_rounded, 1)

            def fill_lo(slot, pos, n):
                hi, lo = place(pos)
                pool.wait_ge(w_rounded, n + 1)
                nc.gpsimd.tensor_tensor(lo, raw[:, slot], hi.bitcast(F32), ALU.subtract).then_inc(w_ready, 1)

            def fill_lo_part(slot, pos, n, part):
                hi, lo = place(pos)
                if part == 0:
                    pool.wait_ge(w_rounded, n + 1)
                ks = slice(4 * part, 4 * part + 4)
                nc.gpsimd.tensor_tensor(lo[:, ks], raw[:, slot, ks], hi[:, ks].bitcast(F32),
                                        ALU.subtract).then_inc((w_half, w_ready)[part], 1)

            def fill(slot, pos, n_slot, n):
                fill_hi(slot, pos, n_slot)
                fill_lo(slot, pos, n)

            pool.sem_inc(w_ready, 1)
            PER = (3 * KVH + (U_L - U_C) // 2, 2 * KVH + (U_L - U_C) // 2)
            with pool.Fori(0, DEPTH) as L:
                n0 = L * U_L
                for i in range(4):
                    if i % 2 == 0:
                        pool.wait_ge(d_out, L * (4 * T) + T * (1 + i // 2))
                    fill(i % 2, i, L * PER[i % 2] + i // 2, n0 + i)
                with pool.Fori(0, KVH) as j:
                    for t in range(T):
                        bt = L * (KVH * T) + j * T + t
                        pool.wait_ge(b_norm, bt * 2 + 2)
                        if t >= 2:
                            pool.wait_ge(b_lo, bt * 2 - 2)
                        nc.gpsimd.tensor_tensor(rta[:, t % 2].rearrange("p (h d) -> p h d", d=HD),
                                                zqk[:, t].rearrange("p (h d) -> p h d", d=HD),
                                                ctA[:, 0, t:t + 1].to_broadcast([P, GRP + 1, HD]), ALU.mult).then_inc(b_cos, 1)
                        pool.wait_ge(b_cos, bt + 1)
                        pool.wait_ge(b_sin, bt * 2 + 2)
                        nc.gpsimd.tensor_tensor(rta[:, t % 2], rta[:, t % 2], rtb[:, t % 2], ALU.add).then_inc(b_rot, 1)
                        if t == 3:
                            pool.wait_ge(b_proj, L * (KVH * T) + j * T + T)
                            fill(0, 0, L * PER[0] + j * 3 + 2, n0 + j * N_B + 4)
                    a0 = L * (KVH * 4 * T) + j * (4 * T)
                    i0 = L * (KVH * 2 * T) + j * (2 * T)

                    def divide(tile):
                        wait_apart(pool, s_rcp, a0 + tile + 1)
                        nc.gpsimd.tensor_scalar(pp[:, tile % 3], pp[:, tile % 3], rrc[:, tile % 4:tile % 4 + 1], 1.0,
                                                ALU.mult, ALU.mult).then_inc(p_norm, 1)

                    for i in range(2 * T + 3):
                        if i >= 3:
                            pool.wait_ge(consts_in, NCONST)
                            pool.wait_ge(av_gated, i0 + min(i - 2, 2 * T))
                        if 2 <= i < 14:
                            u = (i - 2) // 3
                            if i == 2:
                                pool.wait_ge(b_gate, L * (KVH * 4) + j * 4 + 4)
                            if (i - 2) % 3 == 0:
                                fill_hi(u % 2, u, L * PER[u % 2] + j * (3, 2)[u % 2] + (3, 2)[u % 2] + u // 2)
                            else:
                                fill_lo_part(u % 2, u, n0 + j * N_B + N_B + u, (i - 2) % 3 - 1)
                        if i < 2 * T:
                            divide(2 * i)
                        if i >= 3:
                            e = i - 3
                            hh, qp = e // 4, e % 4
                            pr = HD * (hh % 2)
                            pool.wait_ge(consts_in, NCONST)
                            pool.wait_ge(ua_h, i0 + e + 1)
                            if i < 2 * T:
                                pool.wait_ge(p_norm, a0 + 2 * i + 1)
                            else:
                                pool.wait_ge(av_gated, i0 + min(i - 2, 2 * T))
                            o = (slice(pr, pr + HD), bass.ds(j * 2 + hh // 2, 1), slice(qp * 256, (qp + 1) * 256))
                            nc.gpsimd.tensor_tensor(ua_lo[o], av[pr:pr + HD, e % 2:e % 2 + 1], ua_hi[o].bitcast(F32),
                                                    ALU.subtract).then_inc(ua_l, 1)
                            pool.wait_ge(consts_in, NCONST)
                            pool.wait_ge(ua_l, i0 + e + 1)
                        if i < 2 * T:
                            divide(2 * i + 1)
                        if 2 <= i < 2 * T + 2:
                            e = i - 2
                            hh, qp = e // 4, e % 4
                            pr = HD * (hh % 2)
                            pool.wait_ge(av_sum, i0 + e + 1)
                            if i < 2 * T:
                                pool.wait_ge(p_norm, a0 + 2 * i + 2)
                            nc.gpsimd.tensor_tensor(av[pr:pr + HD, e % 2], av[pr:pr + HD, e % 2],
                                                    gT[pr:pr + HD, hh // 2, qp * 256:(qp + 1) * 256], ALU.mult).then_inc(av_gated, 1)
                def rotate(h, fills):
                    c0 = L * (RH * T) + h * T
                    for t in range(T):
                        pool.wait_ge(c_rot, c0 * 3 + 3 * t + 3)
                        nc.gpsimd.tensor_tensor(ra[:, t], ra[:, t], rb[:, t % 2], ALU.add).then_inc(c_o, 1)
                        if fills is not None and t < 4:
                            if t == 0:
                                pool.wait_ge(c_vgp, c0)
                            i = 2 + t // 2
                            if t % 2 == 0:
                                fill_hi(i % 2, i, L * PER[i % 2] + (3, 2)[i % 2] * KVH + fills * 2 + 2 + i // 2)
                            else:
                                fill_lo(i % 2, i, n0 + U_C + fills * N_C + N_C + i)

                def fill_qk(h):
                    pool.wait_ge(c_qkp, L * (RH * T) + h * T + T)
                    for i in range(2):
                        fill(i, i, L * PER[i] + (3, 2)[i] * KVH + h * 2 + 2, n0 + U_C + h * N_C + N_C + i)

                rotate(0, None)
                with pool.Fori(0, RH - 1) as h:
                    fill_qk(h)
                    rotate(h + 1, h)
                fill_qk(RH - 1)
                pool.wait_ge(c_vgp, L * (RH * T) + RH * T)

                def fill_d1(m, kind, pos, u, b):
                    if u > 2:
                        pool.wait_ge((d_gA, d_gB, d_yb)[kind], L * (2 * K) + m * 2)
                    fill(u % 2, pos, L * PER[u % 2] + (3, 2)[u % 2] * KVH + 2 * RH + b * 3 + u // 2, n0 + U_D1 + b * 6 + u)

                fill_d1(0, 2, 2, 2, 0)
                with pool.Fori(0, K // 2 - 1) as b:
                    for i in (1, 2):
                        for kind in range(3):
                            fill_d1(2 * b + i, kind, (0, 1, 2 + i % 2)[kind], 3 * i + kind, b)
                for kind in range(3):
                    fill_d1(K - 1, kind, (0, 1, 3)[kind], 3 + kind, K // 2 - 1)
                for i in range(4):
                    pool.wait_ge((d_gA, d_gB, d_yb, d_yb)[i], L * (2 * K) + 2 * K - (2 if i == 2 else 0))
                    fill(i % 2, i, L * PER[i % 2] + (3, 2)[i % 2] * KVH + 2 * RH + K * N_D1 // 2 + i // 2, n0 + U_D2 + i)
                for i in range(4):
                    pool.wait_ge(d_out, L * (4 * T) + (i // 2 + 3) * T)
                    fill(i % 2, i, L * PER[i % 2] + (3, 2)[i % 2] * KVH + 2 * RH + K * N_D1 // 2 + 2 + i // 2,
                         n0 + U_D2 + 4 + i)

        @block.tensor
        def _(pe):
            held[pe] = pe.alloc_register("held_pe")
            def prod3(outp, pairs, start=True, stop=True):
                for i, ((ah, al), (bh, bl)) in enumerate(pairs):
                    nc.tensor.matmul(outp, ah, bh, start=(start and i == 0), stop=False)
                    nc.tensor.matmul(outp, ah, bl, start=False, stop=False)
                    last = nc.tensor.matmul(outp, al, bh, start=False, stop=(stop and i == len(pairs) - 1))
                return last

            def h_l(k, t):
                return hT_hi[:, k, t * P:(t + 1) * P], hT_lo[:, k, t * P:(t + 1) * P]

            def h_r(k, n):
                return hT_hi[:, k, n * 512:(n + 1) * 512], hT_lo[:, k, n * 512:(n + 1) * 512]

            def w_u(k, a, b):
                return w_hi[:, k, a:b], w_lo[:, k, a:b]

            pe.wait_ge(consts_in, NCONST)
            pe.wait_ge(pro_act, 1)
            pe.sem_inc(d_out, 2 * T)
            pe.drain().then_inc(phase_end, 1)
            with pe.Fori(0, DEPTH) as L:
                def turn_x(t):
                    pe.wait_ge(h_ready, L * T + t + 1)
                    if t >= 2:
                        pe.wait_ge(h_lo, L * (2 * T) + 2 * t - 2)
                    for k in range(K):
                        last = nc.tensor.transpose(ps[:, 4 + 2 * (t % 2) + k // 4, (k % 4) * P:(k % 4 + 1) * P],
                                                   hb[:, t % 2, k * P:(k + 1) * P], idf[:])
                    last.then_inc(h_tr, 1)

                for j in range(KVH):
                    if j == 0:
                        pe.wait_ge(d_res, L * (4 * T) + T)
                        turn_x(0)
                    pe.wait_ge(w_ready, 1 + L * U_L + j * N_B + 3)

                    def project(t):
                        if j == 0:
                            pe.wait_ge(h_lo, L * (2 * T) + 2 * t + 2)
                        if t >= 2:
                            pe.wait_ge(b_free, L * (KVH * T) + j * T + t - 1)
                        prod3(ps[:, t % 2, 0:3 * P], [(h_l(k, t), w_u(k, 0, 3 * P)) for k in range(K)]).then_inc(b_proj, 1)

                    def gate(g, part):
                        mt, n = g // 2, g % 2
                        pos = (3, 0)[mt]
                        if part == 0:
                            if n == 0:
                                pe.wait_ge(w_ready, 1 + L * U_L + j * N_B + 4 + mt)
                            if g == 2:
                                pe.wait_ge(b_gated, L * (KVH * 4) + j * 4 + 1)
                            elif g == 3:
                                pe.wait_ge(b_qT, L * (KVH * T) + j * T + T)
                        last = prod3(ps[:, G_BANK[g], :],
                                     [(w_u(k, pos * P, (pos + 1) * P), h_r(k, n)) for k in range(4 * part, 4 * part + 4)],
                                     start=(part == 0), stop=(part == 1))
                        if part == 1:
                            last.then_inc(b_gate, 1)

                    def turn(t):
                        bt = L * (KVH * T) + j * T + t
                        pe.wait_ge(b_lo, bt * 2 + 2)
                        pe.wait_ge(b_hi, bt * 2 + 2)
                        if t >= 2:
                            pe.wait_ge(b_kT, bt - 1)
                            pe.wait_ge(b_qT, bt - 1)
                        elif j == 0:
                            pe.wait_ge(h_lo, L * (2 * T) + 2 * (T - 2 + t) + 2)
                        for c in range(GRP + 2):
                            bank = 4 + 2 * (t % 2) + c // GRP
                            last = nc.tensor.transpose(ps[:, bank, (c % GRP) * P:(c % GRP + 1) * P].bitcast(F32R),
                                                       qs[:, t % 2, c], idr[:])
                        last.then_inc(b_tr, 1)

                    for t in range(T):
                        if j == 0 and t + 1 < T:
                            turn_x(t + 1)
                        project(t)
                        if t >= 5:
                            turn(t - 5)
                    for i in range(5):
                        gate(i // 2, i % 2)
                        turn(i + 3)
                    gate(2, 1)
                    b2 = L * (KVH * T) + j * T
                    a0 = L * (KVH * 4 * T) + j * (4 * T)

                    def scores(tile):
                        hh, t = tile // T, tile % T
                        if tile >= 2:
                            pe.wait_ge(s_exp, a0 + tile - 1)
                        for c in range(2):
                            for n in range(2):
                                last = nc.tensor.matmul(ps[:, 2 * (tile % 2) + n, :], q_st[:, hh, t * P:(t + 1) * P],
                                                        k_st[:, c, n * 512:(n + 1) * 512], start=(c == 0), stop=(c == 1))
                        last.then_inc(s_done, 1)

                    def turn_probs(tile):
                        pe.wait_ge(p_norm, a0 + tile + 1)
                        for half in range(2):
                            g = 2 * tile + half
                            if g >= 2:
                                pe.wait_ge(p_lo, a0 * 2 + g - 1)
                            for kb in range(4):
                                last = nc.tensor.transpose(ps[:, 4 + g % 2, kb * P:(kb + 1) * P],
                                                           pp[:, tile % 3, (4 * half + kb) * P:(4 * half + kb + 1) * P], idf[:])
                            last.then_inc(p_tr, 1)

                    def values(e):
                        it = L * (KVH * 2 * T) + j * (2 * T) + e
                        pe.wait_ge(p_lo, a0 * 2 + 4 * e + 4)
                        if e >= 2:
                            pe.wait_ge(av_sum, it - 1)
                        elif e == 0:
                            pe.wait_ge(b_gated, L * (KVH * 4) + j * 4 + 4)
                        for kb in range(T):
                            nc.tensor.matmul(ps[:, 6 + e % 2, 0:256], v_st[:, kb], pT_hi[:, e % 2, kb],
                                             start=(kb == 0), stop=False)
                            last = nc.tensor.matmul(ps[:, 6 + e % 2, 0:256], v_st[:, kb], pT_lo[:, e % 2, kb],
                                                    start=False, stop=(kb == T - 1))
                        last.then_inc(pv_done, 1)

                    pe.wait_ge(b_qT, b2 + T)
                    pe.wait_ge(b_kT, b2 + T)
                    pe.wait_ge(b_free, b2 + T)
                    scores(0)
                    gate(3, 0)
                    pe.wait_ge(b_gated, L * (KVH * 4) + j * 4 + 3)
                    scores(1)
                    gate(3, 1)
                    for i in range(2 * T + 1):
                        if i >= 1:
                            turn_probs(2 * i - 1)
                        if i + 1 < 2 * T:
                            scores(2 * i + 2)
                        if i < 2 * T:
                            turn_probs(2 * i)
                        if i + 1 < 2 * T:
                            scores(2 * i + 3)
                        if i >= 1:
                            values(i - 1)
                    pe.drain().then_inc(phase_end, 1)

                def project_qk(h, t, done):
                    c0 = L * (RH * T) + h * T
                    if t == 0:
                        pe.wait_ge(w_ready, 1 + L * U_L + h * N_C + U_C + 2)
                    bank = t % QK_BANKS(done)
                    if t >= QK_BANKS(done):
                        pe.wait_ge(c_rot, c0 * 3 + 3 * (t - QK_BANKS(done)) + 3)
                    elif done is not None:
                        pe.wait_ge(c_g, c0 + t - 1)
                    prod3(ps[:, bank, 0:256], [(h_l(k, t), w_u(k, 0, 256)) for k in range(K)]).then_inc(c_qkp, 1)

                def project_vg(h, t):
                    c0 = L * (RH * T) + h * T
                    if t == 0:
                        pe.wait_ge(w_ready, 1 + L * U_L + h * N_C + U_C + N_C)
                    if t >= 2:
                        pe.wait_ge(c_g, c0 + t - 1)
                    else:
                        pe.wait_ge(c_rot, c0 * 3 + 3 * (T - 1 + t))
                    prod3(ps[:, t % 2, 0:256], [(h_l(k, t), w_u(k, 256, 512)) for k in range(K)]).then_inc(c_vgp, 1)

                def turn(h, t):
                    c0 = L * (RH * T) + h * T
                    pe.wait_ge(c_o, c0 + t + 1)
                    if t >= 1:
                        pe.wait_ge(c_T, c0 + t)
                    nc.tensor.transpose(ps[:, 5, 0:P], ra[:, t, 0:RD], idf[:])
                    nc.tensor.transpose(ps[:, 5, P:2 * P], ra[:, t, RD:2 * RD], idf[:]).then_inc(c_tr, 1)

                def chunk_scores(h, t):
                    c0 = L * (RH * T) + h * T
                    pe.wait_ge(c_T, c0 + t + 1)
                    if t >= 1:
                        pe.wait_ge(c_pm, c0 + t)
                    nc.tensor.matmul(ps[:, 2, 0:P], qkT[:, t, P:2 * P], qkT[:, t, 0:P], start=True, stop=True).then_inc(c_qk, 1)

                def update(h, t):
                    c0 = L * (RH * T) + h * T
                    f0 = L * (RH * (T - 1)) + h * (T - 1)
                    pe.wait_ge(c_v, c0 * 3 + 3 * t + 3)
                    if t >= 1:
                        pe.wait_ge(c_uf, f0 + t)
                    if t >= 2:
                        pe.wait_ge(c_ub, f0 + t - 1)
                    nc.tensor.matmul(ps[:, 3, 0:2 * RD], ra[:, t, RD:2 * RD], vd[:, t % 2], start=True, stop=True).then_inc(c_u, 1)
                    pe.wait_ge(c_pm, c0 + t + 1)
                    if t >= 1:
                        pe.wait_ge(c_oc, c0 + t)
                    nc.tensor.matmul(ps[:, 4, 0:RD], pm[:, t % 2], vv[:, t % 2], start=True, stop=True).then_inc(c_pv, 1)

                def cross(h, e):
                    x0 = L * (RH * 4) + h * 4
                    if e == 0:
                        pe.wait_ge(c_back, L * (RH * 6) + h * 6 + 6)
                        pe.wait_ge(c_zero, L * 2 + 2)
                    elif e >= 2:
                        pe.wait_ge(c_xb, x0 + e - 1)
                    for i in range(2):
                        t = 2 * e + i
                        last = nc.tensor.matmul(ps[:, 6 + e % 2, i * 256:(i + 1) * 256], qkT[:, t, 0:P], us[:, t].rearrange("p s d -> p (s d)"),
                                                start=True, stop=True)
                    last.then_inc(c_x, 1)

                def turn_out(h, half):
                    pe.wait_ge(c_yg, L * (RH * 2) + h * 2 + half + 1)
                    for i in range(4):
                        last = nc.tensor.transpose(ps[:, 7 - half, i * P:(i + 1) * P], oc[:, 4 * half + i], idf[:])
                    last.then_inc(c_ytr, 1)

                def first_pass(h, done):
                    for t in range(T):
                        project_qk(h, t, done)
                        if done is not None and t == 0:
                            update(done, T - 1)
                        if t >= 2:
                            turn(h, t - 2)
                        if done is not None and 1 <= t <= 2:
                            cross(done, 2 * t - 2)
                            cross(done, 2 * t - 1)
                    if done is not None:
                        turn_out(done, 0)
                    else:
                        pe.wait_ge(c_rot, L * (RH * T * 3) + T * 3)
                    chunk_scores(h, 0)
                    project_vg(h, 0)
                    if done is not None:
                        turn_out(done, 1)

                def second_pass(h):
                    for t in range(T):
                        if t >= 1:
                            chunk_scores(h, t)
                            project_vg(h, t)
                        if t < 2:
                            turn(h, T - 2 + t)
                        if t >= 1:
                            update(h, t - 1)

                first_pass(0, None)
                with pe.Fori(0, RH - 1) as h:
                    second_pass(h)
                    first_pass(h + 1, h)
                second_pass(RH - 1)

                def gate_part(m, kind, n, part):
                    if part == 0:
                        if n == 0:
                            pe.wait_ge(w_ready, 1 + L * U_L + m * N_D1 + U_D1 + kind + 1)
                        if type(m) is not int or m > 0:
                            pe.wait_ge((d_tA, d_tB)[kind], L * (2 * K) + m * 2 + n)
                    last = prod3(ps[:, GATE_BANK[kind][n], :],
                                 [(w_u(k, kind * P, (kind + 1) * P), h_r(k, n)) for k in range(4 * part, 4 * part + 4)],
                                 start=(part == 0), stop=(part == 1))
                    if part == 1:
                        last.then_inc((d_gA, d_gB)[kind], 1)

                update(RH - 1, T - 1)
                pe.wait_ge(c_g, L * (RH * T) + RH * T)
                parts = [(kind, n, part) for kind in range(2) for n in range(2) for part in range(2)]
                for i, (kind, n, part) in enumerate(parts):
                    gate_part(0, kind, n, part)
                    if 1 <= i <= 2:
                        cross(RH - 1, 2 * i - 2)
                        cross(RH - 1, 2 * i - 1)
                turn_out(RH - 1, 0)
                turn_out(RH - 1, 1)
                pe.drain().then_inc(phase_end, 1)

                def gates(m):
                    for kind in range(2):
                        for n in range(2):
                            for part in range(2):
                                gate_part(m, kind, n, part)

                def branches(m, pos):
                    pe.wait_ge(w_ready, 1 + L * U_L + m * N_D1 + U_D1 + 3)
                    for br, (uh, ul) in enumerate(((ua_hi, ua_lo), (ur_hi, ur_lo))):
                        for n in range(2):
                            pe.wait_ge((d_mA, d_mB)[br], L * (2 * K) + m * 2 + 1)
                            if br == 1 and n == 0:
                                pe.wait_ge(c_ul, L * (RH * 2) + RH * 2)
                            prod3(ps[:, BRANCH_BANK[br][n], :],
                                  [(w_u(br * KA + k, pos * P, (pos + 1) * P),
                                    (uh[:, k, n * 512:(n + 1) * 512], ul[:, k, n * 512:(n + 1) * 512])) for k in range(KA)]
                                  ).then_inc((d_ya, d_yb)[br], 1)

                with pe.Fori(0, K // 2 - 1) as b:
                    branches(2 * b, 2)
                    gates(2 * b + 1)
                    branches(2 * b + 1, 3)
                    gates(2 * b + 2)
                branches(K - 2, 2)
                gates(K - 1)
                branches(K - 1, 3)

                with pe.Fori(0, 2) as b:
                    for i in range(2):
                        pe.wait_ge(w_ready, 1 + L * U_L + b * 4 + U_D2 + 2 * i + 2)
                        for t in range(T):
                            o = L * (4 * T) + b * (2 * T) + i * T + t
                            pe.wait_ge(d_res, o + 1)
                            if i == 0:
                                pe.wait_ge(d_lo, L * T + t + 1)
                            prod3(ps[:, t, 0:256], [(h_l(k, t), w_u(k, 256 * i, 256 * (i + 1))) for k in range(K)]).then_inc(d_out, 1)
                pe.drain().then_inc(phase_end, 1)

        @block.scalar
        def _(act):
            for d, s in ((idf[:], ident), (dst[:], dist), (icol[:], idx)):
                act.dma_start(d, s).then_inc(consts_in, 16)
            for i, src in enumerate((dec_f, dec_b)):
                for L in range(DEPTH):
                    act.dma_start(lgw[:, 0, (i * DEPTH + L) * RH:(i * DEPTH + L + 1) * RH],
                                  src[L:L + 1, :].to_broadcast([P, RH])).then_inc(consts_in, 16)
            for i in range(4):
                act.dma_start(xm[:, 2 * i:2 * i + 2], x.rearrange("(t p) d -> p t d", p=P)[:, 2 * i:2 * i + 2]).then_inc(x_in[i], 16)
            act.dma_start(gB[:], gains[0:1, :].to_broadcast([P, DM])).then_inc(gain_in, 16)
            act.wait_ge(consts_in, NCONST)
            nc.scalar.copy(idr[:], idf[:]).then_inc(pro_act, 1)
            act.wait_ge(pro_dve, 2)
            nc.scalar.activation(lgw[:, 2], lgw[:, 1], ACT.Exp).then_inc(pro_act, 1)
            for t in range(T):
                act.wait_ge(x_in[t // 2], 16)
                if t:
                    act.wait_ge(a_sq, t)
                nc.scalar.activation(junk[:], xtile(t), ACT.Square, accum_out=ss4[:, t:t + 1]).then_inc(a_sq, 1)
            act.wait_ge(pro_dve, 22)
            nc.scalar.activation(dec[:, :, 0:6], dec[:, :, 0:6], ACT.Exp).then_inc(pro_act, 1)
            for s in (d_tA, d_tB):
                act.sem_inc(s, 1)
            act.drain().then_inc(phase_end, 1)

            with act.Fori(0, DEPTH) as L:
                act.wait_ge(phase_end, 3 + L * PH_L)

                def hi_x(t):
                    act.wait_ge(h_tr, L * T + t + 1)
                    for half in range(2):
                        nc.scalar.copy(hT_hi[:, 4 * half:4 * half + 4, t * P:(t + 1) * P],
                                       ps[:, 4 + 2 * (t % 2) + half].rearrange("p (k c) -> p k c", c=P)).then_inc(h_hi, 1)

                for j in range(KVH):
                    act.wait_ge(phase_end, 3 + L * PH_L + j * 3)
                    for c in range(2):
                        act.dma_start(ctA[:, c], rope_a[:, c]).then_inc(b_tab, 16)
                    for hh in range(GRP):
                        act.dma_start(gqk[:, hh * HD:(hh + 1) * HD], qn[bass.ds(L, 1), :].to_broadcast([P, HD])).then_inc(b_tab, 16)
                    act.dma_start(gqk[:, GRP * HD:], kn[bass.ds(L, 1), :].to_broadcast([P, HD])).then_inc(b_tab, 16)
                    if j == 0:
                        act.dma_start(xs.rearrange("(t p) d -> p t d", p=P), xm[:]).then_inc(x_saved, 16)
                    b0 = L * (KVH * T) + j * T

                    def outputs(t):
                        act.wait_ge(b_proj, b0 + t + 1)
                        if t >= 2:
                            act.wait_ge(b_ssum, b0 + t - 1)
                        nc.scalar.activation(sq[:, t % 2], ps[:, t % 2, 0:QK_W], ACT.Square).then_inc(b_sq, 1)
                        nc.scalar.copy(zqk[:, t], ps[:, t % 2, 0:QK_W]).then_inc(b_z, 1)
                        nc.scalar.copy(v_st[:, t, 0:HD], ps[:, t % 2, QK_W:QK_W + HD]).then_inc(b_vh, 1)

                    def gate(g):
                        act.wait_ge(b_gate, L * (KVH * 4) + j * 4 + g + 1)
                        if g >= 2:
                            act.wait_ge(b_gated, L * (KVH * 4) + j * 4 + g - 1)
                        nc.scalar.activation(tanh_gate(g), ps[:, G_BANK[g]], ACT.Tanh, scale=0.5).then_inc(b_tanh, 1)

                    def hi_parts(t):
                        act.wait_ge(b_rot, b0 + t + 1)
                        if t >= 2:
                            act.wait_ge(b_tr, b0 + t - 1)
                        nc.scalar.copy(qs[:, t % 2, 0:GRP, 0:HD],
                                       rta[:, t % 2, 0:GRP * HD].rearrange("p (h d) -> p h d", d=HD)).then_inc(b_hi, 1)
                        nc.scalar.copy(qs[:, t % 2, GRP].rearrange("p (r d) -> p r d", d=HD),
                                       rta[:, t % 2:t % 2 + 1, GRP * HD:].to_broadcast([P, 2, HD])).then_inc(b_hi, 1)

                    def keep_q(t):
                        act.wait_ge(b_tr, b0 + t + 1)
                        nc.scalar.copy(q_st[:, :, t * P:(t + 1) * P],
                                       ps[:, 4 + 2 * (t % 2)].rearrange("p (h c) -> p h c", c=P)).then_inc(b_qT, 1)

                    if j == 0:
                        hi_x(0)
                    for t in range(T):
                        if j == 0 and t + 1 < T:
                            hi_x(t + 1)
                        outputs(t)
                        if t >= 4:
                            hi_parts(t - 4)
                        if t == 5 and j == 0:
                            act.wait_ge(x_saved, L * 16 + 16)
                        if t >= 5:
                            keep_q(t - 5)
                    hi_parts(4)
                    keep_q(3)
                    gate(0)
                    hi_parts(5)
                    keep_q(4)
                    hi_parts(6)
                    keep_q(5)
                    gate(1)
                    hi_parts(7)
                    keep_q(6)
                    keep_q(7)
                    gate(2)

                    a0 = L * (KVH * 4 * T) + j * (4 * T)
                    i0 = L * (KVH * 2 * T) + j * (2 * T)

                    def exponent(tile):
                        act.wait_ge(s_max, a0 + tile + 1)
                        if tile >= 3:
                            act.wait_ge(p_tr, a0 * 2 + 2 * tile - 4)
                        s = tile % 2
                        nc.scalar.activation(pp[:, tile % 3], ps[:, 2 * s:2 * s + 2].rearrange("p a b -> p (a b)"), ACT.Exp,
                                             bias=nmx[:, tile % 4:tile % 4 + 1],
                                             accum_out=rsm[:, tile % 4:tile % 4 + 1]).then_inc(s_exp, 1)

                    def hi_probs(tile):
                        e = tile // 2
                        for half in range(2):
                            g = 2 * tile + half
                            act.wait_ge(p_tr, a0 * 2 + g + 1)
                            if e >= 2:
                                act.wait_ge(pv_done, i0 + e - 1)
                            nc.scalar.copy(pT_hi[:, e % 2, 4 * half:4 * half + 4, (tile % 2) * P:(tile % 2 + 1) * P],
                                           ps[:, 4 + half].rearrange("p (k c) -> p k c", c=P)).then_inc(p_hi, 1)

                    for i in range(2 * T + 3):
                        for s in range(2):
                            if 1 <= i <= 2 * T:
                                hi_probs(2 * (i - 1) + s)
                            if s == 1 and 2 <= i < 2 * T + 2:
                                e = i - 2
                                pr = HD * (e // 4 % 2)
                                act.wait_ge(pv_done, i0 + e + 1)
                                if e >= 2:
                                    act.wait_ge(ua_l, i0 + e - 1)
                                nc.scalar.activation(av[pr:pr + HD, e % 2], ps[HD:2 * HD, 6 + e % 2, 0:256], ACT.Copy,
                                                     scale=0.5).then_inc(av_lo, 1)
                            if i < 2 * T:
                                exponent(2 * i + s)
                            if s == 0 and i >= 3:
                                e = i - 3
                                hh, qp = e // 4, e % 4
                                pr = HD * (hh % 2)
                                act.wait_ge(consts_in, NCONST)
                                act.wait_ge(av_gated, i0 + e + 1)
                                nc.scalar.copy(ua_hi[pr:pr + HD, bass.ds(j * 2 + hh // 2, 1), qp * 256:(qp + 1) * 256],
                                               av[pr:pr + HD, e % 2:e % 2 + 1]).then_inc(ua_h, 1)
                        if i == 0:
                            gate(3)
                    act.wait_ge(consts_in, NCONST)
                    act.wait_ge(ua_l, i0 + 2 * T)
                    act.drain().then_inc(phase_end, 1)

                act.wait_ge(phase_end, 3 + L * PH_L + 3 * KVH)
                for c in range(2):
                    act.dma_start(ctR[:, c], rope_r[:, c]).then_inc(c_tab, 16)
                act.dma_start(gwc[:], gn_w[:, bass.ds(L, 1), :].rearrange("p a h -> p (a h)")).then_inc(c_tab, 16)
                act.wait_ge(c_arg, L * (RH * 2) + 2)
                nc.scalar.activation(msk[:], msk[:], ACT.Exp).then_inc(c_mexp, 1)

                def keep_qk(h, t):
                    act.wait_ge(c_tr, L * (RH * T) + h * T + t + 1)
                    nc.scalar.copy(qkT[:, t], ps[:, 5, 0:2 * P]).then_inc(c_T, 1)

                def outputs(h, t):
                    c0 = L * (RH * T) + h * T
                    act.wait_ge(c_vgp, c0 + t + 1)
                    if t >= 2:
                        act.wait_ge(c_pv, c0 + t - 1)
                    v = ps[:, t % 2, 0:RD]
                    nc.scalar.copy(vv[:, t % 2], v).then_inc(c_v, 1)
                    for d in range(2):
                        nc.scalar.activation(vd[:, t % 2, d * RD:(d + 1) * RD], v, ACT.Copy, scale=dcur[:, 2 + d:3 + d]).then_inc(c_v, 1)
                    nc.scalar.activation(g2[:, t], ps[:, t % 2, RD:2 * RD], ACT.Tanh, scale=0.5).then_inc(c_th, 1)

                def update(h, t):
                    c0 = L * (RH * T) + h * T
                    if t >= 1:
                        act.wait_ge(c_u, c0 + t + 1)
                        nc.scalar.copy(us[:, t - 1, 1], ps[:, 3, RD:2 * RD]).then_inc(c_ub, 1)
                    act.wait_ge(c_pv, c0 + t + 1)
                    nc.scalar.copy(oc[:, t], ps[:, 4, 0:RD]).then_inc(c_oc, 1)

                def keep_out(h, half):
                    act.wait_ge(consts_in, NCONST)
                    act.wait_ge(c_ytr, L * (RH * 2) + h * 2 + half + 1)
                    nc.scalar.activation(ur_hi[:, bass.ds(h, 1), half * 512:(half + 1) * 512], ps[:, 7 - half:8 - half], ACT.Copy,
                                         scale=gwh[:]).then_inc(c_uh, 1)

                def first_pass(h, done):
                    for t in range(T):
                        if done is not None and t == 0:
                            update(done, T - 1)
                        if t >= 2:
                            keep_qk(h, t - 2)
                        if done is not None and t == 6:
                            act.wait_ge(c_arg, L * (RH * 2) + h * 2 + 2)
                            nc.scalar.activation(msk[:], msk[:], ACT.Exp).then_inc(c_mexp, 1)
                    if done is not None:
                        keep_out(done, 0)
                        keep_out(done, 1)

                def second_pass(h):
                    for t in range(T):
                        if t < 2:
                            keep_qk(h, T - 2 + t)
                        outputs(h, t)
                        if t >= 1:
                            update(h, t - 1)

                first_pass(0, None)
                with act.Fori(0, RH - 1) as h:
                    second_pass(h)
                    first_pass(h + 1, h)
                second_pass(RH - 1)
                update(RH - 1, T - 1)
                keep_out(RH - 1, 0)
                keep_out(RH - 1, 1)
                act.drain().then_inc(phase_end, 1)

                act.wait_ge(consts_in, NCONST)
                act.wait_ge(phase_end, 3 + L * PH_L + 3 * (KVH + 1))
                with act.Fori(0, 2) as b:
                    for i in range(4):
                        m = L * K + b * 4 + i
                        for kind in range(2):
                            for n in range(2):
                                act.wait_ge((d_gA, d_gB)[kind], m * 2 + n + 1)
                                act.wait_ge(d_mg, m * 2 + n if i else m * 2 + 1)
                                nc.scalar.activation((tA, tB)[kind][:, n], ps[:, GATE_BANK[kind][n]], ACT.Tanh, scale=0.5).then_inc((d_tA, d_tB)[kind], 1)

                act.dma_start(gB[:], gains[bass.ds(L + 1, 1), :].to_broadcast([P, DM])).then_inc(gain_in, 16)
                for t in range(T):
                    if t % 4 == 0:
                        act.wait_ge(d_mg, L * (2 * K) + 2 * K + t // 4)
                    nc.scalar.copy(hT_hi[:, :, t * P:(t + 1) * P], xm[:, :, t * P:(t + 1) * P]).then_inc(d_hi, 1)
                act.wait_ge(d_lo, L * T + T)
                act.wait_ge(x_saved, L * 16 + 16)
                for a in (0, 1):
                    act.dma_start(xm[:, 4 * a:4 * a + 4], xs.rearrange("(t p) d -> p t d", p=P)[:, 4 * a:4 * a + 4]).then_inc(x_back[a], 16)
                with act.Fori(0, 4) as q:
                    for t in range(T):
                        o = L * (4 * T) + q * T + t
                        act.wait_ge(consts_in, NCONST)
                        act.wait_ge(d_res, o + T + 1)
                        act.wait_ge(a_sq, o + T)
                        nc.scalar.activation(junk[:, 0:256], xm[:, t:t + 1, bass.ds(q * 256, 256)], ACT.Square,
                                             accum_out=ss4[:, bass.ds(q * T + t, 1)]).then_inc(a_sq, 1)
                act.drain().then_inc(phase_end, 1)

            for t in range(0, T, 2):
                put_out(act, t)
            act.wait_ge(out_done[0], 16 * (T // 2))

        @block.vector
        def _(dve):
            held[dve] = dve.alloc_register("held_dve")
            V = nc.vector

            def rsqrt(a, b, base):
                v, y, t_ = ss[:, a:b], rs[:, a:b], nt[:, a:b]
                V.tensor_scalar(y.bitcast(I32), v.bitcast(I32), -0.5, MAGIC, ALU.mult, ALU.add).then_inc(newton, 1)
                for r in range(3):
                    dve.wait_ge(newton, base + 3 * r + 1)
                    V.scalar_tensor_tensor(t_, y, -0.5, y, ALU.mult, ALU.mult).then_inc(newton, 1)
                    dve.wait_ge(newton, base + 3 * r + 2)
                    V.tensor_tensor(t_, t_, v, ALU.mult).then_inc(newton, 1)
                    dve.wait_ge(newton, base + 3 * r + 3)
                    V.scalar_tensor_tensor(y, t_, 1.5, y, ALU.add, ALU.mult).then_inc(newton, 1)
                dve.wait_ge(newton, base + 10)

            NW_L = 24 + 11 * (2 * KVH + RH)

            def mean_square(L, half):
                nw = L * NW_L + half * 12
                a, b = X0 + half * (T // 2), X0 + (half + 1) * (T // 2)
                dve.wait_ge(consts_in, NCONST)
                dve.wait_ge(a_sq, L * (4 * T) + (half + 1) * (T // 2))
                V.tensor_reduce(ss[:, a:b], ss4[:].rearrange("p (q t) -> p t q", t=T)[:, a - X0:b - X0], AXX, ALU.add).then_inc(newton, 1)
                dve.wait_ge(newton, nw + 1)
                V.tensor_scalar(ss[:, a:b], ss[:, a:b], 1.0 / DM, EPS, ALU.mult, ALU.add).then_inc(newton, 1)
                dve.wait_ge(newton, nw + 2)
                rsqrt(a, b, nw + 2)

            def norm_x(L, t):
                if t >= 2:
                    dve.wait_ge(h_tr, L * T + t - 1)
                V.scalar_tensor_tensor(hb[:, t % 2], xtile(t), rs[:, X0 + t:X0 + t + 1], gB[:], ALU.mult, ALU.mult).then_inc(h_ready, 1)

            done = [0]

            def step(ins):
                done[0] += 1
                ins.then_inc(pro_dve, 1)
                dve.wait_ge(pro_dve, done[0])

            dve.wait_ge(consts_in, NCONST)
            step(V.tensor_scalar(lgw[:, 1], lgw[:, 0], -1.0, None, ALU.mult))
            step(V.tensor_tensor(lgw[:, 1], lgw[:, 1], lgw[:, 0], ALU.min))
            dve.wait_ge(pro_act, 2)
            step(V.tensor_scalar(lgw[:, 3], lgw[:, 2], 2.0, None, ALU.add))
            step(V.reciprocal(lgw[:, 3], lgw[:, 3]))
            step(V.tensor_tensor(lgw[:, 3], lgw[:, 3], lgw[:, 2], ALU.mult))
            step(V.tensor_tensor(lgw[:, 4], lgw[:, 3], lgw[:, 3], ALU.mult))
            step(V.tensor_scalar(lgw[:, 5], lgw[:, 4], 1.0 / 15, None, ALU.mult))
            for c in (13, 11, 9, 7, 5, 3):
                step(V.scalar_tensor_tensor(lgw[:, 5], lgw[:, 5], 1.0 / c, lgw[:, 4], ALU.add, ALU.mult))
            step(V.scalar_tensor_tensor(lgw[:, 5], lgw[:, 5], 1.0, lgw[:, 3], ALU.add, ALU.mult))
            step(V.tensor_scalar(lgw[:, 2], lgw[:, 0], 0.0, None, ALU.min))
            step(V.scalar_tensor_tensor(lgw[:, 2], lgw[:, 5], -2.0, lgw[:, 2], ALU.mult, ALU.add))
            half = DEPTH * RH
            for c in range(6):
                a = (c % 2) * half
                ins = V.tensor_scalar(dec[:, :, c], lgw[:, 2, a:a + half], icol[:, c:c + 1], None, ALU.mult)
                if c == 5:
                    step(ins)
                else:
                    ins.then_inc(pro_dve, 1)
                    done[0] += 1
            assert done[0] == 22, done
            V.memset(ss4[:, T:], 0.0).then_inc(a_zero, 1)
            dve.wait_ge(gain_in, 16)
            dve.wait_ge(a_zero, 1)
            mean_square(0, 0)
            norm_x(0, 0)
            norm_x(0, 1)
            dve.wait_ge(pro_act, 3)
            for c in (2, 3):
                step(V.tensor_scalar(dec[:, :, c], dec[:, :, c], RD ** -0.5, None, ALU.mult))
            for c in (6, 7):
                step(V.tensor_copy(dec[:, :, c], lgw[:, 2, (c - 6) * half:(c - 5) * half]))
            dve.sem_inc(d_res, T)
            for s in (d_mA, d_mB, d_mg):
                dve.sem_inc(s, 1)
            dve.drain().then_inc(phase_end, 1)

            with dve.Fori(0, DEPTH) as L:
                dve.wait_ge(phase_end, 3 + L * PH_L)

                def lo_x(t):
                    for hf in range(2):
                        dve.wait_ge(h_hi, L * (2 * T) + 2 * t + hf + 1)
                        o = (slice(None), slice(4 * hf, 4 * hf + 4), slice(t * P, (t + 1) * P))
                        V.tensor_tensor(hT_lo[o], ps[:, 4 + 2 * (t % 2) + hf].rearrange("p (k c) -> p k c", c=P),
                                        hT_hi[o].bitcast(F32), ALU.subtract).then_inc(h_lo, 1)

                for j in range(KVH):
                    dve.wait_ge(phase_end, 3 + L * PH_L + j * 3)
                    lj = L * KVH + j
                    def outputs(t):
                        bt = lj * T + t
                        dve.wait_ge(b_sq, bt + 1)
                        V.tensor_reduce(ss[:, t * (GRP + 1):(t + 1) * (GRP + 1)],
                                        sq[:, t % 2].rearrange("p (h d) -> p h d", d=HD), AXX, ALU.add).then_inc(b_ssum, 1)
                        dve.wait_ge(b_vh, bt + 1)
                        V.tensor_tensor(v_st[:, t, HD:], ps[:, t % 2, QK_W:QK_W + HD], v_st[:, t, 0:HD].bitcast(F32),
                                        ALU.subtract).then_inc(b_free, 1)

                    def norms(half):
                        if half == 0:
                            dve.wait_ge(b_tab, lj * (16 * (3 + GRP)) + 16 * (3 + GRP))
                            V.tensor_scalar(gqk[:, 0:GRP * HD], gqk[:, 0:GRP * HD], HD ** -0.5, None, ALU.mult).then_inc(b_gain, 1)
                        n = T // 2 * (GRP + 1)
                        nw = L * NW_L + j * 22 + 11 * half + 24
                        dve.wait_ge(b_ssum, lj * T + T // 2 * (half + 1))
                        V.tensor_scalar(ss[:, half * n:(half + 1) * n], ss[:, half * n:(half + 1) * n], 1.0 / HD, EPS,
                                        ALU.mult, ALU.add).then_inc(newton, 1)
                        dve.wait_ge(newton, nw + 1)
                        rsqrt(half * n, (half + 1) * n, nw + 1)
                        dve.wait_ge(b_z, lj * T + T // 2 * (half + 1))
                        dve.wait_ge(b_gain, lj + 1)

                    def gate(g):
                        dve.wait_ge(b_tanh, lj * 4 + g + 1)
                        V.scalar_tensor_tensor(gT[:, g // 2, (g % 2) * 512:(g % 2 + 1) * 512], tanh_gate(g), 1.0, ps[:, G_BANK[g]],
                                               ALU.add, ALU.mult).then_inc(b_gated, 1)

                    def rotate(t):
                        bt = lj * T + t
                        z = zqk[:, t].rearrange("p (h d) -> p h d", d=HD)
                        V.tensor_tensor(z, z, rs[:, t * (GRP + 1):(t + 1) * (GRP + 1)].rearrange("p (h o) -> p h o", o=1)
                                        .to_broadcast([P, GRP + 1, HD]), ALU.mult).then_inc(b_norm, 1)
                        dve.wait_ge(b_norm, bt * 2 + 1)
                        V.tensor_tensor(zqk[:, t], zqk[:, t], gqk[:], ALU.mult).then_inc(b_norm, 1)
                        dve.wait_ge(b_norm, bt * 2 + 2)
                        if t >= 2:
                            dve.wait_ge(b_rot, bt - 1)
                        z5 = zqk[:, t].rearrange("p (h a s d) -> p h a s d", a=2, s=2, d=HD // 4)
                        r5 = rtb[:, t % 2].rearrange("p (h a s d) -> p h a s d", a=2, s=2, d=HD // 4)
                        s5 = ctA[:, 1, t:t + 1].rearrange("p o (a s d) -> p o a s d", a=2, s=2, d=HD // 4)
                        for s in range(2):
                            V.tensor_tensor(r5[:, :, :, s], z5[:, :, :, 1 - s],
                                            s5[:, :, :, s].to_broadcast([P, GRP + 1, 2, HD // 4]), ALU.mult).then_inc(b_sin, 1)

                    def split(t):
                        bt = lj * T + t
                        dve.wait_ge(b_hi, bt * 2 + 2)
                        if t >= 2:
                            dve.wait_ge(b_tr, bt - 1)
                        V.tensor_tensor(qs[:, t % 2, 0:GRP, HD:], rta[:, t % 2, 0:GRP * HD].rearrange("p (h d) -> p h d", d=HD),
                                        qs[:, t % 2, 0:GRP, 0:HD].bitcast(F32), ALU.subtract).then_inc(b_lo, 1)
                        V.tensor_tensor(qs[:, t % 2, GRP + 1].rearrange("p (r d) -> p r d", d=HD),
                                        rta[:, t % 2:t % 2 + 1, GRP * HD:].to_broadcast([P, 2, HD]),
                                        qs[:, t % 2, GRP].rearrange("p (r d) -> p r d", d=HD).bitcast(F32), ALU.subtract).then_inc(b_lo, 1)

                    def keep_k(t):
                        dve.wait_ge(b_tr, lj * T + t + 1)
                        V.tensor_copy(k_st[:, :, t * P:(t + 1) * P],
                                      ps[:, 5 + 2 * (t % 2), 0:2 * P].rearrange("p (h c) -> p h c", c=P)).then_inc(b_kT, 1)

                    if j == 0:
                        lo_x(0)
                        norm_x(L, 2)
                    for t in range(T):
                        if j == 0 and t + 1 < T:
                            lo_x(t + 1)
                            if t == 1:
                                mean_square(L, 1)
                            if t + 3 < T:
                                norm_x(L, t + 3)
                        outputs(t)
                        if t == 3:
                            norms(0)
                            rotate(0)
                        if 4 <= t < 7:
                            rotate(t - 3)
                        if t == 5 and j == 0:
                            dve.wait_ge(x_saved, L * 16 + 16)
                        if 5 <= t < 7:
                            keep_k(t - 5)
                        if 4 <= t < 7:
                            split(t - 4)
                    split(3)
                    norms(1)
                    rotate(4)
                    keep_k(2)
                    rotate(5)
                    split(4)
                    keep_k(3)
                    rotate(6)
                    gate(0)
                    split(5)
                    keep_k(4)
                    rotate(7)
                    split(6)
                    keep_k(5)
                    gate(1)
                    split(7)
                    keep_k(6)
                    keep_k(7)
                    gate(2)

                    a0 = lj * (4 * T)
                    i0 = lj * (2 * T)

                    def row_max(tile):
                        s = tile % 2
                        dve.wait_ge(s_done, a0 + tile + 1)
                        V.tensor_reduce(nmx[:, tile % 4:tile % 4 + 1], ps[:, 2 * s:2 * s + 2].rearrange("p a b -> p (a b)"),
                                        AXX, ALU.max, negate=True).then_inc(s_max, 1)

                    def lo_probs(tile):
                        e = tile // 2
                        for half in range(2):
                            dve.wait_ge(p_hi, a0 * 2 + 2 * tile + half + 1)
                            o = (slice(None), e % 2, slice(4 * half, 4 * half + 4), slice((tile % 2) * P, (tile % 2 + 1) * P))
                            V.tensor_tensor(pT_lo[o], ps[:, 4 + half].rearrange("p (k c) -> p k c", c=P),
                                            pT_hi[o].bitcast(F32), ALU.subtract).then_inc(p_lo, 1)

                    for i in range(2 * T + 2):
                        for s in range(2):
                            if i < 2 * T:
                                row_max(2 * i + s)
                            if 1 <= i <= 2 * T:
                                lo_probs(2 * (i - 1) + s)
                            if i < 2 * T:
                                tile = 2 * i + s
                                dve.wait_ge(s_exp, a0 + tile + 1)
                                V.reciprocal(rrc[:, tile % 4:tile % 4 + 1], rsm[:, tile % 4:tile % 4 + 1]).then_inc(s_rcp, 1)
                        if i == 0:
                            gate(3)
                        if i >= 2:
                            e = i - 2
                            pr = HD * (e // 4 % 2)
                            dve.wait_ge(av_lo, i0 + e + 1)
                            V.scalar_tensor_tensor(av[pr:pr + HD, e % 2], ps[0:HD, 6 + e % 2, 0:256], 0.5, av[pr:pr + HD, e % 2],
                                                   ALU.mult, ALU.add).then_inc(av_sum, 1)
                    dve.drain().then_inc(phase_end, 1)

                dve.wait_ge(phase_end, 3 + L * PH_L + 3 * KVH)
                dve.wait_ge(c_tab, L * 48 + 48)

                def factors(h):
                    lh = L * RH + h
                    V.tensor_copy(dcur[:], dec[:, bass.ds(lh, 1)].rearrange("p o c -> p (o c)")).then_inc(c_dec, 1)
                    dve.wait_ge(c_dec, lh + 1)
                    V.tensor_scalar(msk[:], dst[:, 0], dcur[:, 6:7], None, ALU.mult).then_inc(c_arg, 1)
                    dve.wait_ge(c_arg, lh * 2 + 1)
                    V.scalar_tensor_tensor(msk[:], dst[:, 1], dcur[:, 7:8], msk[:], ALU.mult, ALU.add).then_inc(c_arg, 1)

                def rotate(h, t, done):
                    c0 = L * (RH * T) + h * T
                    dve.wait_ge(c_qkp, c0 + t + 1)
                    if t >= 2:
                        dve.wait_ge(c_o, c0 + t - 1)
                    z = ps[:, t % QK_BANKS(done), 0:2 * RD]
                    V.tensor_tensor(ra[:, t].rearrange("p (h d) -> p h d", d=RD), z.rearrange("p (h d) -> p h d", d=RD),
                                    ctR[:, 0, t:t + 1].to_broadcast([P, 2, RD]), ALU.mult).then_inc(c_rot, 1)
                    z5 = z.rearrange("p (h a s d) -> p h a s d", a=2, s=2, d=RD // 4)
                    r5 = rb[:, t % 2].rearrange("p (h a s d) -> p h a s d", a=2, s=2, d=RD // 4)
                    s5 = ctR[:, 1, t:t + 1].rearrange("p o (a s d) -> p o a s d", a=2, s=2, d=RD // 4)
                    for s in range(2):
                        V.tensor_tensor(r5[:, :, :, s], z5[:, :, :, 1 - s],
                                        s5[:, :, :, s].to_broadcast([P, 2, 2, RD // 4]), ALU.mult).then_inc(c_rot, 1)

                def decay_scores(h, t):
                    c0 = L * (RH * T) + h * T
                    dve.wait_ge(c_qk, c0 + t + 1)
                    if t == 0:
                        dve.wait_ge(c_mexp, L * RH + h + 1)
                    if t >= 2:
                        dve.wait_ge(c_pv, c0 + t - 1)
                    V.scalar_tensor_tensor(pm[:, t % 2], ps[:, 2, 0:P], RD ** -0.5, msk[:], ALU.mult, ALU.mult).then_inc(c_pm, 1)

                def gate(h, t):
                    dve.wait_ge(c_th, L * (RH * T) + h * T + t + 1)
                    V.scalar_tensor_tensor(g2[:, t], g2[:, t], 1.0, ps[:, t % 2, RD:2 * RD], ALU.add, ALU.mult).then_inc(c_g, 1)

                def update(h, t):
                    f0 = L * (RH * (T - 1)) + h * (T - 1)
                    dve.wait_ge(c_u, L * (RH * T) + h * T + t + 1)
                    if t >= 1:
                        dve.wait_ge(c_ub, f0 + t)
                        dve.wait_ge(c_uf, f0 + t)
                    else:
                        dve.wait_ge(c_zero, L * 2 + 2)
                    V.scalar_tensor_tensor(us[:, t + 1, 0], us[:, t, 0], dcur[:, 4:5], ps[:, 3, 0:RD], ALU.mult, ALU.add).then_inc(c_uf, 1)

                def backward(h):
                    dve.wait_ge(c_ub, L * (RH * (T - 1)) + h * (T - 1) + T - 1)
                    for n, c in enumerate(range(T - 3, -1, -1)):
                        if n:
                            dve.wait_ge(c_back, L * (RH * 6) + h * 6 + n)
                        V.scalar_tensor_tensor(us[:, c, 1], us[:, c + 1, 1], dcur[:, 5:6], us[:, c, 1], ALU.mult, ALU.add).then_inc(c_back, 1)
                    dve.wait_ge(consts_in, NCONST)
                    dve.wait_ge(c_oc, L * (RH * T) + h * T + T)

                def cross(h, e):
                    x0 = L * (RH * 4) + h * 4 + e + 1
                    dve.wait_ge(c_x, x0)
                    bank = ps[:, 6 + e % 2].rearrange("p (t s d) -> p t s d", t=2, s=2)
                    o = oc[:, 2 * e:2 * e + 2]
                    V.scalar_tensor_tensor(o, bank[:, :, 0], dcur[:, 0:1], o, ALU.mult, ALU.add).then_inc(c_xa, 1)
                    dve.wait_ge(c_xa, x0)
                    V.scalar_tensor_tensor(o, bank[:, :, 1], dcur[:, 1:2], o, ALU.mult, ALU.add).then_inc(c_xb, 1)
                    dve.wait_ge(c_xb, x0)
                    for t in (2 * e, 2 * e + 1):
                        V.bn_stats(st6[:, t], oc[:, t]).then_inc(c_bn, 1)

                def norms(h):
                    c0 = L * (RH * T) + h * T
                    V.tensor_scalar(gwh[:], gwc[:, bass.ds(h, 1)], 0.5, None, ALU.mult).then_inc(c_gw, 1)
                    dve.wait_ge(consts_in, NCONST)
                    dve.wait_ge(c_bn, c0 + T)
                    for t in range(T):
                        V.bn_aggr(mv[:, t], st6[:, t]).then_inc(c_mv, 1)
                    dve.wait_ge(c_mv, c0 + T)
                    nw = L * NW_L + h * 11 + 11 * (2 * KVH) + 24
                    V.tensor_scalar(ss[:, 0:T], mv[:, :, 1], EPS, None, ALU.add).then_inc(newton, 1)
                    dve.wait_ge(newton, nw + 1)
                    rsqrt(0, T, nw + 1)

                def normed(h, half):
                    for t in range(4 * half, 4 * half + 4):
                        V.tensor_scalar(oc[:, t], oc[:, t], mv[:, t, 0:1], rs[:, t:t + 1], ALU.subtract, ALU.mult).then_inc(c_y, 1)
                    dve.wait_ge(c_y, L * (RH * T) + h * T + 4 * half + 4)
                    o = slice(4 * half, 4 * half + 4)
                    V.tensor_tensor(oc[:, o], oc[:, o], g2[:, o], ALU.mult).then_inc(c_yg, 1)

                def keep_out(h, half):
                    dve.wait_ge(consts_in, NCONST)
                    dve.wait_ge(c_uh, L * (RH * 2) + h * 2 + half + 1)
                    dve.wait_ge(c_gw, L * RH + h + 1)
                    o = (slice(None), bass.ds(h, 1), slice(half * 512, (half + 1) * 512))
                    V.scalar_tensor_tensor(ur_lo[o], ps[:, 7 - half:8 - half], gwh[:], ur_hi[o].bitcast(F32),
                                           ALU.mult, ALU.subtract).then_inc(c_ul, 1)

                def first_pass(h, done):
                    for t in range(T):
                        if done is not None and 2 <= t <= 3:
                            cross(done, 2 * t - 4)
                            cross(done, 2 * t - 3)
                        rotate(h, t, done)
                        if done is not None:
                            if t == 0:
                                backward(done)
                            if t == 4:
                                norms(done)
                            if 5 <= t <= 6:
                                normed(done, t - 5)
                            if t == 6:
                                factors(h)
                    if done is not None:
                        keep_out(done, 0)
                        keep_out(done, 1)

                def second_pass(h):
                    decay_scores(h, 0)
                    for t in range(T):
                        if t >= 1:
                            update(h, t - 1)
                        if t + 1 < T:
                            decay_scores(h, t + 1)
                        gate(h, t)

                factors(0)
                V.memset(us[:, 0, 0], 0.0).then_inc(c_zero, 1)
                V.memset(us[:, T - 1, 1], 0.0).then_inc(c_zero, 1)
                first_pass(0, None)
                with dve.Fori(0, RH - 1) as h:
                    second_pass(h)
                    first_pass(h + 1, h)
                second_pass(RH - 1)
                backward(RH - 1)
                for e in range(4):
                    cross(RH - 1, e)
                norms(RH - 1)
                for half in range(2):
                    normed(RH - 1, half)
                for half in range(2):
                    keep_out(RH - 1, half)
                dve.drain().then_inc(phase_end, 1)

                wait_apart(dve, phase_end, 3 + L * PH_L + 3 * (KVH + 1))
                with dve.Fori(0, 2) as b:
                    for i in range(4):
                        m = L * K + b * 4 + i
                        for n in range(2):
                            dve.wait_ge(d_tA, m * 2 + n + 2)
                            dve.wait_ge(d_ya, m * 2 + n + 1)
                            V.scalar_tensor_tensor(tA[:, n], tA[:, n], 1.0, ps[:, BRANCH_BANK[0][n]], ALU.add, ALU.mult).then_inc(d_mA, 1)
                        for n in range(2):
                            dve.wait_ge(d_tB, m * 2 + n + 2)
                            dve.wait_ge(d_yb, m * 2 + n + 1)
                            V.scalar_tensor_tensor(tB[:, n], tB[:, n], 1.0, ps[:, BRANCH_BANK[1][n]], ALU.add, ALU.mult).then_inc(d_mB, 1)
                            dve.wait_ge(consts_in, NCONST)
                            dve.wait_ge(d_mB, m * 2 + n + 2)
                            dve.wait_ge(d_mA, m * 2 + n + 2)
                            V.tensor_tensor(xm[:, bass.ds(b * 4 + i, 1), n * 512:(n + 1) * 512], tA[:, n:n + 1], tB[:, n:n + 1],
                                            ALU.add).then_inc(d_mg, 1)

                for t in range(T):
                    dve.wait_ge(d_hi, L * T + t + 1)
                    o = (slice(None), slice(None), slice(t * P, (t + 1) * P))
                    V.tensor_tensor(hT_lo[o], xm[o], hT_hi[o].bitcast(F32), ALU.subtract).then_inc(d_lo, 1)

                def residual(q, t):
                    dve.wait_ge(consts_in, NCONST)
                    dve.wait_ge(d_out, L * (4 * T) + q * T + t + 1 + 2 * T)
                    if t % 4 == 0:
                        dve.wait_ge(x_back[t // 4], L * 16 + 16)
                    o = (slice(None), slice(t, t + 1), bass.ds(q * 256, 256))
                    V.scalar_tensor_tensor(xm[o], ps[:, t:t + 1, 0:256], 0.5, xm[o], ALU.mult, ALU.add).then_inc(d_res, 1)

                with dve.Fori(0, 3) as q:
                    for t in range(T):
                        residual(q, t)
                for t in range(T):
                    residual(3, t)
                    if t == 4:
                        mean_square(L + 1, 0)
                    elif t == 5:
                        dve.wait_ge(consts_in, NCONST)
                        dve.wait_ge(gain_in, L * 16 + 32)
                        norm_x(L + 1, 0)
                    elif t == 6:
                        norm_x(L + 1, 1)
                dve.drain().then_inc(phase_end, 1)

            dve.wait_ge(phase_end, 3 + DEPTH * PH_L)
            mean_square(DEPTH, 1)
            for t in range(2, T):
                V.scalar_tensor_tensor(xtile(t), xtile(t), rs[:, X0 + t:X0 + t + 1], gB[:], ALU.mult, ALU.mult).then_inc(f_y, 1)


def _rope(width):
    d_axis = width // 2
    q = width // 4
    inv = (THETA ** (-np.arange(0, d_axis, 2, dtype=np.float32) / np.float32(d_axis))).astype(np.float32)
    t = np.arange(SEQ)
    ang = np.stack([(t // GRID_W)[:, None].astype(np.float32) * inv, (t % GRID_W)[:, None].astype(np.float32) * inv], 1)
    c, s = np.cos(ang), np.sin(ang)
    full = np.stack([np.stack([c, c], 2), np.stack([-s, s], 2)], 0).reshape(2, T, P, 4 * q)
    return np.ascontiguousarray(full.transpose(2, 0, 1, 3)).astype(np.float32)


def _constants():
    i = np.arange(P, dtype=np.float32)
    diff = i[None, :] - i[:, None]
    dist = np.stack([np.maximum(diff, 0), np.maximum(-diff, 0)], 1)
    full = np.full(P, P, np.float32)
    idx = np.stack([i + 1, P - i, P - 1 - i, i, full, full], 1)
    return {"ident": np.eye(P, dtype=np.float32), "rope_a": _rope(HD), "rope_r": _rope(RD),
            "dist": np.ascontiguousarray(dist), "idx": np.ascontiguousarray(idx)}


def kernel(x, norm_g, w_in, attn_q_norm, attn_k_norm, ret_decay_fwd, ret_decay_bwd, ret_gn_w,
           w_branch_attn, w_branch_ret, w_out, final_norm_g):
    import concourse.bacc as bacc
    from concourse.bass_utils import run_bass_kernel_spmd

    a = lambda v, *s: np.ascontiguousarray(np.asarray(v).reshape(*s))
    arrays = {
        "x": a(x, SEQ, DM), "gains": np.concatenate([a(norm_g, DEPTH, DM), a(final_norm_g, 1, DM)]),
        "w_in": a(w_in, DEPTH * DM, D_IN),
        "qn": a(attn_q_norm, DEPTH, HD), "kn": a(attn_k_norm, DEPTH, HD),
        "dec_f": a(ret_decay_fwd, DEPTH, RH), "dec_b": a(ret_decay_bwd, DEPTH, RH),
        "gn_w": np.ascontiguousarray(np.asarray(ret_gn_w).reshape(DEPTH, RH, RD).transpose(2, 0, 1)),
        "w_a": a(w_branch_attn, DEPTH * AW, DM), "w_r": a(w_branch_ret, DEPTH * RW, DM),
        "w_o": a(w_out, DEPTH * DM, DM), **_constants(),
    }
    nc = bacc.Bacc("TRN2", target_bir_lowering=False, num_devices=1, dynamic_dma_scratch_size=1024)
    aps = {n: nc.dram_tensor(n, v.shape, mybir.dt.from_np(v.dtype), kind="ExternalInput").ap() for n, v in arrays.items()}
    xs = nc.dram_tensor("xs", (SEQ, DM), F32, kind="Internal").ap()
    out = nc.dram_tensor("out", (SEQ, DM), F32, kind="ExternalOutput").ap()
    build(nc, xs=xs, out=out, **aps)
    r = run_bass_kernel_spmd(nc, [arrays], core_ids=[0])
    return r.results[0]["out"].reshape(np.asarray(x).shape)
```
